# Optimizing a Trainium2 kernel written in Bass

```python
import math
import jax, jax.numpy as jnp
from jax import lax
import numpy as np

D_MODEL = 1024
BATCH = 1
SEQ = 256
DEPTH = 1

MEM_LEN = 256
DA_HEADS = 8
DA_DK = D_MODEL // (2 * DA_HEADS)
DA_DV = 2 * DA_DK
Q_BLOCK = 128
RET_HEADS = 4
RET_DV = D_MODEL // RET_HEADS
RET_DK = RET_DV // 2
RET_CHUNK = 128
MEM_HEADS = 4
MEM_DH = D_MODEL // MEM_HEADS
N_BRANCH = 3
BRANCH_W = D_MODEL
N_GROUPS = 4
EXPERTS_PER_GROUP = 4
N_EXPERTS = N_GROUPS * EXPERTS_PER_GROUP
EXPERT_TOPK = 2
D_FF_EXPERT = D_MODEL // 2
DEEPNORM_ALPHA = (2.0 * DEPTH) ** 0.25
DEEPNORM_BETA = (8.0 * DEPTH) ** -0.25
EPS = 1e-5

SPLIT_SIZES = (DA_HEADS * 2 * DA_DK, DA_HEADS * 2 * DA_DK, DA_HEADS * DA_DV,
               RET_HEADS * RET_DK, RET_HEADS * RET_DK, RET_HEADS * RET_DV, RET_HEADS * RET_DV,
               MEM_HEADS * MEM_DH, N_BRANCH * D_MODEL)
SPLIT_POINTS = tuple(int(v) for v in np.cumsum(SPLIT_SIZES)[:-1])
IN_WIDTH = int(sum(SPLIT_SIZES))
VALUE_SLOTS = (2, 5)


def layer_norm(x, g, b):
    xf = x.astype(jnp.float32)
    mu = jnp.mean(xf, axis=-1, keepdims=True)
    var = jnp.mean(jnp.square(xf - mu), axis=-1, keepdims=True)
    return ((xf - mu) * lax.rsqrt(var + EPS) * g + b).astype(x.dtype)

def diff_attention(q, k, v, lam_vecs, norm_g, lambda_init):
    B, S, H = q.shape[0], q.shape[1], q.shape[2]
    lv = lam_vecs.astype(jnp.float32)
    lam = jnp.exp(jnp.sum(lv[0] * lv[1])) - jnp.exp(jnp.sum(lv[2] * lv[3])) + lambda_init
    slopes = 2.0 ** (-8.0 * (jnp.arange(H, dtype=jnp.float32) + 1.0) / H)
    kf = k.astype(jnp.float32)
    vf = v.astype(jnp.float32)
    kpos = jnp.arange(S)
    nblk = S // Q_BLOCK
    qb = q.astype(jnp.float32).reshape(B, nblk, Q_BLOCK, H, 2, DA_DK).transpose(1, 0, 2, 3, 4, 5)
    scale = DA_DK ** -0.5

    def block(args):
        q_blk, i = args
        qpos = i * Q_BLOCK + jnp.arange(Q_BLOCK)
        dist = (qpos[:, None] - kpos[None, :]).astype(jnp.float32)
        s = jnp.einsum('bqhcd,bkhcd->bhcqk', q_blk, kf) * scale
        s = s - slopes[None, :, None, None, None] * dist[None, None, None]
        s = jnp.where(dist[None, None, None] >= 0, s, -jnp.inf)
        p = jax.nn.softmax(s, axis=-1)
        a = p[:, :, 0] - lam * p[:, :, 1]
        return jnp.einsum('bhqk,bkhe->bqhe', a, vf)

    o = lax.map(block, (qb, jnp.arange(nblk)))
    o = o.transpose(1, 0, 2, 3, 4).reshape(B, S, H, DA_DV)
    o = o * lax.rsqrt(jnp.mean(jnp.square(o), axis=-1, keepdims=True) + EPS) * norm_g
    return (o * (1.0 - lambda_init)).reshape(B, S, H * DA_DV)

def retention(q, k, v, gn_g, gn_b):
    B, S, H, dk = q.shape
    dv = v.shape[-1]
    C = RET_CHUNK
    n = S // C
    log_g = jnp.log(1.0 - 2.0 ** (-5.0 - jnp.arange(H, dtype=jnp.float32)))
    idx = jnp.arange(C, dtype=jnp.float32)
    rel = idx[:, None] - idx[None, :]
    intra = jnp.where(rel[None] >= 0, jnp.exp(rel[None] * log_g[:, None, None]), 0.0)
    q_decay = jnp.exp((idx[:, None] + 1.0) * log_g[None, :])
    k_decay = jnp.exp((C - 1.0 - idx[:, None]) * log_g[None, :])
    chunk_decay = jnp.exp(C * log_g)
    qf = q.astype(jnp.float32)
    kf = k.astype(jnp.float32) * dk ** -0.5
    vf = v.astype(jnp.float32)
    qc = qf.reshape(B, n, C, H, dk).transpose(1, 0, 2, 3, 4)
    kc = kf.reshape(B, n, C, H, dk).transpose(1, 0, 2, 3, 4)
    vc = vf.reshape(B, n, C, H, dv).transpose(1, 0, 2, 3, 4)

    def step(state, inp):
        qi, ki, vi = inp
        s = jnp.einsum('bqhd,bkhd->bhqk', qi, ki) * intra[None]
        o = (jnp.einsum('bhqk,bkhe->bqhe', s, vi)
             + jnp.einsum('bqhd,bhde->bqhe', qi, state) * q_decay[None, :, :, None])
        new_state = (state * chunk_decay[None, :, None, None]
                     + jnp.einsum('bkhd,bkhe->bhde', ki * k_decay[None, :, :, None], vi))
        return new_state, o

    state0 = jnp.zeros((B, H, dk, dv), jnp.float32)
    _, o = lax.scan(step, state0, (qc, kc, vc))
    o = o.transpose(1, 0, 2, 3, 4).reshape(B, S, H, dv)
    mu = jnp.mean(o, axis=-1, keepdims=True)
    var = jnp.mean(jnp.square(o - mu), axis=-1, keepdims=True)
    o = ((o - mu) * lax.rsqrt(var + EPS)).reshape(B, S, H * dv)
    return o * gn_g + gn_b

def memory_attention(q, k, v):
    B, S = q.shape[0], q.shape[1]
    s = jnp.einsum('bshd,bmhd->bhsm', q.astype(jnp.float32), k.astype(jnp.float32)) * MEM_DH ** -0.5
    p = jax.nn.softmax(s, axis=-1)
    o = jnp.einsum('bhsm,bmhd->bshd', p, v.astype(jnp.float32))
    return o.reshape(B, S, MEM_HEADS * MEM_DH)

def hier_moe(x, w_rg, b_rg, w_re, b_re, w1, w3, w2):
    B, S, D = x.shape
    t = x.reshape(B * S, D)
    p_grp = jax.nn.softmax((t @ w_rg + b_rg).astype(jnp.float32), axis=-1)
    p_top, g_idx = lax.top_k(p_grp, 1)
    e_logits = (t @ w_re + b_re).astype(jnp.float32).reshape(B * S, N_GROUPS, EXPERTS_PER_GROUP)
    sel = jnp.take_along_axis(e_logits, g_idx[:, :, None], axis=1)[:, 0]
    p_exp = jax.nn.softmax(sel, axis=-1)
    pe_top, e_idx = lax.top_k(p_exp, EXPERT_TOPK)
    pe_top = pe_top / jnp.sum(pe_top, axis=-1, keepdims=True)
    w_tok = p_top * pe_top
    flat_idx = g_idx * EXPERTS_PER_GROUP + e_idx
    combine = jnp.sum(jax.nn.one_hot(flat_idx, N_EXPERTS, dtype=jnp.float32) * w_tok[..., None], axis=1)
    out = jnp.zeros((B * S, D), jnp.float32)
    for e in range(N_EXPERTS):
        h = jax.nn.silu(t @ w1[e]) * (t @ w3[e])
        out = out + combine[:, e:e + 1] * (h @ w2[e])
    return out.reshape(B, S, D).astype(x.dtype)

def first_inputs(seed: int = 0) -> dict:
    key = jax.random.key(seed)
    ks = jax.random.split(key, 24)
    D = D_MODEL

    def nrm(k, shape, scale):
        return jax.random.normal(k, shape, jnp.float32) * scale

    col_scale = np.concatenate([np.full(sz, DEEPNORM_BETA if i in VALUE_SLOTS else 1.0, np.float32)
                                for i, sz in enumerate(SPLIT_SIZES)])
    mem_scale = np.concatenate([np.ones(D, np.float32), np.full(D, DEEPNORM_BETA, np.float32)])
    return {
        'x': nrm(ks[0], (BATCH, SEQ, D), 1.0),
        'mem': nrm(ks[1], (BATCH, MEM_LEN, D), 1.0),
        'w_in': nrm(ks[2], (DEPTH, D, IN_WIDTH), D ** -0.5) * jnp.asarray(col_scale),
        'b_gate': nrm(ks[3], (DEPTH, N_BRANCH * D), 0.02),
        'w_mem_kv': nrm(ks[4], (DEPTH, D, 2 * D), D ** -0.5) * jnp.asarray(mem_scale),
        'da_lambda': nrm(ks[5], (DEPTH, 4, DA_DK), 0.1),
        'da_norm_g': 1.0 + nrm(ks[6], (DEPTH, DA_DV), 0.02),
        'ret_gn_g': 1.0 + nrm(ks[7], (DEPTH, RET_HEADS * RET_DV), 0.02),
        'ret_gn_b': nrm(ks[8], (DEPTH, RET_HEADS * RET_DV), 0.02),
        'w_branch': nrm(ks[9], (DEPTH, N_BRANCH, BRANCH_W, D), BRANCH_W ** -0.5),
        'w_o': nrm(ks[10], (DEPTH, D, D), D ** -0.5 * DEEPNORM_BETA),
        'ln1_g': 1.0 + nrm(ks[11], (DEPTH, D), 0.02),
        'ln1_b': nrm(ks[12], (DEPTH, D), 0.02),
        'w_rg': nrm(ks[13], (DEPTH, D, N_GROUPS), D ** -0.5),
        'b_rg': nrm(ks[14], (DEPTH, N_GROUPS), 0.01),
        'w_re': nrm(ks[15], (DEPTH, D, N_EXPERTS), D ** -0.5),
        'b_re': nrm(ks[16], (DEPTH, N_EXPERTS), 0.01),
        'w1': nrm(ks[17], (DEPTH, N_EXPERTS, D, D_FF_EXPERT), D ** -0.5),
        'w3': nrm(ks[18], (DEPTH, N_EXPERTS, D, D_FF_EXPERT), D ** -0.5),
        'w2': nrm(ks[19], (DEPTH, N_EXPERTS, D_FF_EXPERT, D), D_FF_EXPERT ** -0.5 * DEEPNORM_BETA),
        'ln2_g': 1.0 + nrm(ks[20], (DEPTH, D), 0.02),
        'ln2_b': nrm(ks[21], (DEPTH, D), 0.02),
    }

def first_block(x, mem, w_in, b_gate, w_mem_kv, da_lambda, da_norm_g, ret_gn_g, ret_gn_b,
              w_branch, w_o, ln1_g, ln1_b, w_rg, b_rg, w_re, b_re, w1, w3, w2, ln2_g, ln2_b):
    B, S, D = x.shape
    M = mem.shape[1]
    for l in range(DEPTH):
        lambda_init = 0.8 - 0.6 * math.exp(-0.3 * l)
        proj = x @ w_in[l]
        da_q, da_k, da_v, r_q, r_k, r_v, r_g, m_q, gate_logits = jnp.split(proj, SPLIT_POINTS, axis=-1)

        y_da = diff_attention(da_q.reshape(B, S, DA_HEADS, 2, DA_DK),
                              da_k.reshape(B, S, DA_HEADS, 2, DA_DK),
                              da_v.reshape(B, S, DA_HEADS, DA_DV),
                              da_lambda[l], da_norm_g[l], lambda_init).astype(x.dtype)

        y_ret = retention(r_q.reshape(B, S, RET_HEADS, RET_DK),
                          r_k.reshape(B, S, RET_HEADS, RET_DK),
                          r_v.reshape(B, S, RET_HEADS, RET_DV),
                          ret_gn_g[l], ret_gn_b[l])
        y_ret = (jax.nn.silu(r_g.astype(jnp.float32)) * y_ret).astype(x.dtype)

        m_k, m_v = jnp.split(mem @ w_mem_kv[l], 2, axis=-1)
        y_mem = memory_attention(m_q.reshape(B, S, MEM_HEADS, MEM_DH),
                                 m_k.reshape(B, M, MEM_HEADS, MEM_DH),
                                 m_v.reshape(B, M, MEM_HEADS, MEM_DH)).astype(x.dtype)

        gates = jax.nn.sigmoid(gate_logits + b_gate[l]).reshape(B, S, N_BRANCH, D)
        branches = jnp.stack([y_da, y_ret, y_mem], axis=2)
        branch_d = jnp.einsum('bsnc,ncd->bsnd', branches, w_branch[l])
        merged = jnp.sum(gates * branch_d, axis=2)
        x = layer_norm(DEEPNORM_ALPHA * x + merged @ w_o[l], ln1_g[l], ln1_b[l])

        y_moe = hier_moe(x, w_rg[l], b_rg[l], w_re[l], b_re[l], w1[l], w3[l], w2[l])
        x = layer_norm(DEEPNORM_ALPHA * x + y_moe, ln2_g[l], ln2_b[l])
    return x


_first_inputs = first_inputs


def first_inputs(seed=0):
    import zlib

    import numpy as np

    out = dict(_first_inputs(seed))
    spreads = {}
    factors = {'mem': 2.814,
     'b_gate': 8.0,
     'w_mem_kv': 2.715,
     'da_lambda': 3.501,
     'da_norm_g': 74.833,
     'ret_gn_g': 106.684,
     'ret_gn_b': 108.9,
     'b_rg': 18.856,
     'b_re': 26.31,
     'ln2_g': 26.042,
     'ln2_b': 24.107}
    for name, (base, spread) in spreads.items():
        noise = np.random.default_rng([zlib.crc32(name.encode()), seed]).standard_normal(out[name].shape)
        drawn = base * np.exp(spread * noise) if base else spread * noise
        out[name] = __import__('jax').numpy.asarray(drawn.astype(out[name].dtype))
    for name, factor in factors.items():
        out[name] = (out[name] * factor).astype(out[name].dtype)
    return out


_narrow_inputs = first_inputs


def first_inputs(seed=0):

    out = dict(_narrow_inputs(seed))
    wider = {'da_norm_g': 3.74, 'ret_gn_g': 3.54, 'ret_gn_b': 3.53, 'ln2_g': 3.34, 'ln2_b': 3.34}
    for name, times in wider.items():
        mean = out[name].mean()
        out[name] = (mean + times * (out[name] - mean)).astype(out[name].dtype)
    return out


DEPTH_2 = 2

GRID_W = 64
CTX_LEN = 256
N_MIXERS = 2
N_HEADS = 16
N_KV_HEADS = 4
HEAD_DIM = 64
GROUP = N_HEADS // N_KV_HEADS
Q_WIDTH = N_HEADS * HEAD_DIM
KV_WIDTH = N_KV_HEADS * HEAD_DIM
WINDOW = 128
BLOCK = 128
SPAN = BLOCK + 2 * WINDOW
ROPE_BASE = 10000.0
AXIS_DIM = HEAD_DIM // 2
FOURIER_GROUPS = 4
FOURIER_GROUP_CH = D_MODEL // FOURIER_GROUPS
D_FF = 2816
N_MOD = 9
LN_EPS = 1e-5
ALPHA = (2.0 * DEPTH_2) ** 0.25
BETA = (8.0 * DEPTH_2) ** -0.25
NEG_INF = -1e30
N_ATTN_LAYERS = (DEPTH_2 + N_MIXERS - 1) // N_MIXERS
N_FOURIER_LAYERS = (DEPTH_2 + N_MIXERS - 2) // N_MIXERS


def layer_norm_2(x, g, b):
    xf = x.astype(jnp.float32)
    mu = xf.mean(-1, keepdims=True)
    var = jnp.square(xf - mu).mean(-1, keepdims=True)
    return ((xf - mu) * lax.rsqrt(var + LN_EPS) * g + b).astype(x.dtype)

def modulate(x, mod, j):
    shift, scale = mod[:, 3 * j], mod[:, 3 * j + 1]
    return x * (1 + scale[:, None, :]) + shift[:, None, :]

def post_norm_update(x, y, mod, j, g, b):
    gate = mod[:, 3 * j + 2][:, None, :]
    return layer_norm_2(ALPHA * x + gate * y, g, b)

def swiglu(h, wi, wo):
    a, g = jnp.split(h @ wi, 2, axis=-1)
    return (a * jax.nn.silu(g)) @ wo

def half_ffn_sublayer(x, mod, j, wi, wo, g, b):
    y = 0.5 * swiglu(modulate(x, mod, j), wi, wo)
    return post_norm_update(x, y, mod, j, g, b)

def axial_rope_tables(n_tokens):
    rows = n_tokens // GRID_W
    row = jnp.repeat(jnp.arange(rows), GRID_W).astype(jnp.float32)
    col = jnp.tile(jnp.arange(GRID_W), rows).astype(jnp.float32)
    inv = ROPE_BASE ** (-jnp.arange(0, AXIS_DIM, 2, dtype=jnp.float32) / AXIS_DIM)
    ang = jnp.concatenate([row[:, None] * inv, col[:, None] * inv], axis=-1)
    return jnp.cos(ang), jnp.sin(ang)

def apply_axial_rope(x, cos, sin):
    B_, L_, H_, Dh = x.shape
    half = AXIS_DIM // 2
    xr = x.astype(jnp.float32).reshape(B_, L_, H_, 2, 2, half)
    x1, x2 = xr[..., 0, :], xr[..., 1, :]
    c = cos.reshape(L_, 1, 2, half)
    s = sin.reshape(L_, 1, 2, half)
    out = jnp.stack([x1 * c - x2 * s, x1 * s + x2 * c], axis=-2)
    return out.reshape(B_, L_, H_, Dh).astype(x.dtype)

def window_sink_attention(h, hc, w_qkv, b_qkv, w_o, sink, cos, sin, ctx_queries):
    B_, S_, _ = h.shape
    C_ = hc.shape[1]
    n_blocks = S_ // BLOCK
    scale = HEAD_DIM ** -0.5
    q, k, v = jnp.split(h @ w_qkv + b_qkv, [Q_WIDTH, Q_WIDTH + KV_WIDTH], axis=-1)
    q = apply_axial_rope(q.reshape(B_, S_, N_HEADS, HEAD_DIM) * scale, cos, sin)
    q = q.reshape(B_, S_, N_KV_HEADS, GROUP, HEAD_DIM)
    k = apply_axial_rope(k.reshape(B_, S_, N_KV_HEADS, HEAD_DIM), cos, sin)
    v = v.reshape(B_, S_, N_KV_HEADS, HEAD_DIM)
    kvc = hc @ w_qkv[:, Q_WIDTH:] + b_qkv[Q_WIDTH:]
    kc, vc = jnp.split(kvc, [KV_WIDTH], axis=-1)
    kc = kc.reshape(B_, C_, N_KV_HEADS, HEAD_DIM)
    vc = vc.reshape(B_, C_, N_KV_HEADS, HEAD_DIM)

    pad = ((0, 0), (WINDOW, WINDOW), (0, 0), (0, 0))
    k_pad = jnp.pad(k, pad)
    v_pad = jnp.pad(v, pad)
    sink_logit = sink.astype(jnp.float32).reshape(1, N_KV_HEADS, GROUP, 1, 1)
    rel = jnp.arange(BLOCK)[:, None] - jnp.arange(SPAN)[None, :] + WINDOW
    band = jnp.abs(rel) <= WINDOW

    def block(bi):
        start = bi * BLOCK
        q_b = lax.dynamic_slice_in_dim(q, start, BLOCK, axis=1)
        k_b = lax.dynamic_slice_in_dim(k_pad, start, SPAN, axis=1)
        v_b = lax.dynamic_slice_in_dim(v_pad, start, SPAN, axis=1)
        key_pos = start - WINDOW + jnp.arange(SPAN)
        valid = band & ((key_pos >= 0) & (key_pos < S_))[None, :]
        s_win = jnp.einsum('bqhgd,bkhd->bhgqk', q_b, k_b, preferred_element_type=jnp.float32)
        s_win = jnp.where(valid, s_win, NEG_INF)
        s_ctx = jnp.einsum('bqhgd,bkhd->bhgqk', q_b, kc, preferred_element_type=jnp.float32)
        sinks = jnp.broadcast_to(sink_logit, s_ctx.shape[:-1] + (1,))
        p = jax.nn.softmax(jnp.concatenate([s_win, s_ctx, sinks], axis=-1), axis=-1).astype(v.dtype)
        o = (jnp.einsum('bhgqk,bkhd->bqhgd', p[..., :SPAN], v_b)
             + jnp.einsum('bhgqk,bkhd->bqhgd', p[..., SPAN:SPAN + C_], vc))
        return o

    o = lax.map(block, jnp.arange(n_blocks))
    o = jnp.moveaxis(o, 0, 1).reshape(B_, S_, Q_WIDTH)
    y = o @ w_o
    if not ctx_queries:
        return y, None
    qc = (hc @ w_qkv[:, :Q_WIDTH] + b_qkv[:Q_WIDTH]) * scale
    qc = qc.reshape(B_, C_, N_KV_HEADS, GROUP, HEAD_DIM)
    sc = jnp.einsum('bqhgd,bkhd->bhgqk', qc, kc, preferred_element_type=jnp.float32)
    sinks_c = jnp.broadcast_to(sink_logit, sc.shape[:-1] + (1,))
    pc = jax.nn.softmax(jnp.concatenate([sc, sinks_c], axis=-1), axis=-1).astype(vc.dtype)
    oc = jnp.einsum('bhgqk,bkhd->bqhgd', pc[..., :C_], vc).reshape(B_, C_, Q_WIDTH)
    return y, oc @ w_o

def fourier_mix(h, w_o):
    B_, L_, D_ = h.shape
    hg = h.astype(jnp.float32).reshape(B_, L_, FOURIER_GROUPS, FOURIER_GROUP_CH)
    f = jnp.fft.fft2(hg, axes=(1, 3), norm="ortho").real
    return f.reshape(B_, L_, D_).astype(h.dtype) @ w_o

def second_inputs(seed: int = 0) -> dict:
    key = jax.random.key(seed)
    ks = jax.random.split(key, 16)

    def nrm(k, shape, s):
        return jax.random.normal(k, shape, jnp.float32) * s

    qkv_w = Q_WIDTH + 2 * KV_WIDTH
    return {
        "x": nrm(ks[0], (BATCH, SEQ, D_MODEL), 1.0),
        "c": nrm(ks[1], (BATCH, D_MODEL), 1.0),
        "ctx": nrm(ks[2], (BATCH, CTX_LEN, D_MODEL), 1.0),
        "c_ctx": nrm(ks[3], (D_MODEL,), 1.0),
        "mod_w": nrm(ks[4], (DEPTH_2, D_MODEL, N_MOD * D_MODEL), D_MODEL ** -0.5),
        "mod_b": nrm(ks[5], (DEPTH_2, N_MOD * D_MODEL), 0.02),
        "ln_g": 1.0 + nrm(ks[6], (DEPTH_2, 3, D_MODEL), 0.02),
        "ln_b": nrm(ks[7], (DEPTH_2, 3, D_MODEL), 0.02),
        "ffn_wi": nrm(ks[8], (DEPTH_2, 2, D_MODEL, 2 * D_FF), D_MODEL ** -0.5),
        "ffn_wo": nrm(ks[9], (DEPTH_2, 2, D_FF, D_MODEL), BETA * D_FF ** -0.5),
        "attn_wqkv": nrm(ks[10], (N_ATTN_LAYERS, D_MODEL, qkv_w), D_MODEL ** -0.5),
        "attn_bqkv": nrm(ks[11], (N_ATTN_LAYERS, qkv_w), 0.02),
        "attn_wo": nrm(ks[12], (N_ATTN_LAYERS, Q_WIDTH, D_MODEL), BETA * Q_WIDTH ** -0.5),
        "attn_sink": nrm(ks[13], (N_ATTN_LAYERS, N_HEADS), 1.0),
        "fourier_wo": nrm(ks[14], (N_FOURIER_LAYERS, D_MODEL, D_MODEL), BETA * D_MODEL ** -0.5),
    }

def second_block(x, c, ctx, c_ctx, mod_w, mod_b, ln_g, ln_b, ffn_wi, ffn_wo,
              attn_wqkv, attn_bqkv, attn_wo, attn_sink, fourier_wo):
    cos, sin = axial_rope_tables(x.shape[1])
    silu_c = jax.nn.silu(c)
    silu_cc = jax.nn.silu(c_ctx)
    ctx_s = ctx
    for i in range(DEPTH_2):
        kind = i % N_MIXERS
        ctx_out_live = any(j % N_MIXERS == 0 for j in range(i + 1, DEPTH_2))
        ctx_in_live = (kind == 0) or ctx_out_live
        g, b = ln_g[i], ln_b[i]
        mod_lat = (silu_c @ mod_w[i] + mod_b[i]).reshape(-1, N_MOD, D_MODEL)
        x = half_ffn_sublayer(x, mod_lat, 0, ffn_wi[i, 0], ffn_wo[i, 0], g[0], b[0])
        if ctx_in_live:
            mod_ctx = (silu_cc @ mod_w[i] + mod_b[i]).reshape(1, N_MOD, D_MODEL)
            ctx_s = half_ffn_sublayer(ctx_s, mod_ctx, 0, ffn_wi[i, 0], ffn_wo[i, 0], g[0], b[0])
        h = modulate(x, mod_lat, 1)
        if kind == 0:
            a = i // N_MIXERS
            y, yc = window_sink_attention(h, modulate(ctx_s, mod_ctx, 1), attn_wqkv[a], attn_bqkv[a],
                                          attn_wo[a], attn_sink[a], cos, sin, ctx_out_live)
        else:
            f = i // N_MIXERS
            y = fourier_mix(h, fourier_wo[f])
            yc = fourier_mix(modulate(ctx_s, mod_ctx, 1), fourier_wo[f]) if ctx_out_live else None
        x = post_norm_update(x, y, mod_lat, 1, g[1], b[1])
        x = half_ffn_sublayer(x, mod_lat, 2, ffn_wi[i, 1], ffn_wo[i, 1], g[2], b[2])
        if ctx_out_live:
            ctx_s = post_norm_update(ctx_s, yc, mod_ctx, 1, g[1], b[1])
            ctx_s = half_ffn_sublayer(ctx_s, mod_ctx, 2, ffn_wi[i, 1], ffn_wo[i, 1], g[2], b[2])
    return x


def setup_inputs(seed=0):
    out = dict(first_inputs(seed))
    for name, value in second_inputs(seed + 1).items():
        if name != "x":
            out[name + "_2"] = value
    return out


def reference(
    x, mem, w_in, b_gate, w_mem_kv, da_lambda, da_norm_g, ret_gn_g, ret_gn_b, w_branch, w_o,
    ln1_g, ln1_b, w_rg, b_rg, w_re, b_re, w1, w3, w2, ln2_g, ln2_b, c_2, ctx_2, c_ctx_2,
    mod_w_2, mod_b_2, ln_g_2, ln_b_2, ffn_wi_2, ffn_wo_2, attn_wqkv_2, attn_bqkv_2, attn_wo_2,
    attn_sink_2, fourier_wo_2,
):
    x = first_block(
        x, mem, w_in, b_gate, w_mem_kv, da_lambda, da_norm_g, ret_gn_g, ret_gn_b, w_branch, w_o,
        ln1_g, ln1_b, w_rg, b_rg, w_re, b_re, w1, w3, w2, ln2_g, ln2_b,
    )
    return second_block(
        x, c_2, ctx_2, c_ctx_2, mod_w_2, mod_b_2, ln_g_2, ln_b_2, ffn_wi_2, ffn_wo_2,
        attn_wqkv_2, attn_bqkv_2, attn_wo_2, attn_sink_2, fourier_wo_2,
    )


_drawn_inputs = setup_inputs


def setup_inputs(seed=0):
    import zlib

    import numpy as np

    out = dict(_drawn_inputs(seed))
    spreads = {}
    factors = {'attn_bqkv_2': 8.0, 'attn_sink_2': 8.0}
    for name, (base, spread) in spreads.items():
        noise = np.random.default_rng([zlib.crc32(name.encode()), seed]).standard_normal(out[name].shape)
        drawn = base * np.exp(spread * noise) if base else spread * noise
        out[name] = __import__('jax').numpy.asarray(drawn.astype(out[name].dtype))
    for name, factor in factors.items():
        out[name] = (out[name] * factor).astype(out[name].dtype)
    return out
```

```python
from contextlib import ExitStack

import numpy as np

import concourse.bass as bass
from concourse import mybir

F32 = mybir.dt.float32
F32R = mybir.dt.float32r
ALU = mybir.AluOpType
ACT = mybir.ActivationFunctionType
AX = mybir.AxisListType

P = 128
BANK = 512
PIECE = 2048
RAW_SLOTS = 4
SPLIT_SLOTS = 4
SEQ = 256
NT = SEQ // P
D = 1024
KD = D // P
KH = KD // 2
EPS = 1e-5
MASKED = 1e30

DA_HEADS, DA_DK, DA_DV = 8, 64, 128
RET_HEADS, RET_DK, RET_DV = 4, 128, 256
MEM_HEADS, MEM_DH = 4, 256
N_GROUPS, PER_GROUP, N_EXPERTS = 4, 4, 16
D_FF_EXPERT = 512
LAMBDA_INIT = 0.2
ALPHA_1 = 2.0 ** 0.25
ALPHA_2 = 4.0 ** 0.25
N_HEADS, N_KV, HEAD_DIM, GROUP = 16, 4, 64, 4
WINDOW = 128
D_FF = 2816
F_CHUNK = 256
GRID_W, ROPE_BASE, AXIS_DIM = 64, 10000.0, 32
N_MOD = 9


def constants():
    q = np.arange(P, dtype=np.float64)[:, None]
    dist = (P + q) - np.arange(SEQ)[None, :]
    dist = np.where(dist >= 0, dist, MASKED)
    log_g = np.log(1.0 - 2.0 ** (-5.0 - np.arange(RET_HEADS)))
    k = np.arange(P)[:, None]
    qq = np.arange(P)[None, :]
    decay = []
    for h in range(RET_HEADS):
        diagonal = np.where(qq >= k, np.exp((qq - k) * log_g[h]), 0.0)
        behind = np.exp((P + qq - k) * log_g[h])
        decay.append(np.stack([diagonal, behind], axis=1))
    decay = np.stack(decay, axis=1) * RET_DK ** -0.5
    key = np.arange(P)[None, :]
    window = np.stack([np.where(key <= q, 0.0, -MASKED), np.where(key >= q, 0.0, -MASKED)], axis=1)
    tok = np.arange(SEQ)
    inv = ROPE_BASE ** (-np.arange(0, AXIS_DIM, 2) / AXIS_DIM)
    inv = inv.astype(np.float32)
    ang = np.concatenate([(tok // GRID_W)[:, None].astype(np.float32) * inv,
                          (tok % GRID_W)[:, None].astype(np.float32) * inv], axis=-1)
    cos, sin = np.cos(ang), np.sin(ang)
    rope = np.stack([cos, sin, cos * HEAD_DIM ** -0.5, sin * HEAD_DIM ** -0.5], axis=1)
    turn = 2.0 * np.pi * ((tok[:, None] * tok[None, :]) % SEQ) / SEQ
    dft = np.concatenate([np.cos(turn), np.sin(turn)], axis=1)
    out = {"dist": dist, "decay": decay, "window": window, "rope": rope, "dft": dft,
           "ident": np.eye(P), "index": np.tile(np.arange(N_GROUPS), (P, 1))}
    return {n: np.ascontiguousarray(a, dtype=np.float32) for n, a in out.items()}


class Queue:

    def __init__(self, name):
        self.name, self.count, self.steps, self.seen = name, 0, [], {}

    def wait(self, *after):
        last = {}
        for sem, value in flat(after):
            last[sem] = max(last.get(sem, 0), value)
        for sem, value in last.items():
            if self.seen.get(sem, 0) < value:
                self.seen[sem] = value
                self.steps.append(("wait", sem, value))

    def do(self, issue, *after):
        self.wait(*after)
        self.count += 1
        self.steps.append(("do", issue, self.name))
        return (self.name, self.count)

    def run(self, engine, sems):
        for kind, a, b in self.steps:
            if kind == "wait":
                engine.wait_ge(sems[a], b)
            elif kind == "do":
                a(engine).then_inc(sems[b], 1)
            else:
                a(engine).then_inc(sems[b], 16)


def flat(tokens):
    for t in tokens:
        if t is None:
            continue
        if isinstance(t, list):
            yield from flat(t)
        else:
            yield t


class Banks(dict):

    def __setitem__(self, bank, token):
        if token is not None:
            super().__setitem__(bank, token)
            self.held.discard(bank)


class Program:
    def __init__(self, dram, mem, plan, stop):
        self.dram, self.m, self.plan, self.stop = dram, mem, plan, stop
        self.pe, self.act, self.dve = Queue("pe"), Queue("act"), Queue("dve")
        self.sync, self.pool = Queue("sync"), Queue("pool")
        self.sems = {"pe", "act", "dve"}
        self.taken, self.loaded, self.split = [], 0, 0
        self.raw_full, self.raw_free = {}, {}
        self.half_full, self.half_free = {}, {}
        self.raw_count = [0] * RAW_SLOTS
        self.is_split = [p[1] for p in plan or []]
        self.split_slot = list(np.cumsum([0] + self.is_split)[:-1])
        self.bank_free, self.held = Banks(), set()
        self.bank_free.held = self.held
        self.ring, self.ring_at = list(range(8)), 0
        self.freed = {}
        self.stores = []

    def load(self, name, dst, src, *after, queue=None):
        q = queue or self.pool
        q.wait(*after)
        sem = f"ld_{name}"
        assert sem not in self.sems
        self.sems.add(sem)
        q.steps.append(("dma", lambda e: e.dma_start(dst, src), sem))
        return (sem, 16)

    def take(self, sources, split=True, size=PIECE):
        n = len(self.taken)
        self.taken.append((sources, split, size))
        if self.plan is None:
            return n
        self.run_ahead()
        return n

    def run_ahead(self):
        plan = self.plan
        while True:
            moved = False
            n = self.loaded
            if n < len(plan) and (n < RAW_SLOTS or (n - RAW_SLOTS) in self.raw_free):
                slot = n % RAW_SLOTS
                if n >= RAW_SLOTS:
                    self.sync.wait(self.raw_free[n - RAW_SLOTS])
                sem = f"raw{slot}"
                self.sems.add(sem)
                for view, src in plan[n][0]:
                    dst = view(self.m["raw"][:, slot, :])
                    self.sync.steps.append(("dma", lambda e, dst=dst, src=src: e.dma_start(dst, src), sem))
                    self.raw_count[slot] += 16
                self.raw_full[n] = (sem, self.raw_count[slot])
                self.loaded += 1
                moved = True
            n = self.split
            if n < self.loaded:
                if not self.is_split[n]:
                    self.split += 1
                    moved = True
                else:
                    s = self.split_slot[n]
                    if s < SPLIT_SLOTS or (s - SPLIT_SLOTS) in self.half_free:
                        self.split_piece(n, s)
                        self.split += 1
                        moved = True
            if not moved:
                return

    def split_piece(self, n, s):
        raw = self.m["raw"][:, n % RAW_SLOTS, :]
        hi, lo = self.m["hi"][:, s % SPLIT_SLOTS, :], self.m["lo"][:, s % SPLIT_SLOTS, :]
        used = self.plan[n][2]
        if used < PIECE:
            raw, hi, lo = raw[:, 0:used], hi[:, 0:used], lo[:, 0:used]
        free = self.half_free.get(s - SPLIT_SLOTS)
        a = self.act.do(lambda e: e.activation(hi, raw, ACT.Copy), self.raw_full[n], free)
        b = self.dve.do(lambda e: e.tensor_tensor(lo, raw, hi.bitcast(F32), ALU.subtract), a)
        self.half_full[n] = [a, b]
        self.raw_free[n] = b

    def halves(self, n):
        if self.plan is None:
            s = 0
        else:
            s = self.split_slot[n] % SPLIT_SLOTS
        return self.m["hi"][:, s, :], self.m["lo"][:, s, :]

    def full(self, n):
        return [] if self.plan is None else self.half_full[n]

    def done_with(self, n, token):
        if self.plan is not None:
            self.half_free[self.split_slot[n]] = token

    def bank(self):
        b = self.ring[self.ring_at % len(self.ring)]
        while b in self.held:
            self.ring_at += 1
            b = self.ring[self.ring_at % len(self.ring)]
        self.ring_at += 1
        self.held.add(b)
        return b, self.bank_free.get(b)

    def use_ring(self, banks):
        self.ring, self.ring_at = list(banks), 0

    def ps(self, b):
        return self.m["psum"][b]

    def gemm_token(self, lhs, weights, evacuate):
        hi, lo, ready = lhs
        for c, (first, second) in enumerate(weights):
            banks = [self.bank() for _ in range(NT)]
            for part, sources in enumerate((first, second)):
                n = self.take(sources)
                wh, wl = self.halves(n)
                wh = wh.rearrange("p (k n) -> p k n", k=KH)
                wl = wl.rearrange("p (k n) -> p k n", k=KH)
                frees = [f for _, f in banks] if part == 0 else None

                def issue(e, part=part, wh=wh, wl=wl, banks=banks):
                    for t in range(NT):
                        for k in range(KH):
                            kk = part * KH + k
                            tok = slice(t * P, t * P + P)
                            for i, (a, b) in enumerate(((hi, wh), (hi, wl), (lo, wh))):
                                last = e.matmul(self.ps(banks[t][0])[:], a[:, kk, tok], b[:, k, :],
                                                start=(kk == 0 and i == 0), stop=(kk == KD - 1 and i == 2))
                    return last
                done = self.pe.do(issue, self.full(n), ready, frees)
                self.done_with(n, done)
                yield
            for t in range(NT):
                self.bank_free[banks[t][0]] = evacuate(c, t, self.ps(banks[t][0]), done)

    def gemm_feature(self, lhs, weights, evacuate, bias=None):
        hi, lo, ready = lhs
        for c, (first, second) in enumerate(weights):
            banks = [self.bank() for _ in range(2)]
            n0 = self.take(first)
            yield
            n1 = self.take(second)
            parts = [[x.rearrange("p (k n) -> p k n", k=KH) for x in self.halves(n)] for n in (n0, n1)]

            def issue(e, m, parts=parts, banks=banks):
                out = self.ps(banks[m // 2][0])[:, (m % 2) * SEQ:(m % 2) * SEQ + SEQ]
                for kk in range(KD):
                    wh, wl = parts[kk // KH]
                    cols = slice(m * P, m * P + P)
                    for i, (a, b) in enumerate(((hi, wh), (hi, wl), (lo, wh))):
                        last = e.matmul(out, b[:, kk % KH, cols], a[:, kk, :], start=(kk == 0 and i == 0),
                                        stop=(kk == KD - 1 and i == 2))
                return last
            for m in range(4):
                done = self.pe.do(lambda e, m=m, issue=issue: issue(e, m), self.full(n0), self.full(n1), ready,
                                  [f for _, f in banks])
                if m % 2:
                    b = banks[m // 2][0]
                    self.bank_free[b] = evacuate(c, m // 2, self.ps(b), done)
            self.done_with(n0, done)
            self.done_with(n1, done)
            yield

    def to_lhs(self, src, ready, dst, free, affine=None):
        hi, lo = dst
        m = self.m
        tokens = []
        for j in range(KD // 2):
            b, bank_free = self.bank()
            ps = self.ps(b)

            def turn(e, j=j, ps=ps):
                for k in range(2):
                    for t in range(NT):
                        kk = 2 * j + k
                        last = e.transpose(ps[:, k * SEQ + t * P:k * SEQ + t * P + P],
                                           src[:, t, kk * P:kk * P + P], m["ident"][:])
                return last
            turned = self.pe.do(turn, ready, self.const, bank_free)
            value, at, last_read = ps[:], turned, None
            if affine is not None:
                scale, shift, known = affine
                tmp = m["ex"][:, j % 2, :]
                for k in range(2):
                    kk = 2 * j + k
                    s = slice(k * SEQ, k * SEQ + SEQ)
                    at = self.dve.do(lambda e, s=s, kk=kk, tmp=tmp, ps=ps: e.tensor_scalar(
                        tmp[:, s], ps[:, s], scale[:, kk:kk + 1], shift[:, kk:kk + 1], ALU.mult, ALU.add),
                        turned, known, self.freed.get("ex"), tokens[2 * j - 4:2 * j - 2] if j >= 2 else None)
                self.bank_free[b] = at
                value = tmp
            h, l = hi[:, 2 * j:2 * j + 2, :], lo[:, 2 * j:2 * j + 2, :]
            a = self.act.do(lambda e, h=h, value=value: e.activation(h, value, ACT.Copy), at, free)
            d = self.dve.do(lambda e, h=h, l=l, value=value: e.tensor_tensor(l, value, h.bitcast(F32), ALU.subtract),
                            a, free)
            if affine is None:
                self.bank_free[b] = d
            tokens += [a, d]
        self.freed["ex"] = [self.freed.get("ex"), tokens]
        return (hi, lo, tokens)

    def latest(self):
        return [(q.name, q.count) for q in (self.pe, self.act, self.dve) if q.count]

    def inverse_root(self, x, eps, scratch, after):
        a = self.dve.do(lambda e: e.tensor_scalar(scratch, x, eps, None, ALU.add), after)
        b = self.act.do(lambda e: e.activation(scratch, scratch, ACT.Sqrt), a)
        return self.dve.do(lambda e: e.reciprocal(scratch, scratch), b)

    def layer_norm(self, x, ready, g, b, rows):
        m = self.m
        tokens = []
        for t in range(NT):
            for h in range(2):
                tokens.append(self.dve.do(lambda e, t=t, h=h: e.bn_stats(
                    m["bn"][:, t, h, :], x[:, t, h * BANK:(h + 1) * BANK]), ready[t]))
        agg = [self.dve.do(lambda e, t=t: e.bn_aggr(m["mv"][:, t, :], m["bn"][:, t, :, :]), tokens) for t in range(NT)]
        rstd = m["rstd"][:, 0:NT]
        r = self.inverse_root(m["mv"][:, :, 1], EPS, rstd, agg)
        nb = self.dve.do(lambda e: e.scalar_tensor_tensor(out=m["nb"][:, 0:NT], in0=m["mv"][:, :, 0], scalar=-1.0,
                                                          in1=rstd, op0=ALU.mult, op1=ALU.mult), r)
        out = []
        for t in range(NT):
            n = self.dve.do(lambda e, t=t: e.tensor_scalar(x[:, t, :], x[:, t, :], m["rstd"][:, t:t + 1],
                                                           m["nb"][:, t:t + 1], ALU.mult, ALU.add), nb)
            n = self.dve.do(lambda e, t=t: e.tensor_tensor(x[:, t, :], x[:, t, :], g, ALU.mult), n, rows)
            out.append(self.dve.do(lambda e, t=t: e.tensor_tensor(x[:, t, :], x[:, t, :], b, ALU.add), n))
        self.freed["rows"] = out
        return out

    def rows(self, name, g, b):
        m = self.m
        free = self.freed.get("rows")
        a = self.load(name + "_g", m["row_g"][:], g.partition_broadcast(P), free)
        c = self.load(name + "_b", m["row_b"][:], b.partition_broadcast(P), free)
        return m["row_g"][:], m["row_b"][:], [a, c]


def whole(n):
    return lambda slot: slot.rearrange("p (k n) -> p k n", n=n)


def column_pieces(w, c0):
    v = w.rearrange("(k p) n -> p k n", p=P)
    return [[(whole(BANK), v[:, part * KH:(part + 1) * KH, c0:c0 + BANK])] for part in range(2)]


def columns(w, c0, n):
    return [column_pieces(w, c0 + c * BANK) for c in range(n // BANK)]


def drain(steps):
    for _ in steps:
        pass


def step(steps):
    next(steps, None)


def mover(queue):
    if queue.name == "act":
        return lambda dst, src, *after: queue.do(lambda e: e.activation(dst, src, ACT.Copy), *after)
    return lambda dst, src, *after: queue.do(lambda e: e.tensor_copy(dst, src), *after)


class Blocks(Program):

    def claim(self, *names):
        return [self.freed.get(n) for n in names]

    def release(self, *names):
        for n in names:
            self.freed[n] = self.latest()

    def tok(self, name):
        return self.m[name][:].rearrange("p (t n) -> p t n", t=NT)

    def feat(self, name, tokens=SEQ):
        return self.m[name][:].rearrange("p (k s) -> p k s", s=tokens)

    def begin(self):
        d, m = self.dram, self.m
        self.const = self.load("ident", m["ident"][:], d["ident"], queue=self.act)
        mem = self.load("mem", self.tok("b4"), d["mem"][0].rearrange("(t p) n -> p t n", p=P), queue=self.act)
        self.x_in = self.load("x", self.tok("x"), d["x"][0].rearrange("(t p) n -> p t n", p=P), queue=self.act)
        self.mem_in = mem
        self.ones = self.dve.do(lambda e: e.memset(m["ones"][:], 1.0))
        self.tables = [self.load("dist", m["dist"][:], d["dist"]),
                       self.load("decay", m["decay"][:], d["decay"].rearrange("p h w n -> p (h w n)")),
                       self.load("window", m["window"][:], d["window"]),
                       self.load("rope", m["rope"][:], d["rope"].rearrange("(t p) w n -> p t w n", p=P)),
                       self.load("index", m["index"][:], d["index"])]

    def first_block(self):
        d, m = self.dram, self.m
        w_in, w_kv = d["w_in"][0], d["w_mem_kv"][0]
        x = self.tok("x")
        mem_t = self.to_lhs(self.tok("b4"), self.mem_in, (m["yt_hi"], m["yt_lo"]), None)
        self.release("b4")
        self.xt = self.to_lhs(x, self.x_in, (m["xt_hi"], m["xt_lo"]), None)

        act_move, dve_move = mover(self.act), mover(self.dve)
        k_f, v_t, q_f = self.feat("b2"), self.tok("b3"), self.feat("b0")
        made = {"k": [], "v": [], "q": [], "gate": []}

        def to_feat(dst, key, free):
            def evacuate(c, pair, ps, done):
                f = 4 * c + 2 * pair
                token = act_move(dst[:, f:f + 2, :], ps[:], done, free)
                made[key].append(token)
                return token
            return evacuate

        def to_tok(dst, key, free, func=ACT.Copy):
            def evacuate(c, t, ps, done):
                token = self.act.do(lambda e: e.activation(dst[:, t, c * BANK:(c + 1) * BANK], ps[:], func),
                                    done, free)
                made[key].append(token)
                return token
            return evacuate
        drain(self.gemm_feature(mem_t, columns(w_kv, 0, D), to_feat(k_f, "k", self.claim("b2"))))
        drain(self.gemm_token(mem_t, columns(w_kv, D, D), to_tok(v_t, "v", self.claim("b3"))))
        self.release("b0", "b1")
        drain(self.gemm_feature(self.xt, columns(w_in, 6 * D, D), to_feat(q_f, "q", self.claim("b0"))))
        y = self.tok("b4")
        free = self.claim("b4")
        written = self.softmax_heads(self.memory_units(q_f, k_f, v_t, y, made, free), None)
        self.release("b0", "b1", "b2", "b3")
        yt = self.to_lhs(y, written, (m["yt_hi"], m["yt_lo"]), self.claim("b0", "b1"))
        self.release("b4")
        drain(self.gates(2, "b2"))
        self.branch(2, yt, "b2", first=True)
        if self.stop == "mem":
            return

        made.update({"k": [], "v": [], "q": []})
        q_f, k_f, v_t, y = self.feat("b0"), self.feat("b1"), self.tok("b2"), self.tok("b3")
        drain(self.gemm_feature(self.xt, columns(w_in, 0, D), to_feat(q_f, "q", self.claim("b0"))))
        drain(self.gemm_feature(self.xt, columns(w_in, D, D), to_feat(k_f, "k", self.claim("b1"))))
        drain(self.gemm_token(self.xt, columns(w_in, 2 * D, D), to_tok(v_t, "v", self.claim("b2"))))
        lam = self.lambda_full()
        filler = self.gates(0, "b4")
        written = self.softmax_heads(self.differential_units(q_f, k_f, v_t, y, made, self.claim("b3"), lam), filler)
        drain(filler)
        written = self.differential_norm(y, written)
        self.release("b0", "b1", "b2")
        yt = self.to_lhs(y, written, (m["yt_hi"], m["yt_lo"]), self.claim("b0", "b1"))
        self.release("b3")
        self.branch(0, yt, "b4", first=False)

        made.update({"k": [], "v": [], "q": []})
        qk, v_t, y = self.feat("b0"), self.tok("b1"), self.tok("b3")
        gate_silu = self.tok("b2")
        g, b, rows = self.rows("gn", d["ret_gn_g"][0], d["ret_gn_b"][0])
        drain(self.gemm_feature(self.xt, columns(w_in, 3 * D, D), to_feat(qk, "q", self.claim("b0"))))
        drain(self.gemm_token(self.xt, columns(w_in, 4 * D, D), to_tok(v_t, "v", self.claim("b1"))))
        filler = self.then(self.gemm_token(self.xt, columns(w_in, 5 * D, D),
                                           to_tok(gate_silu, "gate", self.claim("b2"), ACT.Silu)),
                           self.gates(1, "b4"))
        written = self.retention(qk, v_t, y, made, self.claim("b3"), filler)
        drain(filler)
        written = self.retention_norm(y, written, gate_silu, made["gate"], g, b, rows)
        self.release("b0", "b1", "b2", "xt")
        yt = self.to_lhs(y, written, (m["yt_hi"], m["yt_lo"]), self.claim("b0", "b1"))
        self.release("b3")
        self.branch(1, yt, "b4", first=False)

        g, b, rows = self.rows("ln1", d["ln1_g"][0], d["ln1_b"][0])
        yt = self.to_lhs(self.tok("mg"), self.merged, (m["yt_hi"], m["yt_lo"]), self.claim("b0", "b1"))
        self.release("mg")
        sums = [[] for _ in range(NT)]

        def residual(c, t, ps, done):
            s = slice(c * BANK, (c + 1) * BANK)
            token = self.dve.do(lambda e: e.scalar_tensor_tensor(out=x[:, t, s], in0=x[:, t, s], scalar=ALPHA_1,
                                                                 in1=ps[:], op0=ALU.mult, op1=ALU.add), done)
            sums[t].append(token)
            return token
        drain(self.gemm_token(yt, columns(d["w_o"][0], 0, D), residual))
        self.release("b0", "b1")
        x_ready = self.layer_norm(x, sums, g, b, rows)
        self.xt = self.to_lhs(x, x_ready, (m["xt_hi"], m["xt_lo"]), self.claim("xt"))
        if self.stop == "ln1":
            return
        self.experts(x, x_ready)

    def then(self, *parts):
        for p in parts:
            yield from p

    def gates(self, n, name):
        d, m = self.dram, self.m
        dst, free = self.tok(name), self.claim(name)
        row = self.load(f"gate{n}", m["row_c"][:], d["b_gate"][0, n * D:(n + 1) * D].partition_broadcast(P),
                        self.freed.get("row_c"))
        self.logits = []

        def evacuate(c, t, ps, done):
            s = slice(c * BANK, (c + 1) * BANK)
            token = self.dve.do(lambda e: e.tensor_tensor(dst[:, t, s], ps[:], m["row_c"][:, s], ALU.add),
                                done, free, row)
            self.logits.append(token)
            self.freed["row_c"] = token
            return token
        yield from self.gemm_token(self.xt, columns(d["w_in"][0], 7 * D + n * D, D), evacuate)

    def branch(self, n, yt, gate_name, first):
        m = self.m
        gate, merged = self.tok(gate_name), self.tok("mg")
        known = [self.act.do(lambda e, t=t: e.activation(gate[:, t, :], gate[:, t, :], ACT.Sigmoid), self.logits)
                 for t in range(NT)]
        out = []

        def evacuate(c, t, ps, done):
            s = slice(c * BANK, (c + 1) * BANK)
            if first:
                token = self.dve.do(lambda e: e.tensor_tensor(merged[:, t, s], ps[:], gate[:, t, s], ALU.mult),
                                    done, known)
                out.append(token)
                return token
            tmp = m["sm"][:, t, :]
            token = self.dve.do(lambda e: e.tensor_tensor(tmp, ps[:], gate[:, t, s], ALU.mult), done, known,
                                self.claim("sm"))
            out.append(self.dve.do(lambda e: e.tensor_tensor(merged[:, t, s], merged[:, t, s], tmp, ALU.add),
                                   token, self.merged))
            return token
        drain(self.gemm_token(yt, columns(self.dram["w_branch"][0, n], 0, D), evacuate))
        self.merged = out
        self.freed["sm"] = out
        self.release("b0", "b1", gate_name)

    def softmax_heads(self, units, filler):
        units = list(units)
        written = []
        scored = units[0][0](0)
        for u, (_, weigh, mix) in enumerate(units):
            weighed = weigh(u, scored)
            if u + 1 < len(units):
                scored = units[u + 1][0](u + 1)
            if filler is not None:
                step(filler)
            written.append(mix(u, weighed))
        return written

    def mix_weights(self, u, weights, known, n_blocks, values, ready):
        m = self.m
        b, free = self.bank()
        ps = self.ps(b)

        def turn(e):
            for k in range(n_blocks):
                last = e.transpose(ps[:, k * P:k * P + P], weights[:, k * P:k * P + P], m["ident"][:])
            return last
        turned = self.pe.do(turn, known, free, self.const)
        at = m["at"][:, u % 2, 0:n_blocks * P]
        copied = self.dve.do(lambda e: e.tensor_copy(at, ps[:, 0:n_blocks * P]), turned,
                             self.freed.get(f"at{u % 2}"))
        self.bank_free[b] = copied
        o, free = self.bank()
        out = self.ps(o)[:, 0:values[0].shape[-1]]

        def mix(e):
            for k in range(n_blocks):
                last = e.matmul(out, at[:, k * P:k * P + P], values[k], start=(k == 0), stop=(k == n_blocks - 1))
            return last
        mixed = self.pe.do(mix, copied, free, ready)
        self.freed[f"at{u % 2}"] = mixed
        return o, out, mixed, turned

    def memory_units(self, q_f, k_f, v_t, y, made, free):
        m = self.m
        scale = MEM_DH ** -0.5
        for h in range(MEM_HEADS):
            for t in range(NT):
                def score(u, h=h, t=t):
                    b, bank_free = self.bank()

                    def issue(e):
                        for k in range(2):
                            last = e.matmul(self.ps(b)[:, 0:SEQ], q_f[:, 2 * h + k, t * P:t * P + P],
                                            k_f[:, 2 * h + k, :], start=(k == 0), stop=(k == 1))
                        return last
                    return b, self.pe.do(issue, bank_free, made["q"], made["k"])

                def weigh(u, scored):
                    b, done = scored
                    st = m["st"][:, u % 2, :]
                    ps, ex = self.ps(b)[:, 0:SEQ], m["ex"][:, u % 2, 0:SEQ]
                    a = self.dve.do(lambda e: e.tensor_reduce(st[:, 0:1], ps, AX.X, ALU.max, negate=True), done,
                                    self.freed.get(f"st{u % 2}"))
                    a = self.dve.do(lambda e: e.tensor_scalar(st[:, 1:2], st[:, 0:1], scale, None, ALU.mult), a)
                    a = self.act.do(lambda e: e.activation(ex, ps, ACT.Exp, bias=st[:, 1:2], scale=scale,
                                                           accum_out=st[:, 2:3]), a, self.freed.get(f"ex{u % 2}"),
                                    self.claim("ex"))
                    self.bank_free[b] = a
                    r = self.dve.do(lambda e: e.reciprocal(st[:, 3:4], st[:, 2:3]), a)
                    return ex, a, r, st

                def mix(u, weighed, h=h, t=t):
                    ex, known, r, st = weighed
                    values = [v_t[:, k, h * MEM_DH:(h + 1) * MEM_DH] for k in range(2)]
                    b, out, mixed, turned = self.mix_weights(u, ex, known, 2, values, made["v"])
                    self.freed[f"ex{u % 2}"] = turned
                    a = self.act.do(lambda e: e.activation(y[:, t, h * MEM_DH:(h + 1) * MEM_DH], out, ACT.Copy,
                                                           scale=st[:, 3:4]), mixed, r, free)
                    self.bank_free[b] = a
                    self.freed[f"st{u % 2}"] = a
                    return a
                yield score, weigh, mix

    def lambda_full(self):
        d, m = self.dram, self.m
        lv = m["row_c"][:, 0:4 * DA_DK]
        got = self.load("lambda", lv, d["da_lambda"][0].rearrange("a b -> (a b)").partition_broadcast(P),
                        self.freed.get("row_c"))
        g = self.load("da_g", m["da_g"][:], d["da_norm_g"][0].partition_broadcast(P))
        v = lv.rearrange("p (a b n) -> p a b n", a=2, b=2)
        tmp = m["sm"][:, 0, 0:2 * DA_DK].rearrange("p (a n) -> p a n", a=2)
        a = self.dve.do(lambda e: e.tensor_tensor(tmp, v[:, :, 0, :], v[:, :, 1, :], ALU.mult), got,
                        self.claim("sm"))
        self.freed["row_c"] = a
        lam = m["lam"]
        a = self.dve.do(lambda e: e.tensor_reduce(lam[:, 0:2], tmp, AX.X, ALU.add), a)
        self.freed["sm"] = a
        a = self.act.do(lambda e: e.activation(lam[:, 2:4], lam[:, 0:2], ACT.Exp), a)
        a = self.dve.do(lambda e: e.tensor_tensor(lam[:, 4:5], lam[:, 3:4], lam[:, 2:3], ALU.subtract), a)
        a = self.dve.do(lambda e: e.tensor_scalar(lam[:, 5:6], lam[:, 4:5], -LAMBDA_INIT, None, ALU.add), a)
        self.da_gain = self.dve.do(lambda e: e.tensor_scalar(m["da_g"][:], m["da_g"][:], 1.0 - LAMBDA_INIT, None,
                                                             ALU.mult), g)
        return a

    def differential_units(self, q_f, k_f, v_t, y, made, free, lam):
        m = self.m
        scale = DA_DK ** -0.5
        for h in range(DA_HEADS):
            for t in range(NT):
                nk = (t + 1) * P

                def score(u, h=h, t=t, nk=nk):
                    banks = [self.bank() for _ in range(2)]

                    def issue(e):
                        for c in range(2):
                            rows = slice(c * DA_DK, (c + 1) * DA_DK)
                            last = e.matmul(self.ps(banks[c][0])[:, 0:nk], q_f[rows, h, t * P:t * P + P],
                                            k_f[rows, h, 0:nk], start=True, stop=True)
                        return last
                    return banks, self.pe.do(issue, [f for _, f in banks], made["q"], made["k"])

                def weigh(u, scored, h=h, nk=nk):
                    banks, done = scored
                    st = m["st"][:, u % 2, :]
                    sm = m["sm"][:, u % 2, :].rearrange("p (c n) -> p c n", c=2)[:, :, 0:nk]
                    ex = m["ex"][:, u % 2, :].rearrange("p (c n) -> p c n", c=2)[:, :, 0:nk]
                    slope = 2.0 ** -(h + 1.0)
                    for c in range(2):
                        ps = self.ps(banks[c][0])[:, 0:nk]
                        a = self.dve.do(lambda e, c=c, ps=ps: e.scalar_tensor_tensor(
                            out=sm[:, c, :], in0=m["dist"][:, SEQ - nk:SEQ], scalar=-slope / scale, in1=ps,
                            op0=ALU.mult, op1=ALU.add), done, self.tables, self.freed.get(f"sm{u % 2}"),
                            self.claim("sm"))
                        self.bank_free[banks[c][0]] = a
                    a = self.dve.do(lambda e: e.tensor_reduce(st[:, 0:2], sm, AX.X, ALU.max, negate=True), a,
                                    self.freed.get(f"st{u % 2}"))
                    a = self.dve.do(lambda e: e.tensor_scalar(st[:, 2:4], st[:, 0:2], scale, None, ALU.mult), a)
                    for c in range(2):
                        x = self.act.do(lambda e, c=c: e.activation(ex[:, c, :], sm[:, c, :], ACT.Exp,
                                                                    bias=st[:, 2 + c:3 + c], scale=scale,
                                                                    accum_out=st[:, 4 + c:5 + c]), a,
                                        self.freed.get(f"ex{u % 2}"), self.claim("ex"))
                    a = self.dve.do(lambda e: e.reciprocal(st[:, 6:8], st[:, 4:6]), x)
                    a = self.dve.do(lambda e: e.tensor_tensor(st[:, 8:9], st[:, 7:8], m["lam"][:, 5:6], ALU.mult),
                                    a, lam)
                    b = self.dve.do(lambda e: e.tensor_scalar(sm[:, 0, :], ex[:, 0, :], st[:, 6:7], None, ALU.mult), a)
                    b = self.dve.do(lambda e: e.scalar_tensor_tensor(out=sm[:, 0, :], in0=ex[:, 1, :],
                                                                     scalar=st[:, 8:9], in1=sm[:, 0, :],
                                                                     op0=ALU.mult, op1=ALU.add), b)
                    self.freed[f"ex{u % 2}"] = b
                    self.freed[f"st{u % 2}"] = b
                    return sm[:, 0, :], b

                def mix(u, weighed, h=h, t=t):
                    weights, known = weighed
                    values = [v_t[:, k, h * DA_DV:(h + 1) * DA_DV] for k in range(t + 1)]
                    b, out, mixed, turned = self.mix_weights(u, weights, known, t + 1, values, made["v"])
                    self.freed[f"sm{u % 2}"] = turned
                    a = self.act.do(lambda e: e.activation(y[:, t, h * DA_DV:(h + 1) * DA_DV], out, ACT.Copy),
                                    mixed, free)
                    a = self.act.do(lambda e: e.activation(m["junk"][:], out, ACT.Square,
                                                           accum_out=m["unit"][:, t * DA_HEADS + h:
                                                                               t * DA_HEADS + h + 1]), a)
                    self.bank_free[b] = a
                    return a
                yield score, weigh, mix

    def differential_norm(self, y, written):
        m = self.m
        ms = m["unit"][:, 0:NT * DA_HEADS]
        a = self.dve.do(lambda e: e.tensor_scalar(ms, ms, 1.0 / DA_DV, EPS, ALU.mult, ALU.add), written)
        a = self.act.do(lambda e: e.activation(ms, ms, ACT.Sqrt), a)
        r = self.dve.do(lambda e: e.reciprocal(ms, ms), a)
        out = []
        for t in range(NT):
            for h in range(DA_HEADS):
                s = slice(h * DA_DV, (h + 1) * DA_DV)
                out.append(self.dve.do(lambda e, t=t, h=h, s=s: e.scalar_tensor_tensor(
                    out=y[:, t, s], in0=y[:, t, s], scalar=ms[:, t * DA_HEADS + h:t * DA_HEADS + h + 1],
                    in1=m["da_g"][:], op0=ALU.mult, op1=ALU.mult), r, self.da_gain))
        self.freed["sm"] = self.latest()
        self.freed["ex"] = self.freed["sm"]
        return out[-1]

    def retention(self, qk, v_t, y, made, free, filler):
        m = self.m
        decay = m["decay"][:].rearrange("p (h n) -> p h n", h=RET_HEADS)
        written = []
        pairs = ((0, 0), (0, 1), (1, 1))
        for h in range(RET_HEADS):
            b, bank_free = self.bank()
            ps = self.ps(b)

            def score(e, h=h, ps=ps):
                for i, (k, q) in enumerate(pairs):
                    last = e.matmul(ps[:, i * P:i * P + P], qk[:, RET_HEADS + h, k * P:k * P + P],
                                    qk[:, h, q * P:q * P + P], start=True, stop=True)
                return last
            scored = self.pe.do(score, bank_free, made["q"])
            sm = m["sm"][:, h % 2, :]
            last_use = self.freed.get(f"sm{h % 2}")
            a = self.dve.do(lambda e, h=h, ps=ps, sm=sm: e.tensor_tensor(sm[:, 0:2 * P], ps[:, 0:2 * P],
                                                                         decay[:, h, :], ALU.mult),
                            scored, self.tables, last_use, self.claim("sm"))
            a = self.dve.do(lambda e, h=h, ps=ps, sm=sm: e.tensor_tensor(sm[:, 2 * P:3 * P], ps[:, 2 * P:3 * P],
                                                                         decay[:, h, 0:P], ALU.mult), scored)
            self.bank_free[b] = a
            step(filler)
            step(filler)
            o, bank_free = self.bank()
            out = self.ps(o)

            def mix(e, h=h, sm=sm, out=out):
                v = slice(h * RET_DV, (h + 1) * RET_DV)
                e.matmul(out[:, 0:RET_DV], sm[:, 0:P], v_t[:, 0, v], start=True, stop=True)
                e.matmul(out[:, RET_DV:], sm[:, P:2 * P], v_t[:, 0, v], start=True, stop=False)
                return e.matmul(out[:, RET_DV:], sm[:, 2 * P:3 * P], v_t[:, 1, v], start=False, stop=True)
            mixed = self.pe.do(mix, a, bank_free, made["v"])
            self.freed[f"sm{h % 2}"] = mixed
            for t in range(NT):
                s = self.dve.do(lambda e, t=t, out=out: e.bn_stats(m["bn"][:, t, 0, :],
                                                                   out[:, t * RET_DV:(t + 1) * RET_DV]),
                                mixed, written)
                s = self.dve.do(lambda e, t=t, h=h: e.bn_aggr(m["gn"][:, t * RET_HEADS + h, :],
                                                              m["bn"][:, t, 0, :]), s)
            a = self.act.do(lambda e, h=h, out=out: e.activation(
                y[:, :, h * RET_DV:(h + 1) * RET_DV], out[:].rearrange("p (t n) -> p t n", t=NT), ACT.Copy), s, free)
            self.bank_free[o] = a
            written = [s, a]
        return written

    def retention_norm(self, y, written, gate, gate_ready, g, b, rows):
        m = self.m
        n = NT * RET_HEADS
        mean, var = m["gn"][:, :, 0], m["gn"][:, :, 1]
        rstd, nb = m["rstd"][:, 0:n], m["nb"][:, 0:n]
        r = self.inverse_root(var, EPS, rstd, written)
        r = self.dve.do(lambda e: e.scalar_tensor_tensor(out=nb, in0=mean, scalar=-1.0, in1=rstd, op0=ALU.mult,
                                                         op1=ALU.mult), r)
        out = []
        for t in range(NT):
            for h in range(RET_HEADS):
                s, i = slice(h * RET_DV, (h + 1) * RET_DV), t * RET_HEADS + h
                a = self.dve.do(lambda e, t=t, s=s, i=i: e.tensor_scalar(
                    y[:, t, s], y[:, t, s], rstd[:, i:i + 1], nb[:, i:i + 1], ALU.mult, ALU.add), r)
            a = self.dve.do(lambda e, t=t: e.tensor_tensor(y[:, t, :], y[:, t, :], g, ALU.mult), a, rows)
            a = self.dve.do(lambda e, t=t: e.tensor_tensor(y[:, t, :], y[:, t, :], b, ALU.add), a)
            a = self.dve.do(lambda e, t=t: e.tensor_tensor(y[:, t, :], y[:, t, :], gate[:, t, :], ALU.mult), a,
                            gate_ready)
            out.append(a)
        self.freed["rows"] = out
        self.freed["sm"] = self.latest()
        return out

    def feed_forward(self, lhs, n_chunks, up, down, pair, finish, between=None):
        m = self.m
        self.use_ring(range(4, 8))
        acc_free = [self.bank_free.get(b) for b in range(4)]
        hidden = m["b1"][:, 0:2 * NT * F_CHUNK].rearrange("p (s t n) -> p s t n", s=2, t=NT)
        gated = m["b1"][:, 2 * NT * F_CHUNK:].rearrange("p (s t n) -> p s t n", s=2, t=NT)
        hidden_free, turned_free = [self.claim("b1")] * 2, [self.claim("b0")] * 2
        state = {}

        def up_part(i):
            banks = []

            def keep(c, t, ps, done):
                b = [x for x in range(8) if self.ps(x) is ps][0]
                banks.append((b, done))
                return None
            drain(self.gemm_token(lhs, [up(i)], keep))
            slot = i % 2
            out = []
            for t, (b, done) in enumerate(banks):
                ps = self.ps(b)
                a = self.act.do(lambda e, t=t, ps=ps: e.activation(gated[:, slot, t, :], ps[:, F_CHUNK:], ACT.Silu),
                                done, hidden_free[slot])
                h = self.dve.do(pair(i, t, hidden[:, slot, t, :], ps[:, 0:F_CHUNK], gated[:, slot, t, :]), a,
                                self.combined, hidden_free[slot])
                self.bank_free[b] = h
                out.append(h)
            state[i] = out

        def down_part(i):
            slot = i % 2
            b, bank_free = self.bank()
            ps = self.ps(b)

            def turn(e):
                for k in range(2):
                    for t in range(NT):
                        last = e.transpose(ps[:, k * SEQ + t * P:k * SEQ + t * P + P],
                                           hidden[:, slot, t, k * P:k * P + P], m["ident"][:])
                return last
            turned = self.pe.do(turn, state.pop(i), bank_free)
            hidden_free[slot] = turned
            hi, lo = m["ht_hi"][:, slot, :, :], m["ht_lo"][:, slot, :, :]
            a = self.act.do(lambda e: e.activation(hi, ps[:], ACT.Copy), turned, turned_free[slot])
            v = self.dve.do(lambda e: e.tensor_tensor(lo, ps[:], hi.bitcast(F32), ALU.subtract), a,
                            turned_free[slot])
            self.bank_free[b] = v
            n = self.take(down(i))
            wh, wl = [w.rearrange("p (k n) -> p k n", k=2) for w in self.halves(n)]

            def issue(e):
                for t in range(NT):
                    for k in range(2):
                        tok = slice(t * P, t * P + P)
                        for j, (x, w) in enumerate(((hi, wh), (hi, wl), (lo, wh))):
                            for half in range(2):
                                last = e.matmul(self.ps(2 * t + half)[:], x[:, k, tok],
                                                w[:, k, half * BANK:(half + 1) * BANK],
                                                start=(i == 0 and k == 0 and j == 0),
                                                stop=(i == n_chunks - 1 and k == 1 and j == 2))
                return last
            done = self.pe.do(issue, a, v, self.full(n), acc_free if i == 0 else None)
            turned_free[slot] = done
            self.done_with(n, done)
            return done

        up_part(0)
        for i in range(n_chunks):
            if i + 1 < n_chunks:
                up_part(i + 1)
            if between is not None:
                step(between)
                step(between)
                if n_chunks * 2 < 36:
                    step(between)
                    step(between)
            done = down_part(i)
        for t in range(NT):
            for half in range(2):
                self.bank_free[2 * t + half] = finish(t, half, self.ps(2 * t + half), done)
        self.freed["b0"] = self.freed["b1"] = self.latest()
        self.use_ring(range(8))

    def experts(self, x, x_ready):
        d, m = self.dram, self.m
        self.combined = self.router()
        w1, w3, w2 = d["w1"][0], d["w3"][0], d["w2"][0]

        def up(i):
            e, c0 = i // 2, (i % 2) * F_CHUNK
            a = w3[e].rearrange("(k p) n -> p k n", p=P)
            g = w1[e].rearrange("(k p) n -> p k n", p=P)
            return [[(lambda s: whole(BANK)(s)[:, :, 0:F_CHUNK], a[:, q * KH:(q + 1) * KH, c0:c0 + F_CHUNK]),
                     (lambda s: whole(BANK)(s)[:, :, F_CHUNK:], g[:, q * KH:(q + 1) * KH, c0:c0 + F_CHUNK])]
                    for q in range(2)]

        def down(i):
            e, c0 = i // 2, (i % 2) * F_CHUNK
            return [(whole(D), w2[e, c0:c0 + F_CHUNK, :].rearrange("(k p) n -> p k n", p=P))]

        def pair(i, t, out, a, g):
            c = m["combine"][:, t, i // 2:i // 2 + 1]
            return lambda e: e.scalar_tensor_tensor(out=out, in0=a, scalar=c, in1=g, op0=ALU.mult, op1=ALU.mult)
        sums = [[] for _ in range(NT)]

        def finish(t, half, ps, done):
            s = slice(half * BANK, (half + 1) * BANK)
            token = self.dve.do(lambda e: e.scalar_tensor_tensor(out=x[:, t, s], in0=x[:, t, s], scalar=ALPHA_1,
                                                                 in1=ps[:], op0=ALU.mult, op1=ALU.add), done)
            sums[t].append(token)
            return token
        g, b, rows = self.rows("ln2", d["ln2_g"][0], d["ln2_b"][0])
        self.condition()
        mods = iter(()) if self.stop == "first" else self.modulation(0)
        self.feed_forward(self.xt, N_EXPERTS * 2, up, down, pair, finish, mods)
        drain(mods)
        self.release("xt")
        self.x_ready = self.layer_norm(x, sums, g, b, rows)

    def router(self):
        d, m = self.dram, self.m
        nr = N_GROUPS + N_EXPERTS
        raw = m["sm"][:, 0, 0:KD * nr].rearrange("p (k n) -> p k n", k=KD)
        w = [self.load("w_rg", raw[:, :, 0:N_GROUPS], d["w_rg"][0].rearrange("(k p) n -> p k n", p=P),
                       self.claim("sm")),
             self.load("w_re", raw[:, :, N_GROUPS:], d["w_re"][0].rearrange("(k p) n -> p k n", p=P))]
        bias = [self.load("b_rg", m["r_bias"][:, 0:N_GROUPS], d["b_rg"][0].partition_broadcast(P)),
                self.load("b_re", m["r_bias"][:, N_GROUPS:], d["b_re"][0].partition_broadcast(P))]
        a = self.act.do(lambda e: e.activation(m["r_hi"][:], raw, ACT.Copy), w)
        s = self.dve.do(lambda e: e.tensor_tensor(m["r_lo"][:], raw, m["r_hi"][:].bitcast(F32), ALU.subtract), a)
        self.freed["sm"] = s
        hi, lo, ready = self.xt
        b, bank_free = self.bank()
        ps = self.ps(b)

        def issue(e):
            for t in range(NT):
                for k in range(KD):
                    for i, (x, w_) in enumerate(((hi, m["r_hi"]), (hi, m["r_lo"]), (lo, m["r_hi"]))):
                        last = e.matmul(ps[:, t * nr:(t + 1) * nr], x[:, k, t * P:t * P + P], w_[:, k, :],
                                        start=(k == 0 and i == 0), stop=(k == KD - 1 and i == 2))
            return last
        done = self.pe.do(issue, ready, a, s, bank_free)
        out = []
        for t in range(NT):
            out.append(self.route(t, ps[:, t * nr:(t + 1) * nr], done, bias, b))
        return out

    def route(self, t, ps, done, bias, bank):
        m, v = self.m, self.dve.do
        r = m["route"][:, t, :]
        lg = r[:, 0:20]
        groups, experts = r[:, 0:4], r[:, 4:20]
        a = v(lambda e: e.tensor_tensor(lg, ps, m["r_bias"][:], ALU.add), done, bias)
        self.bank_free[bank] = a

        def first_of_largest(values, top, tmp, hot, a):
            a = v(lambda e: e.tensor_reduce(top, values, AX.X, ALU.max), a)
            a = v(lambda e: e.tensor_scalar(tmp, values, top, None, ALU.is_equal), a)
            a = v(lambda e: e.scalar_tensor_tensor(out=tmp, in0=tmp, scalar=-100.0, in1=m["index"][:],
                                                   op0=ALU.mult, op1=ALU.add), a, self.tables)
            a = v(lambda e: e.tensor_reduce(r[:, 50:51], tmp, AX.X, ALU.min), a)
            return v(lambda e: e.tensor_scalar(hot, tmp, r[:, 50:51], None, ALU.is_equal), a)
        tmp, g_hot, sel, hot1, hot2 = r[:, 20:24], r[:, 24:28], r[:, 28:32], r[:, 32:36], r[:, 36:40]
        a = first_of_largest(groups, r[:, 40:41], tmp, g_hot, a)
        a = v(lambda e: e.tensor_scalar(r[:, 41:42], r[:, 40:41], -1.0, None, ALU.mult), a)
        x = self.act.do(lambda e: e.activation(tmp, groups, ACT.Exp, bias=r[:, 41:42], accum_out=r[:, 42:43]), a)
        p_top = v(lambda e: e.reciprocal(r[:, 43:44], r[:, 42:43]), x)
        a = v(lambda e: e.tensor_scalar(sel, experts[:, 0:4], g_hot[:, 0:1], None, ALU.mult), p_top)
        for g in range(1, N_GROUPS):
            a = v(lambda e, g=g: e.scalar_tensor_tensor(out=sel, in0=experts[:, 4 * g:4 * g + 4],
                                                        scalar=g_hot[:, g:g + 1], in1=sel, op0=ALU.mult,
                                                        op1=ALU.add), a)
        a = first_of_largest(sel, r[:, 44:45], tmp, hot1, a)
        a = v(lambda e: e.scalar_tensor_tensor(out=sel, in0=hot1, scalar=-MASKED, in1=sel, op0=ALU.mult,
                                               op1=ALU.add), a)
        a = first_of_largest(sel, r[:, 45:46], tmp, hot2, a)
        a = v(lambda e: e.tensor_tensor(r[:, 46:47], r[:, 45:46], r[:, 44:45], ALU.subtract), a)
        x = self.act.do(lambda e: e.activation(r[:, 47:48], r[:, 46:47], ACT.Exp), a)
        a = v(lambda e: e.tensor_scalar(r[:, 48:49], r[:, 47:48], 1.0, None, ALU.add), x)
        a = v(lambda e: e.reciprocal(r[:, 49:50], r[:, 48:49]), a)
        a = v(lambda e: e.tensor_tensor(r[:, 49:50], r[:, 49:50], r[:, 43:44], ALU.mult), a)
        a = v(lambda e: e.tensor_tensor(r[:, 48:49], r[:, 49:50], r[:, 47:48], ALU.mult), a)
        a = v(lambda e: e.tensor_scalar(hot1, hot1, r[:, 49:50], None, ALU.mult), a)
        a = v(lambda e: e.scalar_tensor_tensor(out=hot1, in0=hot2, scalar=r[:, 48:49], in1=hot1, op0=ALU.mult,
                                               op1=ALU.add), a)
        for g in range(N_GROUPS):
            last = v(lambda e, g=g: e.tensor_scalar(m["combine"][:, t, 4 * g:4 * g + 4], hot1, g_hot[:, g:g + 1],
                                                    None, ALU.mult), a)
        return last

    def condition(self):
        d, m = self.dram, self.m
        rows = m["junk"][0:2 * KD, :]
        free = self.latest()
        got = [self.load("c", rows[0:KD, :], d["c_2"][0].rearrange("(k p) -> k p", p=P), free),
               self.load("c_ctx", rows[KD:2 * KD, :], d["c_ctx_2"].rearrange("(k p) -> k p", p=P))]
        b, bank_free = self.bank()
        ps = self.ps(b)
        done = self.pe.do(lambda e: e.transpose(ps[:, 0:2 * KD], rows, m["ident"][0:2 * KD, 0:2 * KD]), got,
                          bank_free, self.const)
        self.c_ready = self.act.do(lambda e: e.activation(m["cvec"][:].rearrange("p v k -> p (v k)"),
                                                          ps[:, 0:2 * KD], ACT.Silu), done)
        self.bank_free[b] = self.c_ready

    def modulation(self, layer):
        d, m = self.dram, self.m
        w = d["mod_w_2"][layer].rearrange("(k p) n -> p k n", p=P)
        acc = m["b2"][:].rearrange("p (s v n) -> p s v n", s=2, v=2)
        acc_free = [self.claim("b2")] * 2
        bias_free = [self.freed.get("row_c")] * 2
        mg, b4 = self.tok("mg"), self.tok("b4")
        gate_rows = {0: [[mg[:, 0, :], mg[:, 1, :]], [b4[:, 0, :]], [b4[:, 1, :]]],
                     1: [[mg[:, 0, :]], [mg[:, 1, :]], [b4[:, 0, :]]]}[layer]
        gate_free = self.claim("mg", "b4")
        ready = []
        self.mod_ready = self.mod_ready or {}
        self.mod_ready[layer] = ready

        def start(c):
            vectors = 2 if layer == 0 and c // 2 < 5 else 1
            slot = c % 2
            bias = m["row_c"][0:1, slot * BANK:(slot + 1) * BANK]
            b = self.load(f"mod_b{layer}_{c}", bias, d["mod_b_2"][layer:layer + 1, c * BANK:(c + 1) * BANK],
                          bias_free[slot])
            for part in range(2):
                n = self.take([(whole(BANK), w[:, part * KH:(part + 1) * KH, c * BANK:(c + 1) * BANK])], split=False)
                raw = m["raw"][:, n % RAW_SLOTS, :].rearrange("p (k n) -> p k n", k=KH)
                for v in range(vectors):
                    out = acc[:, slot, v, :]
                    a = None
                    for k in range(KH):
                        kk = part * KH + k
                        col = m["cvec"][:, v, kk:kk + 1]
                        after = [self.raw_full.get(n), self.c_ready, acc_free[slot] if kk == 0 else None, a]
                        if kk == 0:
                            a = self.dve.do(lambda e, out=out, raw=raw, k=k, col=col: e.tensor_scalar(
                                out, raw[:, k, :], col, None, ALU.mult), after)
                        else:
                            a = self.dve.do(lambda e, out=out, raw=raw, k=k, col=col: e.scalar_tensor_tensor(
                                out=out, in0=raw[:, k, :], scalar=col, in1=out, op0=ALU.mult, op1=ALU.add), after)
                self.raw_free[n] = a
                yield
            self.started = (c, vectors, slot, bias, b, a)

        def finish(c, vectors, slot, bias, b, a):
            j, half = c // 2, c % 2
            for v in range(vectors):
                if j % 3 == 2:
                    if v >= len(gate_rows[j // 3]):
                        continue
                    bank, free = self.bank()
                    ps = self.ps(bank)

                    def issue(e, v=v, ps=ps):
                        e.matmul(ps[:], m["ones"][:], acc[:, slot, v, :], start=True, stop=False)
                        return e.matmul(ps[:], m["ones"][0:1, :], bias, start=False, stop=True)
                    done = self.pe.do(issue, a, b, free, self.ones)
                    row = gate_rows[j // 3][v][:, half * BANK:(half + 1) * BANK]
                    half_of = 1.0 if j // 3 == 1 else 0.5
                    token = self.act.do(lambda e, ps=ps, row=row: e.activation(row, ps[:], ACT.Copy, scale=half_of),
                                        done, gate_free)
                else:
                    bank, free = self.bank()
                    ps = self.ps(bank)

                    def issue(e, v=v, ps=ps):
                        for i in range(4):
                            cols = slice(i * P, i * P + P)
                            e.matmul(ps[:, i:i + 1], acc[:, slot, v, cols], m["ones"][:, 0:1], start=True, stop=False)
                            last = e.matmul(ps[:, i:i + 1], bias[:, cols], m["ones"][0:1, 0:1], start=False,
                                            stop=True)
                        return last
                    done = self.pe.do(issue, a, b, free, self.ones)
                    f = j * KD + half * 4
                    out = m["mod"][:, 2 * layer + v, f:f + 4]
                    token = self.dve.do(lambda e, out=out, ps=ps: e.tensor_scalar(
                        out, ps[:, 0:4], 1.0 if j % 3 == 1 else 0.0, None, ALU.add), done)
                self.bank_free[bank] = token
                ready.append(token)
                acc_free[slot] = done
                bias_free[slot] = done

        started = None
        for c in range(2 * N_MOD):
            yield from start(c)
            if started is not None:
                finish(*started)
            started = self.started
        finish(*started)
        self.release("b2", "row_c")

    def affine(self, which, layer, j):
        cols = self.m["mod"][:, 2 * layer + which, :]
        return cols[:, (3 * j + 1) * KD:(3 * j + 2) * KD], cols[:, 3 * j * KD:(3 * j + 1) * KD], self.mod_ready[layer]

    def gated_residual(self, x, gate, sums, known):
        m = self.m

        def finish(t, half, ps, done):
            s = slice(half * BANK, (half + 1) * BANK)
            tmp = m["sm"][:, t, :]
            a = self.dve.do(lambda e: e.tensor_tensor(tmp, ps[:], gate[:, s], ALU.mult), done, known,
                            self.freed.get("sm"), self.freed.get(f"sm{t}"))
            sums[t].append(self.dve.do(lambda e: e.scalar_tensor_tensor(out=x[:, t, s], in0=x[:, t, s],
                                                                        scalar=ALPHA_2, in1=tmp, op0=ALU.mult,
                                                                        op1=ALU.add), a))
            self.freed[f"sm{t}"] = sums[t][-1]
            return a
        return finish

    def conditioned_ffn(self, x, ready, which, layer, j, gate, between=None):
        d, m = self.dram, self.m
        f = j // 2
        lhs = self.to_lhs(x, ready, (m["xt_hi"], m["xt_lo"]), self.claim("xt"), self.affine(which, layer, j))
        g, b, rows = self.rows(f"ln_{layer}{which}{j}", d["ln_g_2"][layer, j], d["ln_b_2"][layer, j])
        wi = d["ffn_wi_2"][layer, f].rearrange("(k p) n -> p k n", p=P)
        wo = d["ffn_wo_2"][layer, f]

        def up(i):
            c0 = i * F_CHUNK
            return [[(lambda s: whole(BANK)(s)[:, :, 0:F_CHUNK], wi[:, q * KH:(q + 1) * KH, c0:c0 + F_CHUNK]),
                     (lambda s: whole(BANK)(s)[:, :, F_CHUNK:],
                      wi[:, q * KH:(q + 1) * KH, D_FF + c0:D_FF + c0 + F_CHUNK])] for q in range(2)]

        def down(i):
            return [(whole(D), wo[i * F_CHUNK:(i + 1) * F_CHUNK, :].rearrange("(k p) n -> p k n", p=P))]

        def pair(i, t, out, a, g_):
            return lambda e: e.tensor_tensor(out, a, g_, ALU.mult)
        sums = [[] for _ in range(NT)]
        self.combined = None
        self.feed_forward(lhs, D_FF // F_CHUNK, up, down, pair,
                          self.gated_residual(x, gate, sums, self.mod_ready[layer]), between)
        self.release("xt")
        return self.layer_norm(x, sums, g, b, rows)

    def rotate(self, x, heads, t, table, tmp, ready):
        m = self.m
        v = x.rearrange("p (h a s f) -> p h a s f", a=2, s=2, f=AXIS_DIM // 2)
        x1, x2 = v[:, :, :, 0, :], v[:, :, :, 1, :]
        shape = [P, heads, 2, AXIS_DIM // 2]
        cos, sin = [m["rope"][:, t, table + i, :].rearrange("p (a f) -> p a f", a=2).unsqueeze(1).to_broadcast(shape)
                    for i in range(2)]
        half = heads * HEAD_DIM // 2
        t1, t2 = [tmp[:, i * half:(i + 1) * half].rearrange("p (h a f) -> p h a f", h=heads, a=2) for i in range(2)]
        v_ = self.dve.do
        a = v_(lambda e: e.tensor_tensor(t1, x1, sin, ALU.mult), ready, self.tables, self.freed.get("rotated"))
        b = v_(lambda e: e.tensor_tensor(t2, x2, sin, ALU.mult), a)
        c = v_(lambda e: e.tensor_tensor(x1, x1, cos, ALU.mult), b)
        e_ = v_(lambda e: e.tensor_tensor(x2, x2, cos, ALU.mult), c)
        f = v_(lambda e: e.tensor_tensor(x1, x1, t2, ALU.subtract), e_)
        self.freed["rotated"] = v_(lambda e: e.tensor_tensor(x2, x2, t1, ALU.add), f)
        return self.freed["rotated"]

    def keys_values(self, lhs, kv, twice, k_f, free, rotated):
        d, m = self.dram, self.m
        made = {}

        def evacuate(c, t, ps, done):
            made[t] = self.dve.do(lambda e: e.tensor_tensor(kv[:, t, :], ps[:], m["row_b"][:, 0:BANK], ALU.add),
                                  done, free, self.qkv_bias)
            return made[t]
        drain(self.gemm_token(lhs, columns(d["attn_wqkv_2"][0], N_HEADS * HEAD_DIM, 2 * N_KV * HEAD_DIM), evacuate))
        out = []
        n = N_KV * HEAD_DIM
        copied = []
        for t in range(NT):
            a = made[t]
            if rotated:
                a = self.rotate(kv[:, t, 0:n], N_KV, t, 0, m["b2"][:, 2 * BANK:], a)
            src = kv[:, t, 0:n].rearrange("p (g n) -> p g n", g=N_KV)
            dst = twice[:, t * 2 * n:(t + 1) * 2 * n].rearrange("p (g c n) -> p g c n", g=N_KV, c=2)
            for c in range(2):
                copied.append(self.dve.do(lambda e, c=c, src=src, dst=dst: e.tensor_copy(dst[:, :, c, :], src), a,
                                          free))
        for g in range(0, N_KV, 2):
            b, bank_free = self.bank()
            ps = self.ps(b)

            def turn(e, g=g, ps=ps):
                for i in range(2):
                    for t in range(NT):
                        cols = t * 2 * n + (g + i) * P
                        last = e.transpose(ps[:, i * SEQ + t * P:i * SEQ + t * P + P], twice[:, cols:cols + P],
                                           m["ident"][:])
                return last
            turned = self.pe.do(turn, copied, bank_free)
            a = self.act.do(lambda e, g=g, ps=ps: e.activation(k_f[:, g:g + 2, :], ps[:], ACT.Copy), turned, free)
            self.bank_free[b] = a
            out.append(a)
        return [out, copied]

    def window_units(self, q_f, k_f, v_t, kc_f, vc_t, y, ready):
        m = self.m
        n = N_KV * HEAD_DIM
        for h in range(N_HEADS):
            for t in range(NT):
                g = h // GROUP

                def score(u, h=h, t=t, g=g):
                    b, free = self.bank()
                    ps = self.ps(b)
                    rows = slice((h % 2) * HEAD_DIM, (h % 2 + 1) * HEAD_DIM)

                    def issue(e):
                        q = q_f[rows, h // 2, t * P:t * P + P]
                        e.matmul(ps[:, 0:SEQ], q, k_f[rows, g, :], start=True, stop=True)
                        return e.matmul(ps[:, SEQ:], q, kc_f[rows, g, :], start=True, stop=True)
                    return b, self.pe.do(issue, free, ready)

                def weigh(u, scored, h=h, t=t):
                    b, done = scored
                    ps = self.ps(b)
                    st = m["st"][:, u % 2, :]
                    ex = m["ex"][:, u % 2, :]
                    other = slice(P, 2 * P) if t == 0 else slice(0, P)
                    a = self.dve.do(lambda e: e.tensor_tensor(ps[:, other], ps[:, other], m["window"][:, t, :],
                                                              ALU.add), done, self.tables)
                    a = self.dve.do(lambda e: e.tensor_reduce(st[:, 0:1], ps[:], AX.X, ALU.max, negate=True), a,
                                    self.freed.get(f"st{u % 2}"))
                    a = self.dve.do(lambda e: e.tensor_scalar(st[:, 1:2], st[:, 0:1], m["sinks"][:, 1, h:h + 1],
                                                              None, ALU.min), a, self.sinks)
                    x = self.act.do(lambda e: e.activation(ex, ps[:], ACT.Exp, bias=st[:, 1:2],
                                                           accum_out=st[:, 2:3]), a, self.freed.get(f"ex{u % 2}"),
                                    self.claim("ex"))
                    self.bank_free[b] = x
                    s = self.act.do(lambda e: e.activation(st[:, 3:4], m["sinks"][:, 0, h:h + 1], ACT.Exp,
                                                           bias=st[:, 1:2]), a)
                    r = self.dve.do(lambda e: e.tensor_tensor(st[:, 4:5], st[:, 2:3], st[:, 3:4], ALU.add), s)
                    r = self.dve.do(lambda e: e.reciprocal(st[:, 5:6], st[:, 4:5]), r)
                    return ex, x, r, st

                def mix(u, weighed, h=h, t=t, g=g):
                    ex, known, r, st = weighed
                    cols = slice(n + g * HEAD_DIM, n + (g + 1) * HEAD_DIM)
                    values = [v_t[:, k, cols] for k in range(NT)] + [vc_t[:, k, cols] for k in range(NT)]
                    b, out, mixed, turned = self.mix_weights(u, ex, known, 4, values, ready)
                    self.freed[f"ex{u % 2}"] = turned
                    a = self.act.do(lambda e: e.activation(y[:, t, h * HEAD_DIM:(h + 1) * HEAD_DIM], out, ACT.Copy,
                                                           scale=st[:, 5:6]), mixed, r, self.claim("b0"))
                    self.bank_free[b] = a
                    self.freed[f"st{u % 2}"] = a
                    return a
                yield score, weigh, mix

    def second_block(self):
        d, m = self.dram, self.m
        x = self.tok("x")
        mg, b4 = self.tok("mg"), self.tok("b4")

        ctx = self.tok("b3")
        got = self.load("ctx", ctx, d["ctx_2"][0].rearrange("(t p) n -> p t n", p=P), self.claim("b3"))
        c_ready = self.conditioned_ffn(ctx, got, 1, 0, 0, mg[:, 1, :])
        lhs = self.to_lhs(ctx, c_ready, (m["xt_hi"], m["xt_lo"]), self.claim("xt"), self.affine(1, 0, 1))
        self.release("b3")
        qkv = d["attn_bqkv_2"][0]
        q_width = N_HEADS * HEAD_DIM
        free = self.freed.get("rows")
        self.qkv_bias = [self.load("bias_kv", m["row_b"][:, 0:BANK], qkv[q_width:].partition_broadcast(P), free)]
        self.sinks = self.load("sink", m["sinks"][:, 0, :], d["attn_sink_2"][0].partition_broadcast(P))
        self.sinks = self.dve.do(lambda e: e.tensor_scalar(m["sinks"][:, 1, :], m["sinks"][:, 0, :], -1.0, None,
                                                           ALU.mult), self.sinks)
        vc_t = m["b3"][:, 0:2 * BANK].rearrange("p (t n) -> p t n", t=NT)
        kc_f = m["b3"][:, 2 * BANK:].rearrange("p (g s) -> p g s", g=N_KV)
        context = self.keys_values(lhs, vc_t, m["b2"][:, 0:2 * BANK], kc_f, self.claim("b2", "b3"), False)
        self.freed["rows"] = self.latest()
        self.release("xt", "b2")
        if self.stop == "ctx":
            self.x_ready = self.x_ready
            return

        x_ready = self.conditioned_ffn(x, self.x_ready, 0, 0, 0, mg[:, 0, :])
        if self.stop == "b2ffn":
            self.x_ready = x_ready
            return

        lhs = self.to_lhs(x, x_ready, (m["xt_hi"], m["xt_lo"]), self.claim("xt"), self.affine(0, 0, 1))
        self.release("mg")
        free = self.freed.get("rows")
        self.qkv_bias = [self.load("bias_kv2", m["row_b"][:, 0:BANK], qkv[q_width:].partition_broadcast(P), free),
                         self.load("bias_q", m["row_g"][:], qkv[0:q_width].partition_broadcast(P), free)]
        v_t = m["b1"][:, 0:2 * BANK].rearrange("p (t n) -> p t n", t=NT)
        k_f = m["b1"][:, 2 * BANK:].rearrange("p (g s) -> p g s", g=N_KV)
        latent = self.keys_values(lhs, v_t, m["b2"][:, 0:2 * BANK], k_f, self.claim("b1", "b2"), True)
        q_t, q_made = self.tok("b0"), [[] for _ in range(NT)]

        def evacuate(c, t, ps, done):
            s = slice(c * BANK, (c + 1) * BANK)
            token = self.dve.do(lambda e: e.tensor_tensor(q_t[:, t, s], ps[:], m["row_g"][:, s], ALU.add), done,
                                self.claim("b0"), self.qkv_bias)
            q_made[t].append(token)
            return token
        drain(self.gemm_token(lhs, columns(d["attn_wqkv_2"][0], 0, q_width), evacuate))
        self.freed["rows"] = self.latest()
        self.release("xt")
        rotated = [self.rotate(q_t[:, t, :], N_HEADS, t, 2, m["b2"][:, 2 * BANK:], q_made[t]) for t in range(NT)]
        q_f, turned_q = self.feat("mg"), []
        for j in range(KD // 2):
            b, free = self.bank()
            ps = self.ps(b)

            def turn(e, j=j, ps=ps):
                for k in range(2):
                    for t in range(NT):
                        last = e.transpose(ps[:, k * SEQ + t * P:k * SEQ + t * P + P],
                                           q_t[:, t, (2 * j + k) * P:(2 * j + k + 1) * P], m["ident"][:])
                return last
            done = self.pe.do(turn, rotated, free)
            a = self.act.do(lambda e, j=j, ps=ps: e.activation(q_f[:, 2 * j:2 * j + 2, :], ps[:], ACT.Copy), done,
                            self.claim("mg"))
            self.bank_free[b] = a
            turned_q.append(a)
        self.release("b0", "b2")
        y = self.tok("b0")
        written = self.softmax_heads(self.window_units(q_f, k_f, v_t, kc_f, vc_t, y, [latent, context, turned_q]),
                                     None)
        self.freed["ex"] = self.latest()
        self.release("mg", "b1", "b3")
        lhs = self.to_lhs(y, written, (m["xt_hi"], m["xt_lo"]), self.claim("xt"))
        self.release("b0")
        x_ready = self.mixer_out(x, lhs, d["attn_wo_2"][0], b4[:, 0, :], 0)
        if self.stop == "attn":
            self.x_ready = x_ready
            return

        mods = self.modulation(1)
        x_ready = self.conditioned_ffn(x, x_ready, 0, 0, 2, b4[:, 1, :], mods)
        drain(mods)
        if self.stop == "layer0":
            self.x_ready = x_ready
            return

        x_ready = self.conditioned_ffn(x, x_ready, 0, 1, 0, mg[:, 0, :])
        x_ready = self.fourier(x, x_ready, mg[:, 1, :])
        self.x_ready = self.conditioned_ffn(x, x_ready, 0, 1, 2, b4[:, 0, :])

    def mixer_out(self, x, lhs, w, gate, layer):
        d = self.dram
        g, b, rows = self.rows(f"mix{layer}", d["ln_g_2"][layer, 1], d["ln_b_2"][layer, 1])
        sums = [[] for _ in range(NT)]
        finish = self.gated_residual(x, gate, sums, self.mod_ready[layer])
        drain(self.gemm_token(lhs, columns(w, 0, D), lambda c, t, ps, done: finish(t, c, ps, done)))
        self.release("xt")
        return self.layer_norm(x, sums, g, b, rows)

    def fourier(self, x, ready, gate):
        d, m = self.dram, self.m
        hi, lo, made = self.to_lhs(x, ready, (m["xt_hi"], m["xt_lo"]), self.claim("xt"), self.affine(0, 1, 1))
        n = self.take([(lambda s: s[:, 0:2 * BANK].rearrange("p (k n) -> p k n", k=2),
                        d["dft"].rearrange("(k p) n -> p k n", p=P))], size=2 * BANK)
        wh, wl = [w[:, 0:2 * BANK].rearrange("p (k n) -> p k n", k=2) for w in self.halves(n)]
        split = []
        free = self.claim("b0", "b1", "b2", "b3")
        for g in range(4):
            for t in range(NT):
                b, bank_free = self.bank()
                ps = self.ps(b)

                def issue(e, g=g, t=t, ps=ps):
                    for k in range(2):
                        for i, (a, w) in enumerate(((hi, wh), (hi, wl), (lo, wh))):
                            last = e.matmul(ps[:], a[:, 2 * g + k, t * P:t * P + P], w[:, k, :],
                                            start=(k == 0 and i == 0), stop=(k == 1 and i == 2))
                    return last
                done = self.pe.do(issue, made, self.full(n), bank_free)
                ph, pl = m["pq_hi"][:, t, g, :], m["pq_lo"][:, t, g, :]
                a = self.act.do(lambda e, ph=ph, ps=ps: e.activation(ph[:, 0:SEQ], ps[:, 0:SEQ], ACT.Copy), done,
                                free)
                a = self.act.do(lambda e, ph=ph, ps=ps: e.activation(ph[:, SEQ:], ps[:, SEQ:], ACT.Copy, scale=-1.0),
                                done)
                v = self.dve.do(lambda e, ph=ph, pl=pl, ps=ps: e.tensor_tensor(
                    pl[:, 0:SEQ], ps[:, 0:SEQ], ph[:, 0:SEQ].bitcast(F32), ALU.subtract), a, free)
                v = self.dve.do(lambda e, ph=ph, pl=pl, ps=ps: e.scalar_tensor_tensor(
                    out=pl[:, SEQ:], in0=ps[:, SEQ:], scalar=-1.0, in1=ph[:, SEQ:].bitcast(F32), op0=ALU.mult,
                    op1=ALU.subtract), a)
                self.bank_free[b] = v
                split.append([a, v])
        first_done = done
        out = []
        for f in range(0, KD, 2):
            b, bank_free = self.bank()
            ps = self.ps(b)

            def issue(e, f=f, ps=ps):
                for i in range(2):
                    g, c0 = (f + i) // 2, ((f + i) % 2) * P
                    terms = [(part, k) for part in range(2) for k in range(NT)]
                    for n_, (part, k) in enumerate(terms):
                        cols = slice(part * SEQ + c0, part * SEQ + c0 + P)
                        w = slice(part * SEQ, (part + 1) * SEQ)
                        ph, pl = m["pq_hi"][:, k, g, cols], m["pq_lo"][:, k, g, cols]
                        for j, (a, c) in enumerate(((ph, wh), (ph, wl), (pl, wh))):
                            last = e.matmul(ps[:, i * SEQ:(i + 1) * SEQ], a, c[:, k, w],
                                            start=(n_ == 0 and j == 0), stop=(n_ == len(terms) - 1 and j == 2))
                return last
            done = self.pe.do(issue, split, bank_free)
            scale = 1.0 / SEQ
            h, l = hi[:, f:f + 2, :], lo[:, f:f + 2, :]
            a = self.act.do(lambda e, h=h, ps=ps: e.activation(h, ps[:], ACT.Copy, scale=scale), done, first_done)
            v = self.dve.do(lambda e, h=h, l=l, ps=ps: e.scalar_tensor_tensor(
                out=l, in0=ps[:], scalar=scale, in1=h.bitcast(F32), op0=ALU.mult, op1=ALU.subtract), a, first_done)
            self.bank_free[b] = v
            out += [a, v]
        self.done_with(n, done)
        self.release("b0", "b1", "b2", "b3")
        return self.mixer_out(x, (hi, lo, out), d["fourier_wo_2"][0], gate, 1)

    def end(self):
        x = self.tok("x")
        self.stores = [self.load("out", self.dram["out"][0].rearrange("(t p) n -> p t n", p=P), x, self.x_ready,
                                 queue=self.sync)]
        self.sync.wait(self.stores)

    def build(self):
        self.combined = self.mod_ready = None
        self.begin()
        self.first_block()
        if self.stop == "mem":
            self.copy_out("mg", self.merged)
        elif self.stop == "ln1":
            self.x_ready = self.xt[2]
            self.end()
        else:
            if self.stop != "first":
                self.second_block()
            self.end()

    def copy_out(self, name, ready):
        self.stores = [self.load("out", self.dram["out"][0].rearrange("(t p) n -> p t n", p=P), self.tok(name), ready,
                                 queue=self.sync)]
        self.sync.wait(self.stores)


def build_program(nc, dram, stop=None):
    with ExitStack() as ctx:
        m = {}

        def sb(name, shape, dt=F32, to=None):
            m[name] = (to or ctx).enter_context(nc.sbuf_tensor(name, shape, dt))
        sb("raw", [P, RAW_SLOTS, PIECE])
        sb("hi", [P, SPLIT_SLOTS, PIECE], F32R)
        sb("lo", [P, SPLIT_SLOTS, PIECE], F32R)
        sb("x", [P, NT * D])
        sb("xt_hi", [P, KD, SEQ], F32R)
        sb("xt_lo", [P, KD, SEQ], F32R)
        sb("mg", [P, NT * D])
        for n in ("row_g", "row_b", "row_c"):
            sb(n, [P, D])
        for n in ("sm", "ex", "at"):
            sb(n, [P, 2, BANK])
        sb("ident", [P, P])
        sb("ones", [P, P])
        sb("dist", [P, SEQ])
        sb("decay", [P, RET_HEADS * 2 * P])
        sb("window", [P, 2, P])
        sb("rope", [P, NT, 4, AXIS_DIM])
        sb("index", [P, N_GROUPS])
        sb("st", [P, 2, 16])
        sb("unit", [P, 16])
        sb("junk", [P, P])
        sb("lam", [P, 8])
        sb("da_g", [P, P])
        sb("bn", [P, NT, 2, 6])
        sb("mv", [P, NT, 2])
        sb("gn", [P, NT * RET_HEADS, 2])
        sb("rstd", [P, 8])
        sb("nb", [P, 8])
        sb("r_hi", [P, KD, 20], F32R)
        sb("r_lo", [P, KD, 20], F32R)
        sb("r_bias", [P, 20])
        sb("route", [P, NT, 52])
        sb("combine", [P, NT, N_EXPERTS])
        sb("cvec", [P, 2, KD])
        sb("mod", [P, 3, N_MOD * KD])
        sb("sinks", [P, 2, N_HEADS])
        with ExitStack() as plain:
            for n in ("b0", "b1", "b2", "b3", "b4"):
                sb(n, [P, NT * D], to=plain)
        with ExitStack() as halves:
            sb("yt_hi", [P, KD, SEQ], F32R, to=halves)
            sb("yt_lo", [P, KD, SEQ], F32R, to=halves)
        with ExitStack() as halves:
            sb("ht_hi", [P, 2, 2, SEQ], F32R, to=halves)
            sb("ht_lo", [P, 2, 2, SEQ], F32R, to=halves)
        with ExitStack() as halves:
            sb("pq_hi", [P, NT, 4, BANK], F32R, to=halves)
            sb("pq_lo", [P, NT, 4, BANK], F32R, to=halves)
        m["psum"] = [ctx.enter_context(nc.psum_tensor(f"bank{i}", [P, BANK], F32)) for i in range(8)]
        first = Blocks(dram, m, None, stop)
        first.build()
        program = Blocks(dram, m, first.taken, stop)
        program.build()
        sems = {n: ctx.enter_context(nc.semaphore(n)) for n in sorted(program.sems)}
        block = ctx.enter_context(nc.Block())

        @block.sync
        def _(e):
            program.sync.run(e, sems)

        @block.gpsimd
        def _(e):
            program.pool.run(e, sems)

        @block.scalar
        def _(e):
            program.act.run(e, sems)

        @block.vector
        def _(e):
            program.dve.run(e, sems)

        @block.tensor
        def _(e):
            program.pe.run(e, sems)


def kernel(**inputs):
    import concourse.bacc as bacc
    from concourse.bass_utils import run_bass_kernel_spmd
    arrays = {n: np.ascontiguousarray(a) for n, a in inputs.items()}
    arrays.update(constants())
    nc = bacc.Bacc("TRN2", target_bir_lowering=False, num_devices=1)
    dram = {n: nc.dram_tensor(f"in_{n}", a.shape, F32, kind="ExternalInput").ap() for n, a in arrays.items()}
    dram["out"] = nc.dram_tensor("out", (1, SEQ, D), F32, kind="ExternalOutput").ap()
    build_program(nc, dram)
    r = run_bass_kernel_spmd(nc, [{f"in_{n}": a for n, a in arrays.items()}], core_ids=[0])
    return r.results[0]["out"]
```

```python
from contextlib import ExitStack

import numpy as np

import concourse.bass as bass
from concourse import mybir

F32 = mybir.dt.float32
F32R = mybir.dt.float32r
ALU = mybir.AluOpType
ACT = mybir.ActivationFunctionType
AX = mybir.AxisListType

P = 128
BANK = 512
PIECE = 2048
RAW_SLOTS = 4
SPLIT_SLOTS = 4
SEQ = 256
NT = SEQ // P
D = 1024
KD = D // P
KH = KD // 2
EPS = 1e-5
MASKED = 1e30

DA_HEADS, DA_DK, DA_DV = 8, 64, 128
RET_HEADS, RET_DK, RET_DV = 4, 128, 256
MEM_HEADS, MEM_DH = 4, 256
N_GROUPS, PER_GROUP, N_EXPERTS = 4, 4, 16
D_FF_EXPERT = 512
LAMBDA_INIT = 0.2
ALPHA_1 = 2.0 ** 0.25
ALPHA_2 = 4.0 ** 0.25
N_HEADS, N_KV, HEAD_DIM, GROUP = 16, 4, 64, 4
WINDOW = 128
D_FF = 2816
F_CHUNK = 256
GRID_W, ROPE_BASE, AXIS_DIM = 64, 10000.0, 32
N_MOD = 9


def constants():
    q = np.arange(P, dtype=np.float64)[:, None]
    dist = (P + q) - np.arange(SEQ)[None, :]
    dist = np.where(dist >= 0, dist, MASKED)
    log_g = np.log(1.0 - 2.0 ** (-5.0 - np.arange(RET_HEADS)))
    k = np.arange(P)[:, None]
    qq = np.arange(P)[None, :]
    decay = []
    for h in range(RET_HEADS):
        diagonal = np.where(qq >= k, np.exp((qq - k) * log_g[h]), 0.0)
        behind = np.exp((P + qq - k) * log_g[h])
        decay.append(np.stack([diagonal, behind], axis=1))
    decay = np.stack(decay, axis=1) * RET_DK ** -0.5
    key = np.arange(P)[None, :]
    window = np.stack([np.where(key <= q, 0.0, -MASKED), np.where(key >= q, 0.0, -MASKED)], axis=1)
    tok = np.arange(SEQ)
    inv = ROPE_BASE ** (-np.arange(0, AXIS_DIM, 2) / AXIS_DIM)
    inv = inv.astype(np.float32)
    ang = np.concatenate([(tok // GRID_W)[:, None].astype(np.float32) * inv,
                          (tok % GRID_W)[:, None].astype(np.float32) * inv], axis=-1)
    cos, sin = np.cos(ang), np.sin(ang)
    rope = np.stack([cos, sin, cos * HEAD_DIM ** -0.5, sin * HEAD_DIM ** -0.5], axis=1)
    turn = 2.0 * np.pi * ((tok[:, None] * tok[None, :]) % SEQ) / SEQ
    dft = np.concatenate([np.cos(turn), np.sin(turn)], axis=1)
    out = {"dist": dist, "decay": decay, "window": window, "rope": rope, "dft": dft,
           "ident": np.eye(P), "index": np.tile(np.arange(N_GROUPS), (P, 1))}
    return {n: np.ascontiguousarray(a, dtype=np.float32) for n, a in out.items()}


class Queue:

    def __init__(self, name):
        self.name, self.count, self.steps, self.seen = name, 0, [], {}

    def wait(self, *after):
        last = {}
        for sem, value in flat(after):
            last[sem] = max(last.get(sem, 0), value)
        for sem, value in last.items():
            if self.seen.get(sem, 0) < value:
                self.seen[sem] = value
                self.steps.append(("wait", sem, value))

    def do(self, issue, *after):
        self.wait(*after)
        self.count += 1
        self.steps.append(("do", issue, self.name))
        return (self.name, self.count)

    def run(self, engine, sems):
        for kind, a, b in self.steps:
            if kind == "wait":
                engine.wait_ge(sems[a], b)
            elif kind == "do":
                a(engine).then_inc(sems[b], 1)
            else:
                a(engine).then_inc(sems[b], 16)


def flat(tokens):
    for t in tokens:
        if t is None:
            continue
        if isinstance(t, list):
            yield from flat(t)
        else:
            yield t


class Banks(dict):

    def __setitem__(self, bank, token):
        if token is not None:
            super().__setitem__(bank, token)
            self.held.discard(bank)


class Program:
    def __init__(self, dram, mem, plan):
        self.dram, self.m, self.plan = dram, mem, plan
        self.pe, self.act, self.dve = Queue("pe"), Queue("act"), Queue("dve")
        self.sync, self.pool = Queue("sync"), Queue("pool")
        self.sems = {"pe", "act", "dve"}
        self.taken, self.loaded, self.split = [], 0, 0
        self.raw_full, self.raw_free = {}, {}
        self.half_full, self.half_free = {}, {}
        self.raw_count = [0] * RAW_SLOTS
        self.is_split = [p[1] for p in plan or []]
        self.mod_count = [0, 0]
        self.split_slot = list(np.cumsum([0] + self.is_split)[:-1])
        self.bank_free, self.held = Banks(), set()
        self.bank_free.held = self.held
        self.ring, self.ring_at = list(range(8)), 0
        self.freed = {}
        self.stores = []

    def load(self, name, dst, src, *after, queue=None):
        q = queue or self.pool
        q.wait(*after)
        sem = f"ld_{name}"
        assert sem not in self.sems
        self.sems.add(sem)
        q.steps.append(("dma", lambda e: e.dma_start(dst, src), sem))
        return (sem, 16)

    def take(self, sources, split=True, size=PIECE):
        n = len(self.taken)
        self.taken.append((sources, split, size))
        if self.plan is None:
            return n
        self.run_ahead()
        return n

    def run_ahead(self):
        plan = self.plan
        while True:
            moved = False
            n = self.loaded
            if n < len(plan) and (n < RAW_SLOTS or (n - RAW_SLOTS) in self.raw_free):
                slot = n % RAW_SLOTS
                if n >= RAW_SLOTS:
                    self.sync.wait(self.raw_free[n - RAW_SLOTS])
                sem = f"raw{slot}"
                self.sems.add(sem)
                for view, src in plan[n][0]:
                    dst = view(self.m["raw"][:, slot, :])
                    self.sync.steps.append(("dma", lambda e, dst=dst, src=src: e.dma_start(dst, src), sem))
                    self.raw_count[slot] += 16
                self.raw_full[n] = (sem, self.raw_count[slot])
                self.loaded += 1
                moved = True
            n = self.split
            if n < self.loaded:
                if not self.is_split[n]:
                    self.split += 1
                    moved = True
                else:
                    s = self.split_slot[n]
                    if s < SPLIT_SLOTS or (s - SPLIT_SLOTS) in self.half_free:
                        self.split_piece(n, s)
                        self.split += 1
                        moved = True
            if not moved:
                return

    def split_piece(self, n, s):
        raw = self.m["raw"][:, n % RAW_SLOTS, :]
        hi, lo = self.m["hi"][:, s % SPLIT_SLOTS, :], self.m["lo"][:, s % SPLIT_SLOTS, :]
        used = self.plan[n][2]
        if used < PIECE:
            raw, hi, lo = raw[:, 0:used], hi[:, 0:used], lo[:, 0:used]
        free = self.half_free.get(s - SPLIT_SLOTS)
        a = self.act.do(lambda e: e.activation(hi, raw, ACT.Copy), self.raw_full[n], free)
        b = self.dve.do(lambda e: e.tensor_tensor(lo, raw, hi.bitcast(F32), ALU.subtract), a)
        self.half_full[n] = [a, b]
        self.raw_free[n] = b

    def halves(self, n):
        if self.plan is None:
            s = 0
        else:
            s = self.split_slot[n] % SPLIT_SLOTS
        return self.m["hi"][:, s, :], self.m["lo"][:, s, :]

    def full(self, n):
        return [] if self.plan is None else self.half_full[n]

    def done_with(self, n, token):
        if self.plan is not None:
            self.half_free[self.split_slot[n]] = token

    def bank(self):
        b = self.ring[self.ring_at % len(self.ring)]
        while b in self.held:
            self.ring_at += 1
            b = self.ring[self.ring_at % len(self.ring)]
        self.ring_at += 1
        self.held.add(b)
        return b, self.bank_free.get(b)

    def use_ring(self, banks):
        self.ring, self.ring_at = list(banks), 0

    def ps(self, b):
        return self.m["psum"][b]

    def gemm_token(self, lhs, weights, evacuate):
        hi, lo, ready = lhs
        for c, (first, second) in enumerate(weights):
            banks = [self.bank() for _ in range(NT)]
            for part, sources in enumerate((first, second)):
                n = self.take(sources)
                wh, wl = self.halves(n)
                wh = wh.rearrange("p (k n) -> p k n", k=KH)
                wl = wl.rearrange("p (k n) -> p k n", k=KH)
                frees = [f for _, f in banks] if part == 0 else None

                def issue(e, part=part, wh=wh, wl=wl, banks=banks):
                    for t in range(NT):
                        for k in range(KH):
                            kk = part * KH + k
                            tok = slice(t * P, t * P + P)
                            for i, (a, b) in enumerate(((hi, wh), (hi, wl), (lo, wh))):
                                last = e.matmul(self.ps(banks[t][0])[:], a[:, kk, tok], b[:, k, :],
                                                start=(kk == 0 and i == 0), stop=(kk == KD - 1 and i == 2))
                    return last
                done = self.pe.do(issue, self.full(n), ready, frees)
                self.done_with(n, done)
                yield
            for t in range(NT):
                self.bank_free[banks[t][0]] = evacuate(c, t, self.ps(banks[t][0]), done)

    def gemm_feature(self, lhs, weights, evacuate, bias=None):
        hi, lo, ready = lhs
        for c, (first, second) in enumerate(weights):
            banks = [self.bank() for _ in range(2)]
            n0 = self.take(first)
            yield
            n1 = self.take(second)
            parts = [[x.rearrange("p (k n) -> p k n", k=KH) for x in self.halves(n)] for n in (n0, n1)]

            def issue(e, m, parts=parts, banks=banks):
                out = self.ps(banks[m // 2][0])[:, (m % 2) * SEQ:(m % 2) * SEQ + SEQ]
                for kk in range(KD):
                    wh, wl = parts[kk // KH]
                    cols = slice(m * P, m * P + P)
                    for i, (a, b) in enumerate(((hi, wh), (hi, wl), (lo, wh))):
                        last = e.matmul(out, b[:, kk % KH, cols], a[:, kk, :], start=(kk == 0 and i == 0),
                                        stop=(kk == KD - 1 and i == 2))
                return last
            for m in range(4):
                done = self.pe.do(lambda e, m=m, issue=issue: issue(e, m), self.full(n0), self.full(n1), ready,
                                  [f for _, f in banks])
                if m % 2:
                    b = banks[m // 2][0]
                    self.bank_free[b] = evacuate(c, m // 2, self.ps(b), done)
            self.done_with(n0, done)
            self.done_with(n1, done)
            yield

    def to_lhs(self, src, ready, dst, free, affine=None):
        hi, lo = dst
        m = self.m
        tokens = []
        for j in range(KD // 2):
            b, bank_free = self.bank()
            ps = self.ps(b)

            def turn(e, j=j, ps=ps):
                for k in range(2):
                    for t in range(NT):
                        kk = 2 * j + k
                        last = e.transpose(ps[:, k * SEQ + t * P:k * SEQ + t * P + P],
                                           src[:, t, kk * P:kk * P + P], m["ident"][:])
                return last
            turned = self.pe.do(turn, ready, self.const, bank_free)
            value, at, last_read = ps[:], turned, None
            if affine is not None:
                scale, shift, known = affine
                tmp = m["ex"][:, j % 2, :]
                for k in range(2):
                    kk = 2 * j + k
                    s = slice(k * SEQ, k * SEQ + SEQ)
                    at = self.dve.do(lambda e, s=s, kk=kk, tmp=tmp, ps=ps: e.tensor_scalar(
                        tmp[:, s], ps[:, s], scale[:, kk:kk + 1], shift[:, kk:kk + 1], ALU.mult, ALU.add),
                        turned, known, self.freed.get("ex"), tokens[2 * j - 4:2 * j - 2] if j >= 2 else None)
                self.bank_free[b] = at
                value = tmp
            h, l = hi[:, 2 * j:2 * j + 2, :], lo[:, 2 * j:2 * j + 2, :]
            a = self.act.do(lambda e, h=h, value=value: e.activation(h, value, ACT.Copy), at, free)
            d = self.dve.do(lambda e, h=h, l=l, value=value: e.tensor_tensor(l, value, h.bitcast(F32), ALU.subtract),
                            a, free)
            if affine is None:
                self.bank_free[b] = d
            tokens += [a, d]
        self.freed["ex"] = [self.freed.get("ex"), tokens]
        return (hi, lo, tokens)

    def latest(self):
        return [(q.name, q.count) for q in (self.pe, self.act, self.dve) if q.count]

    def inverse_root(self, x, eps, scratch, after):
        a = self.dve.do(lambda e: e.tensor_scalar(scratch, x, eps, None, ALU.add), after)
        b = self.act.do(lambda e: e.activation(scratch, scratch, ACT.Sqrt), a)
        return self.dve.do(lambda e: e.reciprocal(scratch, scratch), b)

    def layer_norm(self, x, ready, g, b, rows):
        m = self.m
        tokens = []
        for t in range(NT):
            for h in range(2):
                tokens.append(self.dve.do(lambda e, t=t, h=h: e.bn_stats(
                    m["bn"][:, t, h, :], x[:, t, h * BANK:(h + 1) * BANK]), ready[t]))
        agg = [self.dve.do(lambda e, t=t: e.bn_aggr(m["mv"][:, t, :], m["bn"][:, t, :, :]), tokens) for t in range(NT)]
        rstd = m["rstd"][:, 0:NT]
        r = self.inverse_root(m["mv"][:, :, 1], EPS, rstd, agg)
        nb = self.dve.do(lambda e: e.scalar_tensor_tensor(out=m["nb"][:, 0:NT], in0=m["mv"][:, :, 0], scalar=-1.0,
                                                          in1=rstd, op0=ALU.mult, op1=ALU.mult), r)
        out = []
        for t in range(NT):
            n = self.dve.do(lambda e, t=t: e.tensor_scalar(x[:, t, :], x[:, t, :], m["rstd"][:, t:t + 1],
                                                           m["nb"][:, t:t + 1], ALU.mult, ALU.add), nb)
            n = self.dve.do(lambda e, t=t: e.tensor_tensor(x[:, t, :], x[:, t, :], g, ALU.mult), n, rows)
            out.append(self.dve.do(lambda e, t=t: e.tensor_tensor(x[:, t, :], x[:, t, :], b, ALU.add), n))
        self.freed["rows"] = out
        return out

    def rows(self, name, g, b):
        m = self.m
        free = self.freed.get("rows")
        a = self.load(name + "_g", m["row_g"][:], g.partition_broadcast(P), free)
        c = self.load(name + "_b", m["row_b"][:], b.partition_broadcast(P), free)
        return m["row_g"][:], m["row_b"][:], [a, c]


def whole(n):
    return lambda slot: slot.rearrange("p (k n) -> p k n", n=n)


def column_pieces(w, c0):
    v = w.rearrange("(k p) n -> p k n", p=P)
    return [[(whole(BANK), v[:, part * KH:(part + 1) * KH, c0:c0 + BANK])] for part in range(2)]


def columns(w, c0, n):
    return [column_pieces(w, c0 + c * BANK) for c in range(n // BANK)]


def drain(steps):
    for _ in steps:
        pass


def step(steps):
    next(steps, None)


def mover(queue):
    if queue.name == "act":
        return lambda dst, src, *after: queue.do(lambda e: e.activation(dst, src, ACT.Copy), *after)
    return lambda dst, src, *after: queue.do(lambda e: e.tensor_copy(dst, src), *after)


class Blocks(Program):

    def claim(self, *names):
        return [self.freed.get(n) for n in names]

    def release(self, *names):
        for n in names:
            self.freed[n] = self.latest()

    def tok(self, name):
        return self.m[name][:].rearrange("p (t n) -> p t n", t=NT)

    def feat(self, name, tokens=SEQ):
        return self.m[name][:].rearrange("p (k s) -> p k s", s=tokens)

    def begin(self):
        d, m = self.dram, self.m
        self.const = self.load("ident", m["ident"][:], d["ident"], queue=self.act)
        mem = self.load("mem", self.tok("b4"), d["mem"][0].rearrange("(t p) n -> p t n", p=P), queue=self.act)
        self.x_in = self.load("x", self.tok("x"), d["x"][0].rearrange("(t p) n -> p t n", p=P), queue=self.act)
        self.mem_in = mem
        self.ones = self.dve.do(lambda e: e.memset(m["ones"][:], 1.0))
        self.tables = [self.load("dist", m["dist"][:], d["dist"]),
                       self.load("decay", m["decay"][:], d["decay"].rearrange("p h w n -> p (h w n)")),
                       self.load("window", m["window"][:], d["window"]),
                       self.load("rope", m["rope"][:], d["rope"].rearrange("(t p) w n -> p t w n", p=P)),
                       self.load("index", m["index"][:], d["index"])]

    def first_block(self):
        d, m = self.dram, self.m
        w_in, w_kv = d["w_in"][0], d["w_mem_kv"][0]
        x = self.tok("x")
        mem_t = self.to_lhs(self.tok("b4"), self.mem_in, (m["yt_hi"], m["yt_lo"]), None)
        self.release("b4")
        self.xt = self.to_lhs(x, self.x_in, (m["xt_hi"], m["xt_lo"]), None)

        act_move, dve_move = mover(self.act), mover(self.dve)
        k_f, v_t, q_f = self.feat("b2"), self.tok("b3"), self.feat("b0")
        made = {"k": [], "v": [], "q": [], "gate": []}

        def to_feat(dst, key, free):
            def evacuate(c, pair, ps, done):
                f = 4 * c + 2 * pair
                token = act_move(dst[:, f:f + 2, :], ps[:], done, free)
                made[key].append(token)
                return token
            return evacuate

        def to_tok(dst, key, free, func=ACT.Copy):
            def evacuate(c, t, ps, done):
                token = self.act.do(lambda e: e.activation(dst[:, t, c * BANK:(c + 1) * BANK], ps[:], func),
                                    done, free)
                made[key].append(token)
                return token
            return evacuate
        drain(self.gemm_feature(mem_t, columns(w_kv, 0, D), to_feat(k_f, "k", self.claim("b2"))))
        drain(self.gemm_token(mem_t, columns(w_kv, D, D), to_tok(v_t, "v", self.claim("b3"))))
        self.release("b0", "b1")
        drain(self.gemm_feature(self.xt, columns(w_in, 6 * D, D), to_feat(q_f, "q", self.claim("b0"))))
        y = self.tok("b4")
        free = self.claim("b4")
        written = self.softmax_heads(self.memory_units(q_f, k_f, v_t, y, made, free), None)
        self.release("b0", "b1", "b2", "b3")
        yt = self.to_lhs(y, written, (m["yt_hi"], m["yt_lo"]), self.claim("b0", "b1"))
        self.release("b4")
        drain(self.gates(2, "b2"))
        self.branch(2, yt, "b2", first=True)

        made.update({"k": [], "v": [], "q": []})
        q_f, k_f, v_t, y = self.feat("b0"), self.feat("b1"), self.tok("b2"), self.tok("b3")
        drain(self.gemm_feature(self.xt, columns(w_in, 0, D), to_feat(q_f, "q", self.claim("b0"))))
        drain(self.gemm_feature(self.xt, columns(w_in, D, D), to_feat(k_f, "k", self.claim("b1"))))
        drain(self.gemm_token(self.xt, columns(w_in, 2 * D, D), to_tok(v_t, "v", self.claim("b2"))))
        lam = self.lambda_full()
        filler = self.gates(0, "b4")
        written = self.softmax_heads(self.differential_units(q_f, k_f, v_t, y, made, self.claim("b3"), lam), filler)
        drain(filler)
        written = self.differential_norm(y, written)
        self.release("b0", "b1", "b2")
        yt = self.to_lhs(y, written, (m["yt_hi"], m["yt_lo"]), self.claim("b0", "b1"))
        self.release("b3")
        self.branch(0, yt, "b4", first=False)

        made.update({"k": [], "v": [], "q": []})
        qk, v_t, y = self.feat("b0"), self.tok("b1"), self.tok("b3")
        gate_silu = self.tok("b2")
        g, b, rows = self.rows("gn", d["ret_gn_g"][0], d["ret_gn_b"][0])
        drain(self.gemm_feature(self.xt, columns(w_in, 3 * D, D), to_feat(qk, "q", self.claim("b0"))))
        drain(self.gemm_token(self.xt, columns(w_in, 4 * D, D), to_tok(v_t, "v", self.claim("b1"))))
        filler = self.then(self.gemm_token(self.xt, columns(w_in, 5 * D, D),
                                           to_tok(gate_silu, "gate", self.claim("b2"), ACT.Silu)),
                           self.gates(1, "b4"))
        written = self.retention(qk, v_t, y, made, self.claim("b3"), filler)
        drain(filler)
        written = self.retention_norm(y, written, gate_silu, made["gate"], g, b, rows)
        self.release("b0", "b1", "b2", "xt")
        yt = self.to_lhs(y, written, (m["yt_hi"], m["yt_lo"]), self.claim("b0", "b1"))
        self.release("b3")
        self.branch(1, yt, "b4", first=False)

        g, b, rows = self.rows("ln1", d["ln1_g"][0], d["ln1_b"][0])
        yt = self.to_lhs(self.tok("mg"), self.merged, (m["yt_hi"], m["yt_lo"]), self.claim("b0", "b1"))
        self.release("mg")
        sums = [[] for _ in range(NT)]

        def residual(c, t, ps, done):
            s = slice(c * BANK, (c + 1) * BANK)
            token = self.dve.do(lambda e: e.scalar_tensor_tensor(out=x[:, t, s], in0=x[:, t, s], scalar=ALPHA_1,
                                                                 in1=ps[:], op0=ALU.mult, op1=ALU.add), done)
            sums[t].append(token)
            return token
        drain(self.gemm_token(yt, columns(d["w_o"][0], 0, D), residual))
        self.release("b0", "b1")
        x_ready = self.layer_norm(x, sums, g, b, rows)
        self.xt = self.to_lhs(x, x_ready, (m["xt_hi"], m["xt_lo"]), self.claim("xt"))
        self.experts(x, x_ready)

    def then(self, *parts):
        for p in parts:
            yield from p

    def gates(self, n, name):
        d, m = self.dram, self.m
        dst, free = self.tok(name), self.claim(name)
        row = self.load(f"gate{n}", m["row_c"][:], d["b_gate"][0, n * D:(n + 1) * D].partition_broadcast(P),
                        self.freed.get("row_c"))
        self.logits = []

        def evacuate(c, t, ps, done):
            s = slice(c * BANK, (c + 1) * BANK)
            token = self.dve.do(lambda e: e.tensor_tensor(dst[:, t, s], ps[:], m["row_c"][:, s], ALU.add),
                                done, free, row)
            self.logits.append(token)
            self.freed["row_c"] = token
            return token
        yield from self.gemm_token(self.xt, columns(d["w_in"][0], 7 * D + n * D, D), evacuate)

    def branch(self, n, yt, gate_name, first):
        m = self.m
        gate, merged = self.tok(gate_name), self.tok("mg")
        known = [self.act.do(lambda e, t=t: e.activation(gate[:, t, :], gate[:, t, :], ACT.Sigmoid), self.logits)
                 for t in range(NT)]
        out = []

        def evacuate(c, t, ps, done):
            s = slice(c * BANK, (c + 1) * BANK)
            if first:
                token = self.dve.do(lambda e: e.tensor_tensor(merged[:, t, s], ps[:], gate[:, t, s], ALU.mult),
                                    done, known)
                out.append(token)
                return token
            tmp = m["sm"][:, t, :]
            token = self.dve.do(lambda e: e.tensor_tensor(tmp, ps[:], gate[:, t, s], ALU.mult), done, known,
                                self.claim("sm"))
            out.append(self.dve.do(lambda e: e.tensor_tensor(merged[:, t, s], merged[:, t, s], tmp, ALU.add),
                                   token, self.merged))
            return token
        drain(self.gemm_token(yt, columns(self.dram["w_branch"][0, n], 0, D), evacuate))
        self.merged = out
        self.freed["sm"] = out
        self.release("b0", "b1", gate_name)

    def softmax_heads(self, units, filler):
        m = self.m
        units = list(units)
        n = len(units)
        base = self.claim("sm", "ex", "sm0", "sm1")
        self.slot_free = [base] * 4
        scored, soft, weighed, turned, written = {}, {}, {}, {}, []
        for i in range(-3, n + 1):
            if i + 3 < n:
                scored[i + 3] = units[i + 3][0](i + 3)
            if 0 <= i + 2 < n:
                soft[i + 2] = units[i + 2][1](i + 2, scored.pop(i + 2))
            if 0 <= i + 1 < n:
                weighed[i + 1] = units[i + 1][2](i + 1, soft.pop(i + 1))
            if filler is not None and i >= 0:
                step(filler)
            if 0 <= i < n:
                weights, known, n_blocks = weighed[i][:3]
                b, free = self.bank()
                ps = self.ps(b)

                def turn(e, weights=weights, ps=ps, n_blocks=n_blocks):
                    for k in range(n_blocks):
                        last = e.transpose(ps[:, k * P:k * P + P], weights[:, k * P:k * P + P], m["ident"][:])
                    return last
                t = self.pe.do(turn, known, free, self.const)
                self.slot_free[i % 4] = t
                at = m["at"][:, i % 2, 0:n_blocks * P]
                c = self.act.do(lambda e, at=at, ps=ps, n_blocks=n_blocks: e.activation(
                    at, ps[:, 0:n_blocks * P], ACT.Copy), t, self.freed.get(f"at{i % 2}"))
                self.bank_free[b] = c
                turned[i] = (at, c, n_blocks)
            if 0 <= i - 1 < n:
                u = i - 1
                at, copied, n_blocks = turned.pop(u)
                values, ready = units[u][3]
                o, free = self.bank()
                out = self.ps(o)[:, 0:values[0].shape[-1]]

                def mix(e, at=at, out=out, values=values, n_blocks=n_blocks):
                    for k in range(n_blocks):
                        last = e.matmul(out, at[:, k * P:k * P + P], values[k], start=(k == 0),
                                        stop=(k == n_blocks - 1))
                    return last
                mixed = self.pe.do(mix, copied, free, ready)
                self.freed[f"at{u % 2}"] = mixed
                w = units[u][4](u, out, mixed, weighed.pop(u))
                self.bank_free[o] = w
                self.freed[f"st{u % 4}"] = w
                written.append(w)
        self.freed["sm"] = self.freed["ex"] = self.latest()
        return written

    def memory_units(self, q_f, k_f, v_t, y, made, free):
        m = self.m
        scale = MEM_DH ** -0.5
        for h in range(MEM_HEADS):
            for t in range(NT):
                def score(u, h=h, t=t):
                    b, bank_free = self.bank()

                    def issue(e):
                        for k in range(2):
                            last = e.matmul(self.ps(b)[:, 0:SEQ], q_f[:, 2 * h + k, t * P:t * P + P],
                                            k_f[:, 2 * h + k, :], start=(k == 0), stop=(k == 1))
                        return last
                    return b, self.pe.do(issue, bank_free, made["q"], made["k"])

                def soften(u, scored):
                    b, done = scored
                    st = m["st"][:, u % 4, :]
                    ps, ex = self.ps(b)[:, 0:SEQ], m["work"][:, u % 4, 0:SEQ]
                    a = self.dve.do(lambda e: e.tensor_reduce(st[:, 0:1], ps, AX.X, ALU.max, negate=True), done,
                                    self.freed.get(f"st{u % 4}"))
                    a = self.dve.do(lambda e: e.tensor_scalar(st[:, 1:2], st[:, 0:1], scale, None, ALU.mult), a)
                    a = self.act.do(lambda e: e.activation(ex, ps, ACT.Exp, bias=st[:, 1:2], scale=scale,
                                                           accum_out=st[:, 2:3]), a, self.slot_free[u % 4])
                    self.bank_free[b] = a
                    return ex, a, st

                def weigh(u, soft):
                    ex, a, st = soft
                    r = self.dve.do(lambda e: e.reciprocal(st[:, 3:4], st[:, 2:3]), a)
                    return ex, a, 2, r, st

                def write(u, out, mixed, weighed, h=h, t=t):
                    r, st = weighed[3:]
                    return self.act.do(lambda e: e.activation(y[:, t, h * MEM_DH:(h + 1) * MEM_DH], out, ACT.Copy,
                                                              scale=st[:, 3:4]), mixed, r, free)
                values = [v_t[:, k, h * MEM_DH:(h + 1) * MEM_DH] for k in range(2)]
                yield score, soften, weigh, (values, made["v"]), write

    def lambda_full(self):
        d, m = self.dram, self.m
        lv = m["row_c"][:, 0:4 * DA_DK]
        got = self.load("lambda", lv, d["da_lambda"][0].rearrange("a b -> (a b)").partition_broadcast(P),
                        self.freed.get("row_c"))
        g = self.load("da_g", m["da_g"][:], d["da_norm_g"][0].partition_broadcast(P))
        v = lv.rearrange("p (a b n) -> p a b n", a=2, b=2)
        tmp = m["sm"][:, 0, 0:2 * DA_DK].rearrange("p (a n) -> p a n", a=2)
        a = self.dve.do(lambda e: e.tensor_tensor(tmp, v[:, :, 0, :], v[:, :, 1, :], ALU.mult), got,
                        self.claim("sm"))
        self.freed["row_c"] = a
        lam = m["lam"]
        a = self.dve.do(lambda e: e.tensor_reduce(lam[:, 0:2], tmp, AX.X, ALU.add), a)
        self.freed["sm"] = a
        a = self.act.do(lambda e: e.activation(lam[:, 2:4], lam[:, 0:2], ACT.Exp), a)
        a = self.dve.do(lambda e: e.tensor_tensor(lam[:, 4:5], lam[:, 3:4], lam[:, 2:3], ALU.subtract), a)
        a = self.dve.do(lambda e: e.tensor_scalar(lam[:, 5:6], lam[:, 4:5], -LAMBDA_INIT, None, ALU.add), a)
        self.da_gain = self.dve.do(lambda e: e.tensor_scalar(m["da_g"][:], m["da_g"][:], 1.0 - LAMBDA_INIT, None,
                                                             ALU.mult), g)
        return a

    def differential_units(self, q_f, k_f, v_t, y, made, free, lam):
        m = self.m
        scale = DA_DK ** -0.5
        for h in range(DA_HEADS):
            for t in range(NT):
                nk = (t + 1) * P

                def score(u, h=h, t=t, nk=nk):
                    banks = [self.bank() for _ in range(2)]

                    def issue(e):
                        for c in range(2):
                            rows = slice(c * DA_DK, (c + 1) * DA_DK)
                            last = e.matmul(self.ps(banks[c][0])[:, 0:nk], q_f[rows, h, t * P:t * P + P],
                                            k_f[rows, h, 0:nk], start=True, stop=True)
                        return last
                    return banks, self.pe.do(issue, [f for _, f in banks], made["q"], made["k"])

                def soften(u, scored, h=h, nk=nk):
                    banks, done = scored
                    st = m["st"][:, u % 4, :]
                    sm = m["work"][:, u % 4, :].rearrange("p (c n) -> p c n", c=2)[:, :, 0:nk]
                    slope = 2.0 ** -(h + 1.0)
                    for c in range(2):
                        ps = self.ps(banks[c][0])[:, 0:nk]
                        a = self.dve.do(lambda e, c=c, ps=ps: e.scalar_tensor_tensor(
                            out=sm[:, c, :], in0=m["dist"][:, SEQ - nk:SEQ], scalar=-slope / scale, in1=ps,
                            op0=ALU.mult, op1=ALU.add), done, self.tables, self.slot_free[u % 4])
                        self.bank_free[banks[c][0]] = a
                    a = self.dve.do(lambda e: e.tensor_reduce(st[:, 0:2], sm, AX.X, ALU.max, negate=True), a,
                                    self.freed.get(f"st{u % 4}"))
                    a = self.dve.do(lambda e: e.tensor_scalar(st[:, 2:4], st[:, 0:2], scale, None, ALU.mult), a)
                    for c in range(2):
                        x = self.act.do(lambda e, c=c: e.activation(sm[:, c, :], sm[:, c, :], ACT.Exp,
                                                                    bias=st[:, 2 + c:3 + c], scale=scale,
                                                                    accum_out=st[:, 4 + c:5 + c]), a)
                    return sm, x, st

                def weigh(u, soft, t=t):
                    sm, x, st = soft
                    a = self.dve.do(lambda e: e.reciprocal(st[:, 6:8], st[:, 4:6]), x)
                    a = self.dve.do(lambda e: e.tensor_tensor(st[:, 8:9], st[:, 7:8], m["lam"][:, 5:6], ALU.mult),
                                    a, lam)
                    b = self.dve.do(lambda e: e.tensor_scalar(sm[:, 0, :], sm[:, 0, :], st[:, 6:7], None, ALU.mult), a)
                    b = self.dve.do(lambda e: e.scalar_tensor_tensor(out=sm[:, 0, :], in0=sm[:, 1, :],
                                                                     scalar=st[:, 8:9], in1=sm[:, 0, :],
                                                                     op0=ALU.mult, op1=ALU.add), b)
                    return sm[:, 0, :], b, t + 1

                def write(u, out, mixed, weighed, h=h, t=t):
                    a = self.act.do(lambda e: e.activation(y[:, t, h * DA_DV:(h + 1) * DA_DV], out, ACT.Copy),
                                    mixed, free)
                    i = t * DA_HEADS + h
                    return self.act.do(lambda e: e.activation(m["junk"][:], out, ACT.Square,
                                                              accum_out=m["unit"][:, i:i + 1]), a,
                                       self.junk_free)
                values = [v_t[:, k, h * DA_DV:(h + 1) * DA_DV] for k in range(t + 1)]
                yield score, soften, weigh, (values, made["v"]), write

    def differential_norm(self, y, written):
        m = self.m
        ms = m["unit"][:, 0:NT * DA_HEADS]
        a = self.dve.do(lambda e: e.tensor_scalar(ms, ms, 1.0 / DA_DV, EPS, ALU.mult, ALU.add), written)
        a = self.act.do(lambda e: e.activation(ms, ms, ACT.Sqrt), a)
        r = self.dve.do(lambda e: e.reciprocal(ms, ms), a)
        out = []
        for t in range(NT):
            for h in range(DA_HEADS):
                s = slice(h * DA_DV, (h + 1) * DA_DV)
                out.append(self.dve.do(lambda e, t=t, h=h, s=s: e.scalar_tensor_tensor(
                    out=y[:, t, s], in0=y[:, t, s], scalar=ms[:, t * DA_HEADS + h:t * DA_HEADS + h + 1],
                    in1=m["da_g"][:], op0=ALU.mult, op1=ALU.mult), r, self.da_gain))
        self.freed["sm"] = self.latest()
        self.freed["ex"] = self.freed["sm"]
        return out[-1]

    def retention(self, qk, v_t, y, made, free, filler):
        m = self.m
        decay = m["decay"][:].rearrange("p (h n) -> p h n", h=RET_HEADS)
        written = []
        pairs = ((0, 0), (0, 1), (1, 1))
        for h in range(RET_HEADS):
            b, bank_free = self.bank()
            ps = self.ps(b)

            def score(e, h=h, ps=ps):
                for i, (k, q) in enumerate(pairs):
                    last = e.matmul(ps[:, i * P:i * P + P], qk[:, RET_HEADS + h, k * P:k * P + P],
                                    qk[:, h, q * P:q * P + P], start=True, stop=True)
                return last
            scored = self.pe.do(score, bank_free, made["q"])
            sm = m["sm"][:, h % 2, :]
            last_use = self.freed.get(f"sm{h % 2}")
            a = self.dve.do(lambda e, h=h, ps=ps, sm=sm: e.tensor_tensor(sm[:, 0:2 * P], ps[:, 0:2 * P],
                                                                         decay[:, h, :], ALU.mult),
                            scored, self.tables, last_use, self.claim("sm"))
            a = self.dve.do(lambda e, h=h, ps=ps, sm=sm: e.tensor_tensor(sm[:, 2 * P:3 * P], ps[:, 2 * P:3 * P],
                                                                         decay[:, h, 0:P], ALU.mult), scored)
            self.bank_free[b] = a
            step(filler)
            step(filler)
            o, bank_free = self.bank()
            out = self.ps(o)

            def mix(e, h=h, sm=sm, out=out):
                v = slice(h * RET_DV, (h + 1) * RET_DV)
                e.matmul(out[:, 0:RET_DV], sm[:, 0:P], v_t[:, 0, v], start=True, stop=True)
                e.matmul(out[:, RET_DV:], sm[:, P:2 * P], v_t[:, 0, v], start=True, stop=False)
                return e.matmul(out[:, RET_DV:], sm[:, 2 * P:3 * P], v_t[:, 1, v], start=False, stop=True)
            mixed = self.pe.do(mix, a, bank_free, made["v"])
            self.freed[f"sm{h % 2}"] = mixed
            for t in range(NT):
                s = self.dve.do(lambda e, t=t, out=out: e.bn_stats(m["bn"][:, t, 0, :],
                                                                   out[:, t * RET_DV:(t + 1) * RET_DV]),
                                mixed, written)
                s = self.dve.do(lambda e, t=t, h=h: e.bn_aggr(m["gn"][:, t * RET_HEADS + h, :],
                                                              m["bn"][:, t, 0, :]), s)
            a = self.act.do(lambda e, h=h, out=out: e.activation(
                y[:, :, h * RET_DV:(h + 1) * RET_DV], out[:].rearrange("p (t n) -> p t n", t=NT), ACT.Copy), s, free)
            self.bank_free[o] = a
            written = [s, a]
        return written

    def retention_norm(self, y, written, gate, gate_ready, g, b, rows):
        m = self.m
        n = NT * RET_HEADS
        mean, var = m["gn"][:, :, 0], m["gn"][:, :, 1]
        rstd, nb = m["rstd"][:, 0:n], m["nb"][:, 0:n]
        r = self.inverse_root(var, EPS, rstd, written)
        r = self.dve.do(lambda e: e.scalar_tensor_tensor(out=nb, in0=mean, scalar=-1.0, in1=rstd, op0=ALU.mult,
                                                         op1=ALU.mult), r)
        out = []
        for t in range(NT):
            for h in range(RET_HEADS):
                s, i = slice(h * RET_DV, (h + 1) * RET_DV), t * RET_HEADS + h
                a = self.dve.do(lambda e, t=t, s=s, i=i: e.tensor_scalar(
                    y[:, t, s], y[:, t, s], rstd[:, i:i + 1], nb[:, i:i + 1], ALU.mult, ALU.add), r)
            a = self.dve.do(lambda e, t=t: e.tensor_tensor(y[:, t, :], y[:, t, :], g, ALU.mult), a, rows)
            a = self.dve.do(lambda e, t=t: e.tensor_tensor(y[:, t, :], y[:, t, :], b, ALU.add), a)
            a = self.dve.do(lambda e, t=t: e.tensor_tensor(y[:, t, :], y[:, t, :], gate[:, t, :], ALU.mult), a,
                            gate_ready)
            out.append(a)
        self.freed["rows"] = out
        self.freed["sm"] = self.latest()
        self.release("decay")
        return out

    def feed_forward(self, lhs, n_chunks, up, down, pair, finish, between=None):
        m = self.m
        self.use_ring(range(4, 8))
        acc_free = [self.bank_free.get(b) for b in range(4)]
        hidden = m["b1"][:, 0:2 * NT * F_CHUNK].rearrange("p (s t n) -> p s t n", s=2, t=NT)
        gated = m["b1"][:, 2 * NT * F_CHUNK:].rearrange("p (s t n) -> p s t n", s=2, t=NT)
        hidden_free, turned_free = [self.claim("b1")] * 2, [self.claim("b0")] * 2
        state = {}

        def up_part(i):
            banks = []

            def keep(c, t, ps, done):
                banks.append(([x for x in range(8) if self.ps(x) is ps][0], done))

            yield from self.gemm_token(lhs, [up(i)], keep)
            slot = i % 2
            out = []
            for t, (b, done) in enumerate(banks):
                ps = self.ps(b)
                a = self.act.do(lambda e, t=t, ps=ps: e.activation(gated[:, slot, t, :], ps[:, F_CHUNK:], ACT.Silu),
                                done, hidden_free[slot])
                h = self.dve.do(pair(i, t, hidden[:, slot, t, :], ps[:, 0:F_CHUNK], gated[:, slot, t, :]), a,
                                self.combined, hidden_free[slot])
                self.bank_free[b] = h
                out.append(h)
            state[i] = out

        def turn_part(i):
            slot = i % 2
            b, bank_free = self.bank()
            ps = self.ps(b)

            def turn(e):
                for k in range(2):
                    for t in range(NT):
                        last = e.transpose(ps[:, k * SEQ + t * P:k * SEQ + t * P + P],
                                           hidden[:, slot, t, k * P:k * P + P], m["ident"][:])
                return last
            turned = self.pe.do(turn, state.pop(i), bank_free)
            hidden_free[slot] = turned
            hi, lo = m["ht_hi"][:, slot, :, :], m["ht_lo"][:, slot, :, :]
            a = self.act.do(lambda e: e.activation(hi, ps[:], ACT.Copy), turned, turned_free[slot])
            v = self.dve.do(lambda e: e.tensor_tensor(lo, ps[:], hi.bitcast(F32), ALU.subtract), a,
                            turned_free[slot])
            self.bank_free[b] = v
            return hi, lo, [a, v]

        def down_part(i, hi, lo, halves):
            slot = i % 2
            n = self.take(down(i))
            wh, wl = [w.rearrange("p (k n) -> p k n", k=2) for w in self.halves(n)]

            def issue(e, t):
                for k in range(2):
                    tok = slice(t * P, t * P + P)
                    for j, (x, w) in enumerate(((hi, wh), (hi, wl), (lo, wh))):
                        for half in range(2):
                            last = e.matmul(self.ps(2 * t + half)[:], x[:, k, tok],
                                            w[:, k, half * BANK:(half + 1) * BANK],
                                            start=(i == 0 and k == 0 and j == 0),
                                            stop=(i == n_chunks - 1 and k == 1 and j == 2))
                return last
            done = [self.pe.do(lambda e, t=t: issue(e, t), halves, self.full(n), acc_free if i == 0 else None)
                    for t in range(NT)]
            turned_free[slot] = done[-1]
            self.done_with(n, done[-1])
            return done

        def tick():
            if between is not None:
                between()

        drain(up_part(0))
        for i in range(n_chunks):
            parts = up_part(i + 1) if i + 1 < n_chunks else iter(())
            step(parts)
            tick()
            turned = turn_part(i)
            drain(parts)
            tick()
            done = down_part(i, *turned)
            tick()
        for t in range(NT):
            for half in range(2):
                self.bank_free[2 * t + half] = finish(t, half, self.ps(2 * t + half), done[t])
        self.freed["b0"] = self.freed["b1"] = self.latest()
        self.use_ring(range(8))

    def experts(self, x, x_ready):
        d, m = self.dram, self.m
        self.combined = self.router()
        w1, w3, w2 = d["w1"][0], d["w3"][0], d["w2"][0]

        def up(i):
            e, c0 = i // 2, (i % 2) * F_CHUNK
            a = w3[e].rearrange("(k p) n -> p k n", p=P)
            g = w1[e].rearrange("(k p) n -> p k n", p=P)
            return [[(lambda s: whole(BANK)(s)[:, :, 0:F_CHUNK], a[:, q * KH:(q + 1) * KH, c0:c0 + F_CHUNK]),
                     (lambda s: whole(BANK)(s)[:, :, F_CHUNK:], g[:, q * KH:(q + 1) * KH, c0:c0 + F_CHUNK])]
                    for q in range(2)]

        def down(i):
            e, c0 = i // 2, (i % 2) * F_CHUNK
            return [(whole(D), w2[e, c0:c0 + F_CHUNK, :].rearrange("(k p) n -> p k n", p=P))]

        def pair(i, t, out, a, g):
            c = m["combine"][:, t, i // 2:i // 2 + 1]
            return lambda e: e.scalar_tensor_tensor(out=out, in0=a, scalar=c, in1=g, op0=ALU.mult, op1=ALU.mult)
        sums = [[] for _ in range(NT)]

        def finish(t, half, ps, done):
            s = slice(half * BANK, (half + 1) * BANK)
            token = self.dve.do(lambda e: e.scalar_tensor_tensor(out=x[:, t, s], in0=x[:, t, s], scalar=ALPHA_1,
                                                                 in1=ps[:], op0=ALU.mult, op1=ALU.add), done)
            sums[t].append(token)
            return token
        g, b, rows = self.rows("ln2", d["ln2_g"][0], d["ln2_b"][0])
        self.condition()
        tick, mods = self.paced(0, range(2 * N_MOD), "b3", N_EXPERTS * 2)
        self.feed_forward(self.xt, N_EXPERTS * 2, up, down, pair, finish, tick)
        drain(mods)
        self.release("xt")
        self.x_ready = self.layer_norm(x, sums, g, b, rows)

    def router(self):
        d, m = self.dram, self.m
        nr = N_GROUPS + N_EXPERTS
        raw = m["sm"][:, 0, 0:KD * nr].rearrange("p (k n) -> p k n", k=KD)
        w = [self.load("w_rg", raw[:, :, 0:N_GROUPS], d["w_rg"][0].rearrange("(k p) n -> p k n", p=P),
                       self.claim("sm")),
             self.load("w_re", raw[:, :, N_GROUPS:], d["w_re"][0].rearrange("(k p) n -> p k n", p=P))]
        bias = [self.load("b_rg", m["r_bias"][:, 0:N_GROUPS], d["b_rg"][0].partition_broadcast(P)),
                self.load("b_re", m["r_bias"][:, N_GROUPS:], d["b_re"][0].partition_broadcast(P))]
        a = self.act.do(lambda e: e.activation(m["r_hi"][:], raw, ACT.Copy), w)
        s = self.dve.do(lambda e: e.tensor_tensor(m["r_lo"][:], raw, m["r_hi"][:].bitcast(F32), ALU.subtract), a)
        self.freed["sm"] = s
        hi, lo, ready = self.xt
        b, bank_free = self.bank()
        ps = self.ps(b)

        def issue(e):
            for t in range(NT):
                for k in range(KD):
                    for i, (x, w_) in enumerate(((hi, m["r_hi"]), (hi, m["r_lo"]), (lo, m["r_hi"]))):
                        last = e.matmul(ps[:, t * nr:(t + 1) * nr], x[:, k, t * P:t * P + P], w_[:, k, :],
                                        start=(k == 0 and i == 0), stop=(k == KD - 1 and i == 2))
            return last
        done = self.pe.do(issue, ready, a, s, bank_free)
        out = []
        for t in range(NT):
            out.append(self.route(t, ps[:, t * nr:(t + 1) * nr], done, bias, b))
        return out

    def route(self, t, ps, done, bias, bank):
        m, v = self.m, self.dve.do
        r = m["route"][:, t, :]
        lg = r[:, 0:20]
        groups, experts = r[:, 0:4], r[:, 4:20]
        a = v(lambda e: e.tensor_tensor(lg, ps, m["r_bias"][:], ALU.add), done, bias)
        self.bank_free[bank] = a

        def first_of_largest(values, top, tmp, hot, a):
            a = v(lambda e: e.tensor_reduce(top, values, AX.X, ALU.max), a)
            a = v(lambda e: e.tensor_scalar(tmp, values, top, None, ALU.is_equal), a)
            a = v(lambda e: e.scalar_tensor_tensor(out=tmp, in0=tmp, scalar=-100.0, in1=m["index"][:],
                                                   op0=ALU.mult, op1=ALU.add), a, self.tables)
            a = v(lambda e: e.tensor_reduce(r[:, 50:51], tmp, AX.X, ALU.min), a)
            return v(lambda e: e.tensor_scalar(hot, tmp, r[:, 50:51], None, ALU.is_equal), a)
        tmp, g_hot, sel, hot1, hot2 = r[:, 20:24], r[:, 24:28], r[:, 28:32], r[:, 32:36], r[:, 36:40]
        a = first_of_largest(groups, r[:, 40:41], tmp, g_hot, a)
        a = v(lambda e: e.tensor_scalar(r[:, 41:42], r[:, 40:41], -1.0, None, ALU.mult), a)
        x = self.act.do(lambda e: e.activation(tmp, groups, ACT.Exp, bias=r[:, 41:42], accum_out=r[:, 42:43]), a)
        p_top = v(lambda e: e.reciprocal(r[:, 43:44], r[:, 42:43]), x)
        a = v(lambda e: e.tensor_scalar(sel, experts[:, 0:4], g_hot[:, 0:1], None, ALU.mult), p_top)
        for g in range(1, N_GROUPS):
            a = v(lambda e, g=g: e.scalar_tensor_tensor(out=sel, in0=experts[:, 4 * g:4 * g + 4],
                                                        scalar=g_hot[:, g:g + 1], in1=sel, op0=ALU.mult,
                                                        op1=ALU.add), a)
        a = first_of_largest(sel, r[:, 44:45], tmp, hot1, a)
        a = v(lambda e: e.scalar_tensor_tensor(out=sel, in0=hot1, scalar=-MASKED, in1=sel, op0=ALU.mult,
                                               op1=ALU.add), a)
        a = first_of_largest(sel, r[:, 45:46], tmp, hot2, a)
        a = v(lambda e: e.tensor_tensor(r[:, 46:47], r[:, 45:46], r[:, 44:45], ALU.subtract), a)
        x = self.act.do(lambda e: e.activation(r[:, 47:48], r[:, 46:47], ACT.Exp), a)
        a = v(lambda e: e.tensor_scalar(r[:, 48:49], r[:, 47:48], 1.0, None, ALU.add), x)
        a = v(lambda e: e.reciprocal(r[:, 49:50], r[:, 48:49]), a)
        a = v(lambda e: e.tensor_tensor(r[:, 49:50], r[:, 49:50], r[:, 43:44], ALU.mult), a)
        a = v(lambda e: e.tensor_tensor(r[:, 48:49], r[:, 49:50], r[:, 47:48], ALU.mult), a)
        a = v(lambda e: e.tensor_scalar(hot1, hot1, r[:, 49:50], None, ALU.mult), a)
        a = v(lambda e: e.scalar_tensor_tensor(out=hot1, in0=hot2, scalar=r[:, 48:49], in1=hot1, op0=ALU.mult,
                                               op1=ALU.add), a)
        for g in range(N_GROUPS):
            last = v(lambda e, g=g: e.tensor_scalar(m["combine"][:, t, 4 * g:4 * g + 4], hot1, g_hot[:, g:g + 1],
                                                    None, ALU.mult), a)
        return last

    def condition(self):
        d, m = self.dram, self.m
        rows = m["junk"][0:2 * KD, :]
        free = self.latest()
        got = [self.load("c", rows[0:KD, :], d["c_2"][0].rearrange("(k p) -> k p", p=P), free),
               self.load("c_ctx", rows[KD:2 * KD, :], d["c_ctx_2"].rearrange("(k p) -> k p", p=P))]
        b, bank_free = self.bank()
        ps = self.ps(b)
        done = self.pe.do(lambda e: e.transpose(ps[:, 0:2 * KD], rows, m["ident"][0:2 * KD, 0:2 * KD]), got,
                          bank_free, self.const)
        self.c_ready = self.act.do(lambda e: e.activation(m["cvec"][:].rearrange("p v k -> p (v k)"),
                                                          ps[:, 0:2 * KD], ACT.Silu), done)
        self.bank_free[b] = self.c_ready

    def modulation(self, layer, chunks, ring):
        d, m = self.dram, self.m
        w = d["mod_w_2"][layer].rearrange("(k p) n -> p k n", p=P)
        acc = (m["b2"][:].rearrange("p (s v n) -> p s v n", s=2, v=2) if layer == 0 else
               m["decay"][:].rearrange("p (s v n) -> p s v n", s=2, v=1))
        slots = m[ring][:].rearrange("p (s k n) -> p s k n", s=2, k=2)
        acc_free = [self.claim("b2" if layer == 0 else "decay")] * 2
        slot_free = [self.claim(ring)] * 2
        bias_free = [self.freed.get("row_c")] * 2
        mg, b4 = self.tok("mg"), self.tok("b4")
        gate_rows = {0: [[mg[:, 0, :], mg[:, 1, :]], [b4[:, 0, :]], [b4[:, 1, :]]],
                     1: [[mg[:, 0, :]], [mg[:, 1, :]], [b4[:, 0, :]]]}[layer]
        gate_free = self.claim("mg", "b4")
        self.mod_ready = self.mod_ready or {}
        ready = self.mod_ready.setdefault(layer, [])
        quarters = [(c, q) for c in chunks for q in range(KD // 2)]
        landed = {}

        def fetch(i):
            if i < len(quarters):
                c, q = quarters[i]
                s = i % 2
                self.sync.wait(slot_free[s])
                sem = f"mod{s}"
                self.sems.add(sem)
                src = w[:, 2 * q:2 * q + 2, c * BANK:(c + 1) * BANK]
                self.sync.steps.append(("dma", lambda e: e.dma_start(slots[:, s, :, :], src), sem))
                self.mod_count[s] += 16
                landed[i] = (sem, self.mod_count[s])

        def start(at, c):
            vectors = 2 if layer == 0 and c // 2 < 5 else 1
            slot = (at // 4) % 2
            bias = m["row_c"][0:1, slot * BANK:(slot + 1) * BANK]
            b = self.load(f"mod_b{layer}_{c}", bias, d["mod_b_2"][layer:layer + 1, c * BANK:(c + 1) * BANK],
                          bias_free[slot])
            chain = [None] * vectors
            for q in range(KD // 2):
                i = at + q
                s = i % 2
                for v in range(vectors):
                    out = acc[:, slot, v, :]
                    for k in range(2):
                        kk = 2 * q + k
                        col = m["cvec"][:, v, kk:kk + 1]
                        wk = slots[:, s, k, :]
                        after = [landed[i], self.c_ready, acc_free[slot] if kk == 0 else None, chain[v]]
                        if kk == 0:
                            chain[v] = self.dve.do(lambda e, out=out, wk=wk, col=col: e.tensor_scalar(
                                out, wk, col, None, ALU.mult), after)
                        else:
                            chain[v] = self.dve.do(lambda e, out=out, wk=wk, col=col: e.scalar_tensor_tensor(
                                out=out, in0=wk, scalar=col, in1=out, op0=ALU.mult, op1=ALU.add), after)
                slot_free[s] = chain[-1]
                yield
                fetch(i + 2)
            self.started = (c, vectors, slot, bias, b, chain[-1])

        def finish(c, vectors, slot, bias, b, a):
            j, half = c // 2, c % 2
            for v in range(vectors):
                if j % 3 == 2:
                    if v >= len(gate_rows[j // 3]):
                        continue
                    bank, free = self.bank()
                    ps = self.ps(bank)

                    def issue(e, v=v, ps=ps):
                        e.matmul(ps[:], m["ones"][:], acc[:, slot, v, :], start=True, stop=False)
                        return e.matmul(ps[:], m["ones"][0:1, :], bias, start=False, stop=True)
                    done = self.pe.do(issue, a, b, free, self.ones)
                    row = gate_rows[j // 3][v][:, half * BANK:(half + 1) * BANK]
                    half_of = 1.0 if j // 3 == 1 else 0.5
                    token = self.act.do(lambda e, ps=ps, row=row: e.activation(row, ps[:], ACT.Copy, scale=half_of),
                                        done, gate_free)
                else:
                    bank, free = self.bank()
                    ps = self.ps(bank)

                    def issue(e, v=v, ps=ps):
                        for i in range(4):
                            cols = slice(i * P, i * P + P)
                            e.matmul(ps[:, i:i + 1], acc[:, slot, v, cols], m["ones"][:, 0:1], start=True, stop=False)
                            last = e.matmul(ps[:, i:i + 1], bias[:, cols], m["ones"][0:1, 0:1], start=False,
                                            stop=True)
                        return last
                    done = self.pe.do(issue, a, b, free, self.ones)
                    f = j * KD + half * 4
                    out = m["mod"][:, 2 * layer + v, f:f + 4]
                    token = self.dve.do(lambda e, out=out, ps=ps: e.tensor_scalar(
                        out, ps[:, 0:4], 1.0 if j % 3 == 1 else 0.0, None, ALU.add), done)
                self.bank_free[bank] = token
                ready.append(token)
                acc_free[slot] = done
                bias_free[slot] = done

        fetch(0)
        fetch(1)
        yield
        started = None
        for n, c in enumerate(chunks):
            yield from start(4 * n, c)
            if started is not None:
                finish(*started)
            started = self.started
        finish(*started)
        self.release("b2" if layer == 0 else "decay", "row_c", ring)

    def paced(self, layer, chunks, ring, n_chunks):
        steps = self.modulation(layer, chunks, ring)
        total, ticks = 1 + 4 * len(chunks), 3 * n_chunks - 3
        at = [0, 0]

        def tick():
            at[0] += 1
            while at[1] < total * at[0] / ticks:
                at[1] += 1
                step(steps)
        return tick, steps

    def affine(self, which, layer, j):
        cols = self.m["mod"][:, 2 * layer + which, :]
        return cols[:, (3 * j + 1) * KD:(3 * j + 2) * KD], cols[:, 3 * j * KD:(3 * j + 1) * KD], self.mod_ready[layer]

    def gated_residual(self, x, gate, sums, known):
        m = self.m

        def finish(t, half, ps, done):
            s = slice(half * BANK, (half + 1) * BANK)
            tmp = m["sm"][:, t, :]
            a = self.dve.do(lambda e: e.tensor_tensor(tmp, ps[:], gate[:, s], ALU.mult), done, known,
                            self.freed.get("sm"), self.freed.get(f"sm{t}"))
            sums[t].append(self.dve.do(lambda e: e.scalar_tensor_tensor(out=x[:, t, s], in0=x[:, t, s],
                                                                        scalar=ALPHA_2, in1=tmp, op0=ALU.mult,
                                                                        op1=ALU.add), a))
            self.freed[f"sm{t}"] = sums[t][-1]
            return a
        return finish

    def conditioned_ffn(self, x, ready, which, layer, j, gate, chunks=()):
        d, m = self.dram, self.m
        f = j // 2
        lhs = self.to_lhs(x, ready, (m["xt_hi"], m["xt_lo"]), self.claim("xt"), self.affine(which, layer, j))
        g, b, rows = self.rows(f"ln_{layer}{which}{j}", d["ln_g_2"][layer, j], d["ln_b_2"][layer, j])
        wi = d["ffn_wi_2"][layer, f].rearrange("(k p) n -> p k n", p=P)
        wo = d["ffn_wo_2"][layer, f]

        def up(i):
            c0 = i * F_CHUNK
            return [[(lambda s: whole(BANK)(s)[:, :, 0:F_CHUNK], wi[:, q * KH:(q + 1) * KH, c0:c0 + F_CHUNK]),
                     (lambda s: whole(BANK)(s)[:, :, F_CHUNK:],
                      wi[:, q * KH:(q + 1) * KH, D_FF + c0:D_FF + c0 + F_CHUNK])] for q in range(2)]

        def down(i):
            return [(whole(D), wo[i * F_CHUNK:(i + 1) * F_CHUNK, :].rearrange("(k p) n -> p k n", p=P))]

        def pair(i, t, out, a, g_):
            return lambda e: e.tensor_tensor(out, a, g_, ALU.mult)
        sums = [[] for _ in range(NT)]
        self.combined = None
        n_chunks = D_FF // F_CHUNK
        tick, mods = self.paced(1, chunks, "b2", n_chunks) if chunks else (None, iter(()))
        self.feed_forward(lhs, n_chunks, up, down, pair,
                          self.gated_residual(x, gate, sums, list(self.mod_ready[layer])), tick)
        drain(mods)
        self.release("xt")
        return self.layer_norm(x, sums, g, b, rows)

    def rotate(self, x, heads, t, table, tmp, ready):
        m = self.m
        v = x.rearrange("p (h a s f) -> p h a s f", a=2, s=2, f=AXIS_DIM // 2)
        x1, x2 = v[:, :, :, 0, :], v[:, :, :, 1, :]
        shape = [P, heads, 2, AXIS_DIM // 2]
        cos, sin = [m["rope"][:, t, table + i, :].rearrange("p (a f) -> p a f", a=2).unsqueeze(1).to_broadcast(shape)
                    for i in range(2)]
        half = heads * HEAD_DIM // 2
        t1, t2 = [tmp[:, i * half:(i + 1) * half].rearrange("p (h a f) -> p h a f", h=heads, a=2) for i in range(2)]
        v_ = self.dve.do
        a = v_(lambda e: e.tensor_tensor(t1, x1, sin, ALU.mult), ready, self.tables, self.freed.get("rotated"))
        b = v_(lambda e: e.tensor_tensor(t2, x2, sin, ALU.mult), a)
        c = v_(lambda e: e.tensor_tensor(x1, x1, cos, ALU.mult), b)
        e_ = v_(lambda e: e.tensor_tensor(x2, x2, cos, ALU.mult), c)
        f = v_(lambda e: e.tensor_tensor(x1, x1, t2, ALU.subtract), e_)
        self.freed["rotated"] = v_(lambda e: e.tensor_tensor(x2, x2, t1, ALU.add), f)
        return self.freed["rotated"]

    def keys_values(self, lhs, kv, twice, k_f, free, rotated):
        d, m = self.dram, self.m
        made = {}

        def evacuate(c, t, ps, done):
            made[t] = self.dve.do(lambda e: e.tensor_tensor(kv[:, t, :], ps[:], m["row_b"][:, 0:BANK], ALU.add),
                                  done, free, self.qkv_bias)
            return made[t]
        drain(self.gemm_token(lhs, columns(d["attn_wqkv_2"][0], N_HEADS * HEAD_DIM, 2 * N_KV * HEAD_DIM), evacuate))
        out = []
        n = N_KV * HEAD_DIM
        copied = []
        for t in range(NT):
            a = made[t]
            if rotated:
                a = self.rotate(kv[:, t, 0:n], N_KV, t, 0, m["b2"][:, 2 * BANK:], a)
            src = kv[:, t, 0:n].rearrange("p (g n) -> p g n", g=N_KV)
            dst = twice[:, t * 2 * n:(t + 1) * 2 * n].rearrange("p (g c n) -> p g c n", g=N_KV, c=2)
            for c in range(2):
                copied.append(self.dve.do(lambda e, c=c, src=src, dst=dst: e.tensor_copy(dst[:, :, c, :], src), a,
                                          free))
        for g in range(0, N_KV, 2):
            b, bank_free = self.bank()
            ps = self.ps(b)

            def turn(e, g=g, ps=ps):
                for i in range(2):
                    for t in range(NT):
                        cols = t * 2 * n + (g + i) * P
                        last = e.transpose(ps[:, i * SEQ + t * P:i * SEQ + t * P + P], twice[:, cols:cols + P],
                                           m["ident"][:])
                return last
            turned = self.pe.do(turn, copied, bank_free)
            a = self.act.do(lambda e, g=g, ps=ps: e.activation(k_f[:, g:g + 2, :], ps[:], ACT.Copy), turned, free)
            self.bank_free[b] = a
            out.append(a)
        return [out, copied]

    def window_units(self, q_f, k_f, v_t, kc_f, vc_t, y, ready):
        m = self.m
        n = N_KV * HEAD_DIM
        for h in range(N_HEADS):
            for t in range(NT):
                g = h // GROUP

                def score(u, h=h, t=t, g=g):
                    b, free = self.bank()
                    ps = self.ps(b)
                    rows = slice((h % 2) * HEAD_DIM, (h % 2 + 1) * HEAD_DIM)

                    def issue(e):
                        q = q_f[rows, h // 2, t * P:t * P + P]
                        e.matmul(ps[:, 0:SEQ], q, k_f[rows, g, :], start=True, stop=True)
                        return e.matmul(ps[:, SEQ:], q, kc_f[rows, g, :], start=True, stop=True)
                    return b, self.pe.do(issue, free, ready)

                def soften(u, scored, h=h, t=t):
                    b, done = scored
                    ps = self.ps(b)
                    st = m["st"][:, u % 4, :]
                    ex = m["work"][:, u % 4, :]
                    other = slice(P, 2 * P) if t == 0 else slice(0, P)
                    a = self.dve.do(lambda e: e.tensor_tensor(ps[:, other], ps[:, other], m["window"][:, t, :],
                                                              ALU.add), done, self.tables)
                    a = self.dve.do(lambda e: e.tensor_reduce(st[:, 0:1], ps[:], AX.X, ALU.max, negate=True), a,
                                    self.freed.get(f"st{u % 4}"))
                    a = self.dve.do(lambda e: e.tensor_scalar(st[:, 1:2], st[:, 0:1], m["sinks"][:, 1, h:h + 1],
                                                              None, ALU.min), a, self.sinks)
                    x = self.act.do(lambda e: e.activation(ex, ps[:], ACT.Exp, bias=st[:, 1:2],
                                                           accum_out=st[:, 2:3]), a, self.slot_free[u % 4])
                    self.bank_free[b] = x
                    s = self.act.do(lambda e: e.activation(st[:, 3:4], m["sinks"][:, 0, h:h + 1], ACT.Exp,
                                                           bias=st[:, 1:2]), a)
                    return ex, x, s, st

                def weigh(u, soft):
                    ex, x, s, st = soft
                    r = self.dve.do(lambda e: e.tensor_tensor(st[:, 4:5], st[:, 2:3], st[:, 3:4], ALU.add), s)
                    r = self.dve.do(lambda e: e.reciprocal(st[:, 5:6], st[:, 4:5]), r)
                    return ex, x, 4, r, st

                def write(u, out, mixed, weighed, h=h, t=t):
                    r, st = weighed[3:]
                    return self.act.do(lambda e: e.activation(y[:, t, h * HEAD_DIM:(h + 1) * HEAD_DIM], out,
                                                              ACT.Copy, scale=st[:, 5:6]), mixed, r,
                                       self.claim("b0"))
                cols = slice(n + g * HEAD_DIM, n + (g + 1) * HEAD_DIM)
                values = [v_t[:, k, cols] for k in range(NT)] + [vc_t[:, k, cols] for k in range(NT)]
                yield score, soften, weigh, (values, ready), write

    def second_block(self):
        d, m = self.dram, self.m
        x = self.tok("x")
        mg, b4 = self.tok("mg"), self.tok("b4")

        ctx = self.tok("b3")
        got = self.load("ctx", ctx, d["ctx_2"][0].rearrange("(t p) n -> p t n", p=P), self.claim("b3"))
        columns_1 = [c for c in range(2 * N_MOD) if (c // 2) % 3 < 2]
        rows_1 = [c for c in range(2 * N_MOD) if (c // 2) % 3 == 2]
        c_ready = self.conditioned_ffn(ctx, got, 1, 0, 0, mg[:, 1, :], columns_1[:6])
        lhs = self.to_lhs(ctx, c_ready, (m["xt_hi"], m["xt_lo"]), self.claim("xt"), self.affine(1, 0, 1))
        self.release("b3")
        qkv = d["attn_bqkv_2"][0]
        q_width = N_HEADS * HEAD_DIM
        free = self.freed.get("rows")
        self.qkv_bias = [self.load("bias_kv", m["row_b"][:, 0:BANK], qkv[q_width:].partition_broadcast(P), free)]
        self.sinks = self.load("sink", m["sinks"][:, 0, :], d["attn_sink_2"][0].partition_broadcast(P))
        self.sinks = self.dve.do(lambda e: e.tensor_scalar(m["sinks"][:, 1, :], m["sinks"][:, 0, :], -1.0, None,
                                                           ALU.mult), self.sinks)
        vc_t = m["b3"][:, 0:2 * BANK].rearrange("p (t n) -> p t n", t=NT)
        kc_f = m["b3"][:, 2 * BANK:].rearrange("p (g s) -> p g s", g=N_KV)
        context = self.keys_values(lhs, vc_t, m["b2"][:, 0:2 * BANK], kc_f, self.claim("b2", "b3"), False)
        self.freed["rows"] = self.latest()
        self.release("xt", "b2")

        x_ready = self.conditioned_ffn(x, self.x_ready, 0, 0, 0, mg[:, 0, :], columns_1[6:])

        lhs = self.to_lhs(x, x_ready, (m["xt_hi"], m["xt_lo"]), self.claim("xt"), self.affine(0, 0, 1))
        self.release("mg")
        free = self.freed.get("rows")
        self.qkv_bias = [self.load("bias_kv2", m["row_b"][:, 0:BANK], qkv[q_width:].partition_broadcast(P), free),
                         self.load("bias_q", m["row_g"][:], qkv[0:q_width].partition_broadcast(P), free)]
        v_t = m["b1"][:, 0:2 * BANK].rearrange("p (t n) -> p t n", t=NT)
        k_f = m["b1"][:, 2 * BANK:].rearrange("p (g s) -> p g s", g=N_KV)
        latent = self.keys_values(lhs, v_t, m["b2"][:, 0:2 * BANK], k_f, self.claim("b1", "b2"), True)
        q_t, q_made = self.tok("b0"), [[] for _ in range(NT)]

        def evacuate(c, t, ps, done):
            s = slice(c * BANK, (c + 1) * BANK)
            token = self.dve.do(lambda e: e.tensor_tensor(q_t[:, t, s], ps[:], m["row_g"][:, s], ALU.add), done,
                                self.claim("b0"), self.qkv_bias)
            q_made[t].append(token)
            return token
        drain(self.gemm_token(lhs, columns(d["attn_wqkv_2"][0], 0, q_width), evacuate))
        self.freed["rows"] = self.latest()
        self.release("xt")
        rotated = [self.rotate(q_t[:, t, :], N_HEADS, t, 2, m["b2"][:, 2 * BANK:], q_made[t]) for t in range(NT)]
        q_f, turned_q = self.feat("mg"), []
        for j in range(KD // 2):
            b, free = self.bank()
            ps = self.ps(b)

            def turn(e, j=j, ps=ps):
                for k in range(2):
                    for t in range(NT):
                        last = e.transpose(ps[:, k * SEQ + t * P:k * SEQ + t * P + P],
                                           q_t[:, t, (2 * j + k) * P:(2 * j + k + 1) * P], m["ident"][:])
                return last
            done = self.pe.do(turn, rotated, free)
            a = self.act.do(lambda e, j=j, ps=ps: e.activation(q_f[:, 2 * j:2 * j + 2, :], ps[:], ACT.Copy), done,
                            self.claim("mg"))
            self.bank_free[b] = a
            turned_q.append(a)
        self.release("b0", "b2")
        y = self.tok("b0")
        written = self.softmax_heads(self.window_units(q_f, k_f, v_t, kc_f, vc_t, y, [latent, context, turned_q]),
                                     None)
        self.release("mg", "b1", "b3")
        lhs = self.to_lhs(y, written, (m["xt_hi"], m["xt_lo"]), self.claim("xt"))
        self.release("b0")
        x_ready = self.mixer_out(x, lhs, d["attn_wo_2"][0], b4[:, 0, :], 0)

        x_ready = self.conditioned_ffn(x, x_ready, 0, 0, 2, b4[:, 1, :], rows_1)

        x_ready = self.conditioned_ffn(x, x_ready, 0, 1, 0, mg[:, 0, :])
        x_ready = self.fourier(x, x_ready, mg[:, 1, :])
        self.x_ready = self.conditioned_ffn(x, x_ready, 0, 1, 2, b4[:, 0, :])

    def mixer_out(self, x, lhs, w, gate, layer):
        d = self.dram
        g, b, rows = self.rows(f"mix{layer}", d["ln_g_2"][layer, 1], d["ln_b_2"][layer, 1])
        sums = [[] for _ in range(NT)]
        finish = self.gated_residual(x, gate, sums, self.mod_ready[layer])
        drain(self.gemm_token(lhs, columns(w, 0, D), lambda c, t, ps, done: finish(t, c, ps, done)))
        self.release("xt")
        return self.layer_norm(x, sums, g, b, rows)

    def fourier(self, x, ready, gate):
        d, m = self.dram, self.m
        hi, lo, made = self.to_lhs(x, ready, (m["xt_hi"], m["xt_lo"]), self.claim("xt"), self.affine(0, 1, 1))
        n = self.take([(lambda s: s[:, 0:2 * BANK].rearrange("p (k n) -> p k n", k=2),
                        d["dft"].rearrange("(k p) n -> p k n", p=P))], size=2 * BANK)
        wh, wl = [w[:, 0:2 * BANK].rearrange("p (k n) -> p k n", k=2) for w in self.halves(n)]
        split = []
        free = self.claim("b0", "b1", "b2", "b3")
        for g in range(4):
            for t in range(NT):
                b, bank_free = self.bank()
                ps = self.ps(b)

                def issue(e, g=g, t=t, ps=ps):
                    for k in range(2):
                        for i, (a, w) in enumerate(((hi, wh), (hi, wl), (lo, wh))):
                            last = e.matmul(ps[:], a[:, 2 * g + k, t * P:t * P + P], w[:, k, :],
                                            start=(k == 0 and i == 0), stop=(k == 1 and i == 2))
                    return last
                done = self.pe.do(issue, made, self.full(n), bank_free)
                ph, pl = m["pq_hi"][:, t, g, :], m["pq_lo"][:, t, g, :]
                a = self.act.do(lambda e, ph=ph, ps=ps: e.activation(ph[:, 0:SEQ], ps[:, 0:SEQ], ACT.Copy), done,
                                free)
                a = self.act.do(lambda e, ph=ph, ps=ps: e.activation(ph[:, SEQ:], ps[:, SEQ:], ACT.Copy, scale=-1.0),
                                done)
                v = self.dve.do(lambda e, ph=ph, pl=pl, ps=ps: e.tensor_tensor(
                    pl[:, 0:SEQ], ps[:, 0:SEQ], ph[:, 0:SEQ].bitcast(F32), ALU.subtract), a, free)
                v = self.dve.do(lambda e, ph=ph, pl=pl, ps=ps: e.scalar_tensor_tensor(
                    out=pl[:, SEQ:], in0=ps[:, SEQ:], scalar=-1.0, in1=ph[:, SEQ:].bitcast(F32), op0=ALU.mult,
                    op1=ALU.subtract), a)
                self.bank_free[b] = v
                split.append([a, v])
        first_done = done
        out = []
        for f in range(0, KD, 2):
            b, bank_free = self.bank()
            ps = self.ps(b)

            def issue(e, f=f, ps=ps):
                for i in range(2):
                    g, c0 = (f + i) // 2, ((f + i) % 2) * P
                    terms = [(part, k) for part in range(2) for k in range(NT)]
                    for n_, (part, k) in enumerate(terms):
                        cols = slice(part * SEQ + c0, part * SEQ + c0 + P)
                        w = slice(part * SEQ, (part + 1) * SEQ)
                        ph, pl = m["pq_hi"][:, k, g, cols], m["pq_lo"][:, k, g, cols]
                        for j, (a, c) in enumerate(((ph, wh), (ph, wl), (pl, wh))):
                            last = e.matmul(ps[:, i * SEQ:(i + 1) * SEQ], a, c[:, k, w],
                                            start=(n_ == 0 and j == 0), stop=(n_ == len(terms) - 1 and j == 2))
                return last
            done = self.pe.do(issue, split, bank_free)
            scale = 1.0 / SEQ
            h, l = hi[:, f:f + 2, :], lo[:, f:f + 2, :]
            a = self.act.do(lambda e, h=h, ps=ps: e.activation(h, ps[:], ACT.Copy, scale=scale), done, first_done)
            v = self.dve.do(lambda e, h=h, l=l, ps=ps: e.scalar_tensor_tensor(
                out=l, in0=ps[:], scalar=scale, in1=h.bitcast(F32), op0=ALU.mult, op1=ALU.subtract), a, first_done)
            self.bank_free[b] = v
            out += [a, v]
        self.done_with(n, done)
        self.release("b0", "b1", "b2", "b3")
        return self.mixer_out(x, (hi, lo, out), d["fourier_wo_2"][0], gate, 1)

    def end(self):
        x = self.tok("x")
        self.stores = [self.load("out", self.dram["out"][0].rearrange("(t p) n -> p t n", p=P), x, self.x_ready,
                                 queue=self.sync)]
        self.sync.wait(self.stores)

    def build(self):
        self.combined = self.mod_ready = self.junk_free = None
        self.begin()
        self.first_block()
        self.second_block()
        self.end()


def build_program(nc, dram):
    with ExitStack() as ctx:
        m = {}

        def sb(name, shape, dt=F32, to=None):
            m[name] = (to or ctx).enter_context(nc.sbuf_tensor(name, shape, dt))
        sb("raw", [P, RAW_SLOTS, PIECE])
        sb("hi", [P, SPLIT_SLOTS, PIECE], F32R)
        sb("lo", [P, SPLIT_SLOTS, PIECE], F32R)
        sb("x", [P, NT * D])
        sb("xt_hi", [P, KD, SEQ], F32R)
        sb("xt_lo", [P, KD, SEQ], F32R)
        sb("mg", [P, NT * D])
        for n in ("row_g", "row_b", "row_c"):
            sb(n, [P, D])
        sb("work", [P, 4, BANK])
        m["sm"], m["ex"] = m["work"][:, 0:2, :], m["work"][:, 2:4, :]
        sb("at", [P, 2, BANK])
        sb("ident", [P, P])
        sb("ones", [P, P])
        sb("dist", [P, SEQ])
        sb("decay", [P, RET_HEADS * 2 * P])
        sb("window", [P, 2, P])
        sb("rope", [P, NT, 4, AXIS_DIM])
        sb("index", [P, N_GROUPS])
        sb("st", [P, 4, 16])
        sb("unit", [P, 16])
        sb("junk", [P, P])
        sb("lam", [P, 8])
        sb("da_g", [P, P])
        sb("bn", [P, NT, 2, 6])
        sb("mv", [P, NT, 2])
        sb("gn", [P, NT * RET_HEADS, 2])
        sb("rstd", [P, 8])
        sb("nb", [P, 8])
        sb("r_hi", [P, KD, 20], F32R)
        sb("r_lo", [P, KD, 20], F32R)
        sb("r_bias", [P, 20])
        sb("route", [P, NT, 52])
        sb("combine", [P, NT, N_EXPERTS])
        sb("cvec", [P, 2, KD])
        sb("mod", [P, 3, N_MOD * KD])
        sb("sinks", [P, 2, N_HEADS])
        with ExitStack() as plain:
            for n in ("b0", "b1", "b2", "b3", "b4"):
                sb(n, [P, NT * D], to=plain)
        with ExitStack() as halves:
            sb("yt_hi", [P, KD, SEQ], F32R, to=halves)
            sb("yt_lo", [P, KD, SEQ], F32R, to=halves)
        with ExitStack() as halves:
            sb("ht_hi", [P, 2, 2, SEQ], F32R, to=halves)
            sb("ht_lo", [P, 2, 2, SEQ], F32R, to=halves)
        with ExitStack() as halves:
            sb("pq_hi", [P, NT, 4, BANK], F32R, to=halves)
            sb("pq_lo", [P, NT, 4, BANK], F32R, to=halves)
        m["psum"] = [ctx.enter_context(nc.psum_tensor(f"bank{i}", [P, BANK], F32)) for i in range(8)]
        first = Blocks(dram, m, None)
        first.build()
        program = Blocks(dram, m, first.taken)
        program.build()
        sems = {n: ctx.enter_context(nc.semaphore(n)) for n in sorted(program.sems)}
        block = ctx.enter_context(nc.Block())

        @block.sync
        def _(e):
            program.sync.run(e, sems)

        @block.gpsimd
        def _(e):
            program.pool.run(e, sems)

        @block.scalar
        def _(e):
            program.act.run(e, sems)

        @block.vector
        def _(e):
            program.dve.run(e, sems)

        @block.tensor
        def _(e):
            program.pe.run(e, sems)


def kernel(**inputs):
    import concourse.bacc as bacc
    from concourse.bass_utils import run_bass_kernel_spmd
    arrays = {n: np.ascontiguousarray(a) for n, a in inputs.items()}
    arrays.update(constants())
    nc = bacc.Bacc("TRN2", target_bir_lowering=False, num_devices=1)
    dram = {n: nc.dram_tensor(f"in_{n}", a.shape, F32, kind="ExternalInput").ap() for n, a in arrays.items()}
    dram["out"] = nc.dram_tensor("out", (1, SEQ, D), F32, kind="ExternalOutput").ap()
    build_program(nc, dram)
    r = run_bass_kernel_spmd(nc, [{f"in_{n}": a for n, a in arrays.items()}], core_ids=[0])
    return r.results[0]["out"]
```

```python
from contextlib import ExitStack

import numpy as np

import concourse.bass as bass
from concourse import mybir

F32 = mybir.dt.float32
F32R = mybir.dt.float32r
ALU = mybir.AluOpType
ACT = mybir.ActivationFunctionType
AX = mybir.AxisListType

P = 128
BANK = 512
PIECE = 2048
RAW_SLOTS = 4
SPLIT_SLOTS = 4
SEQ = 256
NT = SEQ // P
D = 1024
KD = D // P
KH = KD // 2
EPS = 1e-5
MASKED = 1e30

DA_HEADS, DA_DK, DA_DV = 8, 64, 128
RET_HEADS, RET_DK, RET_DV = 4, 128, 256
MEM_HEADS, MEM_DH = 4, 256
N_GROUPS, PER_GROUP, N_EXPERTS = 4, 4, 16
D_FF_EXPERT = 512
LAMBDA_INIT = 0.2
ALPHA_1 = 2.0 ** 0.25
ALPHA_2 = 4.0 ** 0.25
N_HEADS, N_KV, HEAD_DIM, GROUP = 16, 4, 64, 4
WINDOW = 128
D_FF = 2816
F_CHUNK = 256
GRID_W, ROPE_BASE, AXIS_DIM = 64, 10000.0, 32
N_MOD = 9


def constants():
    q = np.arange(P, dtype=np.float64)[:, None]
    dist = (P + q) - np.arange(SEQ)[None, :]
    dist = np.where(dist >= 0, dist, MASKED)
    log_g = np.log(1.0 - 2.0 ** (-5.0 - np.arange(RET_HEADS)))
    k = np.arange(P)[:, None]
    qq = np.arange(P)[None, :]
    decay = []
    for h in range(RET_HEADS):
        diagonal = np.where(qq >= k, np.exp((qq - k) * log_g[h]), 0.0)
        behind = np.exp((P + qq - k) * log_g[h])
        decay.append(np.stack([diagonal, behind], axis=1))
    decay = np.stack(decay, axis=1) * RET_DK ** -0.5
    key = np.arange(P)[None, :]
    window = np.stack([np.where(key <= q, 0.0, -MASKED), np.where(key >= q, 0.0, -MASKED)], axis=1)
    tok = np.arange(SEQ)
    inv = ROPE_BASE ** (-np.arange(0, AXIS_DIM, 2) / AXIS_DIM)
    inv = inv.astype(np.float32)
    ang = np.concatenate([(tok // GRID_W)[:, None].astype(np.float32) * inv,
                          (tok % GRID_W)[:, None].astype(np.float32) * inv], axis=-1)
    cos, sin = np.cos(ang), np.sin(ang)
    rope = np.stack([cos, sin, cos * HEAD_DIM ** -0.5, sin * HEAD_DIM ** -0.5], axis=1)
    turn = 2.0 * np.pi * ((tok[:, None] * tok[None, :]) % SEQ) / SEQ
    dft = np.concatenate([np.cos(turn), np.sin(turn)], axis=1)
    out = {"dist": dist, "decay": decay, "window": window, "rope": rope, "dft": dft,
           "ident": np.eye(P), "index": np.tile(np.arange(N_GROUPS), (P, 1)),
           "r_fold": np.tile(np.eye(N_GROUPS + N_EXPERTS), (2, 1))}
    return {n: np.ascontiguousarray(a, dtype=np.float32) for n, a in out.items()}


class Queue:

    def __init__(self, name):
        self.name, self.count, self.steps, self.seen = name, 0, [], {}

    def wait(self, *after):
        last = {}
        for sem, value in flat(after):
            last[sem] = max(last.get(sem, 0), value)
        for sem, value in last.items():
            if self.seen.get(sem, 0) < value:
                self.seen[sem] = value
                self.steps.append(("wait", sem, value))

    def do(self, issue, *after):
        self.wait(*after)
        self.count += 1
        self.steps.append(("do", issue, self.name))
        return (self.name, self.count)

    def run(self, engine, sems):
        for kind, a, b in self.steps:
            if kind == "wait":
                engine.wait_ge(sems[a], b)
            elif kind == "do":
                a(engine).then_inc(sems[b], 1)
            else:
                a(engine).then_inc(sems[b], 16)


def flat(tokens):
    for t in tokens:
        if t is None:
            continue
        if isinstance(t, list):
            yield from flat(t)
        else:
            yield t


class Banks(dict):

    def __setitem__(self, bank, token):
        if token is not None:
            super().__setitem__(bank, token)
            self.held.discard(bank)


class Program:
    def __init__(self, dram, mem, plan):
        self.dram, self.m, self.plan = dram, mem, plan
        self.pe, self.act, self.dve = Queue("pe"), Queue("act"), Queue("dve")
        self.sync, self.pool = Queue("sync"), Queue("pool")
        self.sems = {"pe", "act", "dve"}
        self.taken, self.loaded, self.split = [], 0, 0
        self.raw_full, self.raw_free = {}, {}
        self.half_full, self.half_free = {}, {}
        self.raw_count = [0] * RAW_SLOTS
        self.is_split = [p[1] for p in plan or []]
        self.mod_count = [0, 0]
        self.split_slot = list(np.cumsum([0] + self.is_split)[:-1])
        self.bank_free, self.held = Banks(), set()
        self.bank_free.held = self.held
        self.ring, self.ring_at = list(range(8)), 0
        self.freed = {}
        self.stores = []
        self.hold = False

    def load(self, name, dst, src, *after, queue=None):
        q = queue or self.pool
        q.wait(*after)
        sem = f"ld_{name}"
        assert sem not in self.sems
        self.sems.add(sem)
        q.steps.append(("dma", lambda e: e.dma_start(dst, src), sem))
        return (sem, 16)

    def take(self, sources, split=True, size=PIECE):
        n = len(self.taken)
        self.taken.append((sources, split, size))
        if self.plan is None:
            return n
        self.run_ahead()
        return n

    def run_ahead(self):
        plan = self.plan
        while True:
            moved = False
            n = self.loaded
            if n < len(plan) and (n < RAW_SLOTS or (n - RAW_SLOTS) in self.raw_free):
                slot = n % RAW_SLOTS
                if n >= RAW_SLOTS:
                    self.sync.wait(self.raw_free[n - RAW_SLOTS])
                sem = f"raw{slot}"
                self.sems.add(sem)
                for view, src in plan[n][0]:
                    dst = view(self.m["raw"][:, slot, :])
                    self.sync.steps.append(("dma", lambda e, dst=dst, src=src: e.dma_start(dst, src), sem))
                    self.raw_count[slot] += 16
                self.raw_full[n] = (sem, self.raw_count[slot])
                self.loaded += 1
                moved = True
            n = self.split
            if n < self.loaded:
                if not self.is_split[n]:
                    self.split += 1
                    moved = True
                elif not self.hold or n < len(self.taken):
                    s = self.split_slot[n]
                    if s < SPLIT_SLOTS or (s - SPLIT_SLOTS) in self.half_free:
                        self.split_piece(n, s)
                        self.split += 1
                        moved = True
            if not moved:
                return

    def split_piece(self, n, s):
        raw = self.m["raw"][:, n % RAW_SLOTS, :]
        hi, lo = self.m["hi"][:, s % SPLIT_SLOTS, :], self.m["lo"][:, s % SPLIT_SLOTS, :]
        used = self.plan[n][2]
        if used < PIECE:
            raw, hi, lo = raw[:, 0:used], hi[:, 0:used], lo[:, 0:used]
        free = self.half_free.get(s - SPLIT_SLOTS)
        a = self.act.do(lambda e: e.activation(hi, raw, ACT.Copy), self.raw_full[n], free)
        b = self.dve.do(lambda e: e.tensor_tensor(lo, raw, hi.bitcast(F32), ALU.subtract), a)
        self.half_full[n] = [a, b]
        self.raw_free[n] = b

    def halves(self, n):
        if self.plan is None:
            s = 0
        else:
            s = self.split_slot[n] % SPLIT_SLOTS
        return self.m["hi"][:, s, :], self.m["lo"][:, s, :]

    def full(self, n):
        return [] if self.plan is None else self.half_full[n]

    def done_with(self, n, token):
        if self.plan is not None:
            self.half_free[self.split_slot[n]] = token

    def bank(self):
        b = self.ring[self.ring_at % len(self.ring)]
        while b in self.held:
            self.ring_at += 1
            b = self.ring[self.ring_at % len(self.ring)]
        self.ring_at += 1
        self.held.add(b)
        return b, self.bank_free.get(b)

    def use_ring(self, banks):
        self.ring, self.ring_at = list(banks), 0

    def ps(self, b):
        return self.m["psum"][b]

    def gemm_token(self, lhs, weights, evacuate):
        hi, lo, ready = lhs
        for c, (first, second) in enumerate(weights):
            banks = [self.bank() for _ in range(NT)]
            for part, sources in enumerate((first, second)):
                n = self.take(sources)
                wh, wl = self.halves(n)
                wh = wh.rearrange("p (k n) -> p k n", k=KH)
                wl = wl.rearrange("p (k n) -> p k n", k=KH)
                frees = [f for _, f in banks] if part == 0 else None

                def issue(e, tiles, part=part, wh=wh, wl=wl, banks=banks):
                    for t in tiles:
                        for k in range(KH):
                            kk = part * KH + k
                            tok = slice(t * P, t * P + P)
                            for i, (a, b) in enumerate(((hi, wh), (hi, wl), (lo, wh))):
                                last = e.matmul(self.ps(banks[t][0])[:], a[:, kk, tok], b[:, k, :],
                                                start=(kk == 0 and i == 0), stop=(kk == KD - 1 and i == 2))
                    return last
                known = [self.full(n), ready[2 * part:2 * part + 2], frees]
                if part == 0:
                    done = [self.pe.do(lambda e, issue=issue: issue(e, range(NT)), known)]
                else:
                    done = [self.pe.do(lambda e, t=t, issue=issue: issue(e, [t]), known) for t in range(NT)]
                self.done_with(n, done[-1])
                yield
            for t in range(NT):
                self.bank_free[banks[t][0]] = evacuate(c, t, self.ps(banks[t][0]), done[t])

    def gemm_feature(self, lhs, weights, evacuate, bias=None):
        hi, lo, ready = lhs
        for c, (first, second) in enumerate(weights):
            banks = [self.bank() for _ in range(2)]
            n0 = self.take(first)
            yield
            n1 = self.take(second)
            parts = [[x.rearrange("p (k n) -> p k n", k=KH) for x in self.halves(n)] for n in (n0, n1)]

            def issue(e, m, parts=parts, banks=banks):
                out = self.ps(banks[m // 2][0])[:, (m % 2) * SEQ:(m % 2) * SEQ + SEQ]
                for kk in range(KD):
                    wh, wl = parts[kk // KH]
                    cols = slice(m * P, m * P + P)
                    for i, (a, b) in enumerate(((hi, wh), (hi, wl), (lo, wh))):
                        last = e.matmul(out, b[:, kk % KH, cols], a[:, kk, :], start=(kk == 0 and i == 0),
                                        stop=(kk == KD - 1 and i == 2))
                return last
            for m in range(4):
                done = self.pe.do(lambda e, m=m, issue=issue: issue(e, m), self.full(n0), self.full(n1), ready,
                                  [f for _, f in banks])
                if m % 2:
                    b = banks[m // 2][0]
                    self.bank_free[b] = evacuate(c, m // 2, self.ps(b), done)
            self.done_with(n0, done)
            self.done_with(n1, done)
            yield

    def to_lhs(self, src, ready, dst, free, affine=None):
        hi, lo = dst
        m = self.m
        by_tile = isinstance(ready, list) and len(ready) == NT
        banks = [self.bank() for _ in range(KD // 2)]
        turned = [None] * len(banks)
        for t in range(NT):
            for j, (b, bank_free) in enumerate(banks):
                ps = self.ps(b)

                def turn(e, j=j, t=t, ps=ps):
                    for k in range(2):
                        kk = 2 * j + k
                        last = e.transpose(ps[:, k * SEQ + t * P:k * SEQ + t * P + P],
                                           src[:, t, kk * P:kk * P + P], m["ident"][:])
                    return last
                turned[j] = self.pe.do(turn, ready[t] if by_tile else ready, self.const, bank_free)
        self.turned = turned[-1]
        steps = [[] for _ in banks]
        halves = [(hi[:, 2 * j:2 * j + 2, :], lo[:, 2 * j:2 * j + 2, :]) for j in range(len(banks))]

        def lower(j, value, a):
            h, l = halves[j]
            d = self.dve.do(lambda e: e.tensor_tensor(l, value, h.bitcast(F32), ALU.subtract), a, free)
            steps[j] += [a, d]
            return d
        scratch_free = self.claim("ex")
        scaled = []
        for j, (b, _) in enumerate(banks):
            ps = self.ps(b)
            h, l = halves[j]
            if affine is None:
                a = self.act.do(lambda e, h=h, ps=ps: e.activation(h, ps[:], ACT.Copy), turned[j], free)
                self.bank_free[b] = lower(j, ps[:], a)
                continue
            scale, shift, known = affine
            tmp = m["ex"][:, j % 2, :]
            for k in range(2):
                kk = 2 * j + k
                c = slice(k * SEQ, k * SEQ + SEQ)
                after = [turned[j], known, scratch_free, steps[j - 2] if j >= 2 else None]
                if j % 2:
                    at = self.act.do(lambda e, c=c, kk=kk, tmp=tmp, ps=ps: e.activation(
                        tmp[:, c], ps[:, c], ACT.Identity, bias=shift[:, kk:kk + 1], scale=scale[:, kk:kk + 1]),
                        after)
                else:
                    at = self.dve.do(lambda e, c=c, kk=kk, tmp=tmp, ps=ps: e.tensor_scalar(
                        tmp[:, c], ps[:, c], scale[:, kk:kk + 1], shift[:, kk:kk + 1], ALU.mult, ALU.add), after)
            self.bank_free[b] = at
            scaled.append((j, h, tmp, at))
            if j % 2 == 0:
                continue
            for j_, h_, tmp_, at_ in scaled:
                a = self.act.do(lambda e, h=h_, tmp=tmp_: e.activation(h, tmp, ACT.Copy), at_, free)
                lower(j_, tmp_, a)
            scaled = []
        if affine is not None:
            self.freed["ex"] = steps
        return (hi, lo, steps)

    def latest(self):
        return [(q.name, q.count) for q in (self.pe, self.act, self.dve) if q.count]

    def inverse_root(self, x, eps, scratch, after):
        a = self.dve.do(lambda e: e.tensor_scalar(scratch, x, eps, None, ALU.add), after)
        b = self.act.do(lambda e: e.activation(scratch, scratch, ACT.Sqrt), a)
        return self.dve.do(lambda e: e.reciprocal(scratch, scratch), b)

    def warm(self, func):
        cell = self.m["warm"]
        self.freed["warm"] = self.act.do(lambda e: e.activation(cell[:, 1:2], cell[:, 0:1], func), self.ones_small,
                                         self.freed.get("warm"))

    def norm_half(self, norm, t, half, ready):
        m = self.m
        x = norm["x"]
        norm["stats"][t].append(self.dve.do(
            lambda e: e.bn_stats(m["bn"][:, t, half, :], x[:, t, half * BANK:(half + 1) * BANK]),
            ready, self.freed.get(f"norm{t}")))
        self.norm_finish(norm)
        if len(norm["stats"][t]) < 2:
            return
        agg = self.dve.do(lambda e: e.bn_aggr(m["mv"][:, t, :], m["bn"][:, t, :, :]), norm["stats"][t])
        rstd = m["rstd"][:, t:t + 1]
        a = self.dve.do(lambda e: e.tensor_scalar(rstd, m["mv"][:, t, 1:2], EPS, None, ALU.add), agg)
        norm["waiting"] = (t, self.act.do(lambda e: e.activation(rstd, rstd, ACT.Sqrt), a))

    def norm_finish(self, norm):
        if norm["waiting"] is None:
            return
        t, root = norm["waiting"]
        norm["waiting"] = None
        m = self.m
        x = norm["x"]
        rstd, nb = m["rstd"][:, t:t + 1], m["nb"][:, t:t + 1]
        r = self.dve.do(lambda e: e.reciprocal(rstd, rstd), root)
        n = self.dve.do(lambda e: e.scalar_tensor_tensor(out=nb, in0=m["mv"][:, t, 0:1], scalar=-1.0, in1=rstd,
                                                         op0=ALU.mult, op1=ALU.mult), r)
        v = None
        first = 0
        if t == NT - 1:
            first = BANK
            v = self.dve.do(lambda e: e.tensor_scalar(x[:, t, 0:first], x[:, t, 0:first], rstd, nb, ALU.mult,
                                                      ALU.add), n)
        a = self.act.do(lambda e: e.activation(x[:, t, first:], x[:, t, first:], ACT.Identity, bias=nb, scale=rstd),
                        n)
        self.freed[f"norm{t}"] = [v, a]
        norm["centred"].append([v, a])

    def new_norm(self, x):
        return {"x": x, "stats": [[] for _ in range(NT)], "waiting": None, "centred": []}

    def gain(self, x, centred, g, b, rows, after=None):
        out = []
        for t in range(NT):
            n = self.dve.do(lambda e, t=t: e.tensor_tensor(x[:, t, :], x[:, t, :], g, ALU.mult), centred[t], rows,
                            after)
            out.append(self.dve.do(lambda e, t=t: e.tensor_tensor(x[:, t, :], x[:, t, :], b, ALU.add), n))
        self.freed["rows"] = out
        return out

    def rows(self, name, g, b):
        m = self.m
        free = self.freed.get("rows")
        a = self.load(name + "_g", m["row_g"][:], g.partition_broadcast(P), free)
        c = self.load(name + "_b", m["row_b"][:], b.partition_broadcast(P), free)
        return m["row_g"][:], m["row_b"][:], [a, c]


def whole(n):
    return lambda slot: slot.rearrange("p (k n) -> p k n", n=n)


def column_pieces(w, c0):
    v = w.rearrange("(k p) n -> p k n", p=P)
    return [[(whole(BANK), v[:, part * KH:(part + 1) * KH, c0:c0 + BANK])] for part in range(2)]


def columns(w, c0, n):
    return [column_pieces(w, c0 + c * BANK) for c in range(n // BANK)]


def drain(steps):
    for _ in steps:
        pass


def step(steps):
    next(steps, None)


def mover(queue):
    if queue.name == "act":
        return lambda dst, src, *after: queue.do(lambda e: e.activation(dst, src, ACT.Copy), *after)
    return lambda dst, src, *after: queue.do(lambda e: e.tensor_copy(dst, src), *after)


class Blocks(Program):

    def claim(self, *names):
        return [self.freed.get(n) for n in names]

    def release(self, *names):
        for n in names:
            self.freed[n] = self.latest()

    def tok(self, name):
        return self.m[name][:].rearrange("p (t n) -> p t n", t=NT)

    def feat(self, name, tokens=SEQ):
        return self.m[name][:].rearrange("p (k s) -> p k s", s=tokens)

    def begin(self):
        d, m = self.dram, self.m
        self.const = self.load("ident", m["ident"][:], d["ident"], queue=self.act)
        mem = self.load("mem", self.tok("b4"), d["mem"][0].rearrange("(t p) n -> p t n", p=P), queue=self.act)
        self.x_in = self.load("x", self.tok("x"), d["x"][0].rearrange("(t p) n -> p t n", p=P), queue=self.act)
        self.mem_in = mem
        self.ones = self.dve.do(lambda e: e.memset(m["ones"][:], 1.0))
        self.ones_small = self.dve.do(lambda e: e.memset(m["warm"][:], 1.0))
        self.tables = [self.load("dist", m["dist"][:], d["dist"]),
                       self.load("decay", m["decay"][:], d["decay"].rearrange("p h w n -> p (h w n)")),
                       self.load("window", m["window"][:], d["window"]),
                       self.load("rope", m["rope"][:], d["rope"].rearrange("(t p) w n -> p t w n", p=P)),
                       self.load("index", m["index"][:], d["index"]),
                       self.load("r_fold", m["r_fold"][0:2 * (N_GROUPS + N_EXPERTS), :], d["r_fold"])]

    def first_block(self):
        d, m = self.dram, self.m
        w_in, w_kv = d["w_in"][0], d["w_mem_kv"][0]
        x = self.tok("x")
        mem_t = self.to_lhs(self.tok("b4"), [self.mem_in], (m["yt_hi"], m["yt_lo"]), None)
        self.release("b4")

        act_move, dve_move = mover(self.act), mover(self.dve)
        k_f, v_t, q_f = self.feat("b2"), self.tok("b3"), self.feat("b0")
        made = {"k": [], "v": [], "q": [], "gate": []}

        def to_feat(dst, key, free):
            def evacuate(c, pair, ps, done):
                f = 4 * c + 2 * pair
                token = act_move(dst[:, f:f + 2, :], ps[:], done, free)
                made[key].append(token)
                return token
            return evacuate

        def to_tok(dst, key, free, func=ACT.Copy):
            def evacuate(c, t, ps, done):
                token = self.act.do(lambda e: e.activation(dst[:, t, c * BANK:(c + 1) * BANK], ps[:], func),
                                    done, free)
                made[key].append(token)
                return token
            return evacuate
        drain(self.gemm_token(mem_t, columns(w_kv, D, D), to_tok(v_t, "v", self.claim("b3"))))
        self.xt = self.to_lhs(x, [self.x_in], (m["xt_hi"], m["xt_lo"]), None)
        drain(self.gemm_feature(mem_t, columns(w_kv, 0, D), to_feat(k_f, "k", self.claim("b2"))))
        self.release("b0", "b1")
        drain(self.gemm_feature(self.xt, columns(w_in, 6 * D, D), to_feat(q_f, "q", self.claim("b0"))))
        y = self.tok("b4")
        free = self.claim("b4")
        written = self.softmax_heads(self.memory_units(q_f, k_f, v_t, y, made, free), None)
        self.release("b0", "b1", "b2", "b3")
        drain(self.gates(2, "b2"))
        yt = self.to_lhs(y, [written], (m["yt_hi"], m["yt_lo"]), self.claim("b0", "b1"))
        self.release("b4")
        self.branch(2, yt, "b2", first=True)

        made.update({"k": [], "v": [], "q": []})
        lam = self.lambda_full()
        q_f, k_f, v_t, y = self.feat("b0"), self.feat("b1"), self.tok("b2"), self.tok("b3")
        drain(self.gemm_feature(self.xt, columns(w_in, 0, D), to_feat(q_f, "q", self.claim("b0"))))
        drain(self.gemm_feature(self.xt, columns(w_in, D, D), to_feat(k_f, "k", self.claim("b1"))))
        drain(self.gemm_token(self.xt, columns(w_in, 2 * D, D), to_tok(v_t, "v", self.claim("b2"))))
        filler = self.gates(0, "b4")
        written = self.softmax_heads(self.differential_units(q_f, k_f, v_t, y, made, self.claim("b3"), lam), filler)
        written = self.differential_norm(y, written)
        self.release("b0", "b1", "b2", "junk")
        drain(filler)
        yt = self.to_lhs(y, [written], (m["yt_hi"], m["yt_lo"]), self.claim("b0", "b1"))
        self.release("b3")
        self.branch(0, yt, "b4", first=False)

        made.update({"k": [], "v": [], "q": []})
        qk, v_t, y = self.feat("b0"), self.tok("b1"), self.tok("b3")
        gate_silu = self.tok("b2")
        g, b, rows = self.rows("gn", d["ret_gn_g"][0], d["ret_gn_b"][0])
        drain(self.gemm_feature(self.xt, columns(w_in, 3 * D, D), to_feat(qk, "q", self.claim("b0"))))
        drain(self.gemm_token(self.xt, columns(w_in, 4 * D, D), to_tok(v_t, "v", self.claim("b1"))))
        filler = self.then(self.gemm_token(self.xt, columns(w_in, 5 * D, D),
                                           to_tok(gate_silu, "gate", self.claim("b2"), ACT.Silu)),
                           self.gates(1, "b4"))
        written = self.retention(qk, v_t, y, made, self.claim("b3"), filler)
        step(filler)
        written = self.retention_norm(y, written, gate_silu, made["gate"], g, b, rows)
        drain(filler)
        self.release("b0", "b1", "b2", "xt")
        yt = self.to_lhs(y, written, (m["yt_hi"], m["yt_lo"]), self.claim("b0", "b1"))
        self.release("b3")
        self.branch(1, yt, "b4", first=False)

        g, b, rows = self.rows("ln1", d["ln1_g"][0], d["ln1_b"][0])
        self.warm(ACT.Sqrt)
        self.turn_rows()
        self.router_weights()
        yt = self.to_lhs(self.tok("mg"), [self.merged], (m["yt_hi"], m["yt_lo"]), self.claim("b0", "b1"))
        self.release("mg")
        add = self.residual(x)
        drain(self.gemm_token(yt, columns(d["w_o"][0], 0, D), lambda c, t, ps, done: add(t, c, ps, done)))
        self.release("b0", "b1")
        centred, _ = self.finish_norm(add.norm, g, b, rows)
        self.xt = self.to_lhs(x, centred, (m["xt_hi"], m["xt_lo"]), self.claim("xt"), self.gb_affine("ln1"))
        x_ready = self.gain(x, centred, g, b, rows, self.turned)
        self.warm(ACT.Silu)
        self.experts(x, x_ready)

    def residual(self, x):
        def add(t, c, ps, done):
            s = slice(c * BANK, (c + 1) * BANK)
            token = self.dve.do(lambda e: e.scalar_tensor_tensor(out=x[:, t, s], in0=x[:, t, s], scalar=ALPHA_1,
                                                                 in1=ps[:], op0=ALU.mult, op1=ALU.add), done,
                                self.x_full)
            self.norm_half(add.norm, t, c, token)
            return token
        add.norm = self.new_norm(x)
        return add

    def turn_rows(self):
        d, m = self.dram, self.m
        parts = [("c", d["c_2"][0]), ("c_ctx", d["c_ctx_2"]), ("lng", d["ln_g_2"].rearrange("a b n -> (a b n)")),
                 ("lnb", d["ln_b_2"].rearrange("a b n -> (a b n)")), ("g2", d["ln2_g"][0]), ("b2", d["ln2_b"][0])]
        late = [("g1", d["ln1_g"][0]), ("b1", d["ln1_b"][0])]
        free = self.claim("junk")
        self.column_of = {}
        for tile, rows_of, width in ((m["junk"], parts, P), (m["da_g"], late, 2 * KD)):
            at, got = 0, []
            for name, src in rows_of:
                n = src.shape[0] // P
                got.append(self.load(f"row_{name}", tile[at:at + n, :], src.rearrange("(k p) -> k p", p=P), free))
                self.column_of[name] = (tile is m["junk"], at)
                at += n
            b, bank_free = self.bank()
            ps = self.ps(b)
            out = m["cols"] if tile is m["junk"] else m["cols1"]
            done = self.pe.do(lambda e, tile=tile, ps=ps, width=width: e.transpose(
                ps[:, 0:width], tile[0:width, :], m["ident"][0:width, 0:width]), got, bank_free, self.const)
            a = self.dve.do(lambda e, ps=ps, out=out, width=width: e.tensor_copy(out[:], ps[:, 0:width]), done)
            self.bank_free[b] = a
        self.cols_ready = a
        self.c_ready = self.act.do(lambda e: e.activation(m["cvec"][:].rearrange("p v k -> p (v k)"),
                                                          m["cols"][:, 0:2 * KD], ACT.Silu), a)

    def gb(self, name):
        if name == "ln1":
            c = self.m["cols1"]
            return c[:, 0:KD], c[:, KD:2 * KD]
        c = self.m["cols"]
        if name == "ln2":
            return c[:, 14 * KD:15 * KD], c[:, 15 * KD:16 * KD]
        at = 2 + 3 * name[0] + name[1]
        return c[:, at * KD:(at + 1) * KD], c[:, (at + 6) * KD:(at + 7) * KD]

    def gb_affine(self, name):
        return (*self.gb(name), [self.cols_ready])

    def then(self, *parts):
        for p in parts:
            yield from p

    def gates(self, n, name):
        d, m = self.dram, self.m
        dst, free = self.tok(name), self.claim(name)
        row = self.load(f"gate{n}", m["row_c"][:], d["b_gate"][0, n * D:(n + 1) * D].partition_broadcast(P),
                        self.freed.get("row_c"))
        self.logits = []

        def evacuate(c, t, ps, done):
            s = slice(c * BANK, (c + 1) * BANK)
            token = self.dve.do(lambda e: e.tensor_tensor(dst[:, t, s], ps[:], m["row_c"][:, s], ALU.add),
                                done, free, row)
            self.logits.append(token)
            self.freed["row_c"] = token
            return token
        yield from self.gemm_token(self.xt, columns(d["w_in"][0], 7 * D + n * D, D), evacuate)

    def branch(self, n, yt, gate_name, first):
        m = self.m
        gate, merged = self.tok(gate_name), self.tok("mg")
        known = [self.act.do(lambda e, t=t: e.activation(gate[:, t, :], gate[:, t, :], ACT.Sigmoid), self.logits)
                 for t in range(NT)]
        out = []

        def evacuate(c, t, ps, done):
            s = slice(c * BANK, (c + 1) * BANK)
            if first:
                token = self.dve.do(lambda e: e.tensor_tensor(merged[:, t, s], ps[:], gate[:, t, s], ALU.mult),
                                    done, known)
                out.append(token)
                return token
            tmp = m["sm"][:, t, :]
            token = self.dve.do(lambda e: e.tensor_tensor(tmp, ps[:], gate[:, t, s], ALU.mult), done, known,
                                self.claim("sm"))
            out.append(self.dve.do(lambda e: e.tensor_tensor(merged[:, t, s], merged[:, t, s], tmp, ALU.add),
                                   token, self.merged))
            return token
        drain(self.gemm_token(yt, columns(self.dram["w_branch"][0, n], 0, D), evacuate))
        self.merged = out
        self.freed["sm"] = out
        self.release("b0", "b1", gate_name)

    def softmax_heads(self, units, filler, at_halves=None):
        m = self.m
        units = list(units)
        n = len(units)
        base = self.claim("sm", "ex", "sm0", "sm1")
        self.slot_free = [base] * 4
        at_free = self.claim("b3") if at_halves is not None else None
        scored, soft, weighed, turned, written = {}, {}, {}, {}, []
        for i in range(-3, n + 1):
            if i + 3 < n:
                scored[i + 3] = units[i + 3][0](i + 3)
            if 0 <= i + 2 < n:
                soft[i + 2] = units[i + 2][1](i + 2, scored.pop(i + 2))
            if 0 <= i + 1 < n:
                weighed[i + 1] = units[i + 1][2](i + 1, soft.pop(i + 1))
            if filler is not None and i in (2, 7):
                step(filler)
            if 0 <= i < n:
                weights, known, n_blocks = weighed[i][:3]
                b, free = self.bank()
                ps = self.ps(b)

                def turn(e, weights=weights, ps=ps, n_blocks=n_blocks):
                    for k in range(n_blocks):
                        last = e.transpose(ps[:, k * P:k * P + P], weights[:, k * P:k * P + P], m["ident"][:])
                    return last
                t = self.pe.do(turn, known, free, self.const)
                self.slot_free[i % 4] = t
                to = m["at"] if at_halves is None else at_halves[0]
                at = to[:, i % 2, 0:n_blocks * P]
                c = self.act.do(lambda e, at=at, ps=ps, n_blocks=n_blocks: e.activation(
                    at, ps[:, 0:n_blocks * P], ACT.Copy), t, self.freed.get(f"at{i % 2}"), at_free)
                self.bank_free[b] = c
                if at_halves is not None:
                    lo = at_halves[1][:, i % 2, 0:n_blocks * P]
                    v = self.dve.do(lambda e, at=at, ps=ps, lo=lo: e.tensor_tensor(
                        lo, ps[:], at.bitcast(F32), ALU.subtract), c, self.freed.get(f"at{i % 2}"), at_free)
                    self.bank_free[b] = v
                    at, c = (at, lo), [c, v]
                turned[i] = (at, c, n_blocks)
            if 0 <= i - 1 < n:
                u = i - 1
                at, copied, n_blocks = turned.pop(u)
                values, ready = units[u][3]
                o, free = self.bank()
                width = values[0].shape[-1] * (1 if at_halves is None else 2)
                out = self.ps(o)[:, 0:width]

                def mix(e, at=at, out=out, values=values, n_blocks=n_blocks):
                    if at_halves is not None:
                        n = out.shape[-1] // 2
                        for k in range(n_blocks):
                            e.matmul(out.rearrange("p (w n) -> p w n", w=2), at[0][:, k * P:k * P + P], values[k],
                                     start=(k == 0), stop=False)
                            last = e.matmul(out[:, 0:n], at[1][:, k * P:k * P + P], values[k][:, 0, :], start=False,
                                            stop=(k == n_blocks - 1))
                        return last
                    for k in range(n_blocks):
                        last = e.matmul(out, at[:, k * P:k * P + P], values[k], start=(k == 0),
                                        stop=(k == n_blocks - 1))
                    return last
                mixed = self.pe.do(mix, copied, free, ready)
                self.freed[f"at{u % 2}"] = mixed
                w = units[u][4](u, out, mixed, weighed.pop(u))
                self.bank_free[o] = w
                self.freed[f"st{u % 4}"] = w
                written.append(w)
        self.freed["sm"] = self.freed["ex"] = self.latest()
        return written

    def memory_units(self, q_f, k_f, v_t, y, made, free):
        m = self.m
        scale = MEM_DH ** -0.5
        for h in range(MEM_HEADS):
            for t in range(NT):
                def score(u, h=h, t=t):
                    b, bank_free = self.bank()

                    def issue(e):
                        for k in range(2):
                            last = e.matmul(self.ps(b)[:, 0:SEQ], q_f[:, 2 * h + k, t * P:t * P + P],
                                            k_f[:, 2 * h + k, :], start=(k == 0), stop=(k == 1))
                        return last
                    return b, self.pe.do(issue, bank_free, made["q"], made["k"])

                def soften(u, scored):
                    b, done = scored
                    st = m["st"][:, u % 4, :]
                    ps, ex = self.ps(b)[:, 0:SEQ], m["work"][:, u % 4, 0:SEQ]
                    a = self.dve.do(lambda e: e.tensor_reduce(st[:, 0:1], ps, AX.X, ALU.max, negate=True), done,
                                    self.freed.get(f"st{u % 4}"))
                    a = self.dve.do(lambda e: e.tensor_scalar(st[:, 1:2], st[:, 0:1], scale, None, ALU.mult), a)
                    a = self.act.do(lambda e: e.activation(ex, ps, ACT.Exp, bias=st[:, 1:2], scale=scale,
                                                           accum_out=st[:, 2:3]), a, self.slot_free[u % 4])
                    self.bank_free[b] = a
                    return ex, a, st

                def weigh(u, soft):
                    ex, a, st = soft
                    r = self.dve.do(lambda e: e.reciprocal(st[:, 3:4], st[:, 2:3]), a)
                    return ex, a, 2, r, st

                def write(u, out, mixed, weighed, h=h, t=t):
                    r, st = weighed[3:]
                    return self.act.do(lambda e: e.activation(y[:, t, h * MEM_DH:(h + 1) * MEM_DH], out, ACT.Copy,
                                                              scale=st[:, 3:4]), mixed, r, free)
                values = [v_t[:, k, h * MEM_DH:(h + 1) * MEM_DH] for k in range(2)]
                yield score, soften, weigh, (values, made["v"]), write

    def lambda_full(self):
        d, m = self.dram, self.m
        lv = m["row_c"][:, 0:4 * DA_DK]
        got = self.load("lambda", lv, d["da_lambda"][0].rearrange("a b -> (a b)").partition_broadcast(P),
                        self.freed.get("row_c"))
        g = self.load("da_g", m["da_g"][:], d["da_norm_g"][0].partition_broadcast(P))
        v = lv.rearrange("p (a b n) -> p a b n", a=2, b=2)
        tmp = m["sm"][:, 0, 0:2 * DA_DK].rearrange("p (a n) -> p a n", a=2)
        a = self.dve.do(lambda e: e.tensor_tensor(tmp, v[:, :, 0, :], v[:, :, 1, :], ALU.mult), got,
                        self.claim("sm"))
        self.freed["row_c"] = a
        lam = m["lam"]
        a = self.dve.do(lambda e: e.tensor_reduce(lam[:, 0:2], tmp, AX.X, ALU.add), a)
        self.freed["sm"] = a
        a = self.act.do(lambda e: e.activation(lam[:, 2:4], lam[:, 0:2], ACT.Exp), a)
        a = self.dve.do(lambda e: e.tensor_tensor(lam[:, 4:5], lam[:, 3:4], lam[:, 2:3], ALU.subtract), a)
        a = self.dve.do(lambda e: e.tensor_scalar(lam[:, 5:6], lam[:, 4:5], -LAMBDA_INIT, None, ALU.add), a)
        self.da_gain = self.dve.do(lambda e: e.tensor_scalar(m["da_g"][:], m["da_g"][:], 1.0 - LAMBDA_INIT, None,
                                                             ALU.mult), g)
        return a

    def differential_units(self, q_f, k_f, v_t, y, made, free, lam):
        m = self.m
        scale = DA_DK ** -0.5
        for h in range(DA_HEADS):
            for t in range(NT):
                nk = (t + 1) * P

                def score(u, h=h, t=t, nk=nk):
                    banks = [self.bank() for _ in range(2)]

                    def issue(e):
                        for c in range(2):
                            rows = slice(c * DA_DK, (c + 1) * DA_DK)
                            last = e.matmul(self.ps(banks[c][0])[:, 0:nk], q_f[rows, h, t * P:t * P + P],
                                            k_f[rows, h, 0:nk], start=True, stop=True)
                        return last
                    return banks, self.pe.do(issue, [f for _, f in banks], made["q"], made["k"])

                def soften(u, scored, h=h, nk=nk):
                    banks, done = scored
                    st = m["st"][:, u % 4, :]
                    sm = m["work"][:, u % 4, :].rearrange("p (c n) -> p c n", c=2)[:, :, 0:nk]
                    slope = 2.0 ** -(h + 1.0)
                    for c in range(2):
                        ps = self.ps(banks[c][0])[:, 0:nk]
                        a = self.dve.do(lambda e, c=c, ps=ps: e.scalar_tensor_tensor(
                            out=sm[:, c, :], in0=m["dist"][:, SEQ - nk:SEQ], scalar=-slope / scale, in1=ps,
                            op0=ALU.mult, op1=ALU.add), done, self.tables, self.slot_free[u % 4])
                        self.bank_free[banks[c][0]] = a
                    a = self.dve.do(lambda e: e.tensor_reduce(st[:, 0:2], sm, AX.X, ALU.max, negate=True), a,
                                    self.freed.get(f"st{u % 4}"))
                    a = self.dve.do(lambda e: e.tensor_scalar(st[:, 2:4], st[:, 0:2], scale, None, ALU.mult), a)
                    for c in range(2):
                        x = self.act.do(lambda e, c=c: e.activation(sm[:, c, :], sm[:, c, :], ACT.Exp,
                                                                    bias=st[:, 2 + c:3 + c], scale=scale,
                                                                    accum_out=st[:, 4 + c:5 + c]), a)
                    return sm, x, st

                def weigh(u, soft, t=t):
                    sm, x, st = soft
                    a = self.dve.do(lambda e: e.reciprocal(st[:, 6:8], st[:, 4:6]), x)
                    a = self.dve.do(lambda e: e.tensor_tensor(st[:, 8:9], st[:, 7:8], m["lam"][:, 5:6], ALU.mult),
                                    a, lam)
                    b = self.dve.do(lambda e: e.tensor_scalar(sm[:, 0, :], sm[:, 0, :], st[:, 6:7], None, ALU.mult), a)
                    b = self.dve.do(lambda e: e.scalar_tensor_tensor(out=sm[:, 0, :], in0=sm[:, 1, :],
                                                                     scalar=st[:, 8:9], in1=sm[:, 0, :],
                                                                     op0=ALU.mult, op1=ALU.add), b)
                    return sm[:, 0, :], b, t + 1

                def write(u, out, mixed, weighed, h=h, t=t):
                    a = self.act.do(lambda e: e.activation(y[:, t, h * DA_DV:(h + 1) * DA_DV], out, ACT.Copy),
                                    mixed, free)
                    i = t * DA_HEADS + h
                    return self.act.do(lambda e: e.activation(m["junk"][:], out, ACT.Square,
                                                              accum_out=m["unit"][:, i:i + 1]), a,
                                       self.junk_free)
                values = [v_t[:, k, h * DA_DV:(h + 1) * DA_DV] for k in range(t + 1)]
                yield score, soften, weigh, (values, made["v"]), write

    def differential_norm(self, y, written):
        m = self.m
        ms = m["unit"][:, 0:NT * DA_HEADS]
        a = self.dve.do(lambda e: e.tensor_scalar(ms, ms, 1.0 / DA_DV, EPS, ALU.mult, ALU.add), written)
        a = self.act.do(lambda e: e.activation(ms, ms, ACT.Sqrt), a)
        r = self.dve.do(lambda e: e.reciprocal(ms, ms), a)
        out = []
        for t in range(NT):
            for h in range(DA_HEADS):
                s = slice(h * DA_DV, (h + 1) * DA_DV)
                out.append(self.dve.do(lambda e, t=t, h=h, s=s: e.scalar_tensor_tensor(
                    out=y[:, t, s], in0=y[:, t, s], scalar=ms[:, t * DA_HEADS + h:t * DA_HEADS + h + 1],
                    in1=m["da_g"][:], op0=ALU.mult, op1=ALU.mult), r, self.da_gain))
        self.freed["sm"] = self.latest()
        self.freed["ex"] = self.freed["sm"]
        return out[-1]

    def retention(self, qk, v_t, y, made, free, filler):
        m = self.m
        decay = m["decay"][:].rearrange("p (h n) -> p h n", h=RET_HEADS)
        written = []
        pairs = ((0, 0), (0, 1), (1, 1))
        for h in range(RET_HEADS):
            b, bank_free = self.bank()
            ps = self.ps(b)

            def score(e, h=h, ps=ps):
                for i, (k, q) in enumerate(pairs):
                    last = e.matmul(ps[:, i * P:i * P + P], qk[:, RET_HEADS + h, k * P:k * P + P],
                                    qk[:, h, q * P:q * P + P], start=True, stop=True)
                return last
            scored = self.pe.do(score, bank_free, made["q"])
            sm = m["sm"][:, h % 2, :]
            last_use = self.freed.get(f"sm{h % 2}")
            a = self.dve.do(lambda e, h=h, ps=ps, sm=sm: e.tensor_tensor(sm[:, 0:2 * P], ps[:, 0:2 * P],
                                                                         decay[:, h, :], ALU.mult),
                            scored, self.tables, last_use, self.claim("sm"))
            a = self.dve.do(lambda e, h=h, ps=ps, sm=sm: e.tensor_tensor(sm[:, 2 * P:3 * P], ps[:, 2 * P:3 * P],
                                                                         decay[:, h, 0:P], ALU.mult), scored)
            self.bank_free[b] = a
            step(filler)
            o, bank_free = self.bank()
            out = self.ps(o)

            def mix(e, h=h, sm=sm, out=out):
                v = slice(h * RET_DV, (h + 1) * RET_DV)
                e.matmul(out[:, 0:RET_DV], sm[:, 0:P], v_t[:, 0, v], start=True, stop=True)
                e.matmul(out[:, RET_DV:], sm[:, P:2 * P], v_t[:, 0, v], start=True, stop=False)
                return e.matmul(out[:, RET_DV:], sm[:, 2 * P:3 * P], v_t[:, 1, v], start=False, stop=True)
            mixed = self.pe.do(mix, a, bank_free, made["v"])
            self.freed[f"sm{h % 2}"] = mixed
            for t in range(NT):
                s = self.dve.do(lambda e, t=t, out=out: e.bn_stats(m["bn"][:, t, 0, :],
                                                                   out[:, t * RET_DV:(t + 1) * RET_DV]),
                                mixed, written)
                s = self.dve.do(lambda e, t=t, h=h: e.bn_aggr(m["gn"][:, t * RET_HEADS + h, :],
                                                              m["bn"][:, t, 0, :]), s)
            a = self.act.do(lambda e, h=h, out=out: e.activation(
                y[:, :, h * RET_DV:(h + 1) * RET_DV], out[:].rearrange("p (t n) -> p t n", t=NT), ACT.Copy), s, free)
            self.bank_free[o] = a
            written = [s, a]
        return written

    def retention_norm(self, y, written, gate, gate_ready, g, b, rows):
        m = self.m
        n = NT * RET_HEADS
        mean, var = m["gn"][:, :, 0], m["gn"][:, :, 1]
        rstd, nb = m["rstd"][:, 0:n], m["nb"][:, 0:n]
        r = self.inverse_root(var, EPS, rstd, written)
        r = self.dve.do(lambda e: e.scalar_tensor_tensor(out=nb, in0=mean, scalar=-1.0, in1=rstd, op0=ALU.mult,
                                                         op1=ALU.mult), r)
        out = []
        for t in range(NT):
            for h in range(RET_HEADS):
                s, i = slice(h * RET_DV, (h + 1) * RET_DV), t * RET_HEADS + h
                a = self.dve.do(lambda e, t=t, s=s, i=i: e.tensor_scalar(
                    y[:, t, s], y[:, t, s], rstd[:, i:i + 1], nb[:, i:i + 1], ALU.mult, ALU.add), r)
            a = self.dve.do(lambda e, t=t: e.tensor_tensor(y[:, t, :], y[:, t, :], g, ALU.mult), a, rows)
            a = self.dve.do(lambda e, t=t: e.tensor_tensor(y[:, t, :], y[:, t, :], b, ALU.add), a)
            a = self.dve.do(lambda e, t=t: e.tensor_tensor(y[:, t, :], y[:, t, :], gate[:, t, :], ALU.mult), a,
                            gate_ready)
            out.append(a)
        self.freed["rows"] = out
        self.freed["sm"] = self.latest()
        self.release("decay")
        return out

    def feed_forward(self, lhs, n_chunks, up, down, pair, finish, between=None, early=None, ending=None):
        m = self.m
        self.use_ring(range(4, 8))
        acc_free = [self.bank_free.get(b) for b in range(4)]
        hidden = m["b1"][:, 0:2 * NT * F_CHUNK].rearrange("p (s t n) -> p s t n", s=2, t=NT)
        gated = m["b1"][:, 2 * NT * F_CHUNK:].rearrange("p (s t n) -> p s t n", s=2, t=NT)
        hidden_free, turned_free = [self.claim("b1")] * 2, [self.claim("b0")] * 2
        state = {}

        def up_part(i):
            banks = []

            def keep(c, t, ps, done):
                state["up"] = done
                banks.append(([x for x in range(8) if self.ps(x) is ps][0], done))

            yield from self.gemm_token(lhs, [up(i)], keep)
            slot = i % 2
            out = []
            for t, (b, done) in enumerate(banks):
                ps = self.ps(b)
                a = self.act.do(lambda e, t=t, ps=ps: e.activation(gated[:, slot, t, :], ps[:, F_CHUNK:], ACT.Silu),
                                done, hidden_free[slot])
                h = self.dve.do(pair(i, t, hidden[:, slot, t, :], ps[:, 0:F_CHUNK], gated[:, slot, t, :]), a,
                                self.combined, hidden_free[slot])
                self.bank_free[b] = h
                out.append(h)
            state[i] = out

        def turn_part(i):
            slot = i % 2
            b, bank_free = self.bank()
            ps = self.ps(b)

            def turn(e):
                for k in range(2):
                    for t in range(NT):
                        last = e.transpose(ps[:, k * SEQ + t * P:k * SEQ + t * P + P],
                                           hidden[:, slot, t, k * P:k * P + P], m["ident"][:])
                return last
            turned = self.pe.do(turn, state.pop(i), bank_free)
            hidden_free[slot] = turned
            hi, lo = m["ht_hi"][:, slot, :, :], m["ht_lo"][:, slot, :, :]
            a = self.act.do(lambda e: e.activation(hi, ps[:], ACT.Copy), turned, turned_free[slot])
            v = self.dve.do(lambda e: e.tensor_tensor(lo, ps[:], hi.bitcast(F32), ALU.subtract), a,
                            turned_free[slot])
            self.bank_free[b] = v
            return hi, lo, [a, v]

        def down_part(i, hi, lo, halves):
            slot = i % 2
            n = self.take(down(i))
            wh, wl = [w.rearrange("p (k n) -> p k n", k=2) for w in self.halves(n)]

            def issue(e, t, parts=range(2)):
                for k in range(2):
                    tok = slice(t * P, t * P + P)
                    for j, (x, w) in enumerate(((hi, wh), (hi, wl), (lo, wh))):
                        for half in parts:
                            last = e.matmul(self.ps(2 * t + half)[:], x[:, k, tok],
                                            w[:, k, half * BANK:(half + 1) * BANK],
                                            start=(i == 0 and k == 0 and j == 0),
                                            stop=(i == n_chunks - 1 and k == 1 and j == 2))
                return last
            known = [halves, self.full(n), acc_free if i == 0 else None]
            if i < n_chunks - 1:
                done = [[self.pe.do(lambda e, t=t: issue(e, t), known)] for t in range(NT)]
            else:
                done = [[self.pe.do(lambda e, t=t, half=half: issue(e, t, [half]), known) for half in range(2)]
                        for t in range(NT)]
            turned_free[slot] = done[-1][-1]
            self.done_with(n, done[-1][-1])
            return done

        def tick():
            if between is not None:
                between()

        parts = up_part(0)
        step(parts)
        if early is not None:
            early()
        drain(parts)
        for i in range(n_chunks):
            parts = up_part(i + 1) if i + 1 < n_chunks else iter(())
            step(parts)
            tick()
            turned = turn_part(i)
            drain(parts)
            tick()
            self.hold = i == n_chunks - 1 and ending is None
            if ending is not None and i == n_chunks - 1:
                ending(state["up"])
            done = down_part(i, *turned)
            tick()
        self.warm(ACT.Sqrt)
        for t in range(NT):
            for half in range(2):
                self.bank_free[2 * t + half] = finish(t, half, self.ps(2 * t + half), done[t][half])
        self.freed["b0"] = self.freed["b1"] = self.latest()
        self.use_ring([4, 5, 6, 7, 0, 1, 2, 3])

    def experts(self, x, x_ready):
        d, m = self.dram, self.m
        logits = self.router_logits()
        w1, w3, w2 = d["w1"][0], d["w3"][0], d["w2"][0]

        def up(i):
            e, c0 = i // 2, (i % 2) * F_CHUNK
            a = w3[e].rearrange("(k p) n -> p k n", p=P)
            g = w1[e].rearrange("(k p) n -> p k n", p=P)
            return [[(lambda s: whole(BANK)(s)[:, :, 0:F_CHUNK], a[:, q * KH:(q + 1) * KH, c0:c0 + F_CHUNK]),
                     (lambda s: whole(BANK)(s)[:, :, F_CHUNK:], g[:, q * KH:(q + 1) * KH, c0:c0 + F_CHUNK])]
                    for q in range(2)]

        def down(i):
            e, c0 = i // 2, (i % 2) * F_CHUNK
            return [(whole(D), w2[e, c0:c0 + F_CHUNK, :].rearrange("(k p) n -> p k n", p=P))]

        def pair(i, t, out, a, g):
            c = m["combine"][:, t, i // 2:i // 2 + 1]
            return lambda e: e.scalar_tensor_tensor(out=out, in0=a, scalar=c, in1=g, op0=ALU.mult, op1=ALU.mult)
        finish = self.residual(x)
        self.x_full = x_ready
        g, b, rows = self.rows("ln2", d["ln2_g"][0], d["ln2_b"][0])
        ctx = self.tok("b3")

        def fetch_context():
            self.ctx_in = self.load("ctx", ctx, d["ctx_2"][0].rearrange("(t p) n -> p t n", p=P), self.claim("b3"))
            yield

        def ending(up_done):
            drain(mods)
            self.ctx_lhs = self.modulated(ctx, self.ctx_in, 1, 0, 0, None, up_done)
        tick, mods = self.paced(0, range(2 * N_MOD), "b3", N_EXPERTS * 2 - 3, fetch_context())
        self.feed_forward(self.xt, N_EXPERTS * 2, up, down, pair, finish, tick, lambda: self.route(logits), ending)
        self.release("xt")
        self.x_ready = self.finish_norm(finish.norm, g, b, rows)

    def router_weights(self):
        d, m = self.dram, self.m
        nr = N_GROUPS + N_EXPERTS
        raw = m["r_raw"][:]
        w = [self.load("w_rg", raw[:, :, 0:N_GROUPS], d["w_rg"][0].rearrange("(k p) n -> p k n", p=P)),
             self.load("w_re", raw[:, :, N_GROUPS:], d["w_re"][0].rearrange("(k p) n -> p k n", p=P))]
        self.r_bias = [self.load("b_rg", m["r_bias"][:, 0:N_GROUPS], d["b_rg"][0].partition_broadcast(P)),
                       self.load("b_re", m["r_bias"][:, N_GROUPS:], d["b_re"][0].partition_broadcast(P))]
        hi, lo = m["r_w"][:, :, 0:nr], m["r_w"][:, :, nr:]
        a = self.act.do(lambda e: e.activation(hi, raw, ACT.Copy), w)
        self.r_ready = [a, self.dve.do(lambda e: e.tensor_tensor(lo, raw, hi.bitcast(F32), ALU.subtract), a)]

    def router_logits(self):
        m = self.m
        nr = N_GROUPS + N_EXPERTS
        hi, lo, ready = self.xt
        b, bank_free = self.bank()
        ps = self.ps(b)

        def issue(e):
            for k in range(KD):
                if k:
                    e.matmul(ps[0:nr, 0:SEQ], m["r_w"][:, k, 0:nr], lo[:, k, :], start=False, stop=False)
                last = e.matmul(ps[0:2 * nr, 0:SEQ], m["r_w"][:, k, :], hi[:, k, :], start=(k == 0),
                                stop=(k == KD - 1))
                if k == 0:
                    e.matmul(ps[0:nr, 0:SEQ], m["r_w"][:, k, 0:nr], lo[:, k, :], start=False, stop=False)
            return last
        done = self.pe.do(issue, ready, self.r_ready, bank_free)
        rows = m["r_rows"]
        a = self.act.do(lambda e: e.activation(rows[0:2 * nr, :], ps[0:2 * nr, 0:SEQ], ACT.Copy), done)
        self.bank_free[b] = a
        return a

    def route(self, rows_ready):
        m = self.m
        nr = N_GROUPS + N_EXPERTS
        b, bank_free = self.bank()
        ps = self.ps(b)

        def issue(e):
            for t in range(NT):
                last = e.matmul(ps[:, t * nr:(t + 1) * nr], m["r_rows"][0:2 * nr, t * P:t * P + P],
                                m["r_fold"][0:2 * nr, :], start=True, stop=True)
            return last
        done = self.pe.do(issue, rows_ready, self.tables, bank_free)
        tiles = [self.route_tile(t, ps[:, t * nr:(t + 1) * nr], done, b) for t in range(NT)]
        last = [None] * NT
        running = True
        while running:
            running = False
            for t, steps in enumerate(tiles):
                token = next(steps, None)
                if token is not None:
                    last[t], running = token, True
        self.combined = last

    def route_tile(self, t, ps, done, bank):
        m = self.m
        r = m["route"][:, t, :]
        lg = r[:, 0:20]
        groups, experts = r[:, 0:4], r[:, 4:20]
        v = self.dve.do
        a = v(lambda e: e.tensor_tensor(lg, ps, m["r_bias"][:], ALU.add), done, self.r_bias)
        self.bank_free[bank] = a
        yield a

        def first_of_largest(values, top, tmp, hot, a):
            a = v(lambda e: e.tensor_reduce(top, values, AX.X, ALU.max), a)
            yield a
            a = v(lambda e: e.tensor_scalar(tmp, values, top, None, ALU.is_equal), a)
            yield a
            a = v(lambda e: e.scalar_tensor_tensor(out=tmp, in0=tmp, scalar=-100.0, in1=m["index"][:],
                                                   op0=ALU.mult, op1=ALU.add), a, self.tables)
            yield a
            a = v(lambda e: e.tensor_reduce(r[:, 50:51], tmp, AX.X, ALU.min), a)
            yield a
            yield v(lambda e: e.tensor_scalar(hot, tmp, r[:, 50:51], None, ALU.is_equal), a)
        tmp, g_hot, sel, hot1, hot2 = r[:, 20:24], r[:, 24:28], r[:, 28:32], r[:, 32:36], r[:, 36:40]
        for a in first_of_largest(groups, r[:, 40:41], tmp, g_hot, a):
            yield a
        a = v(lambda e: e.tensor_scalar(r[:, 41:42], r[:, 40:41], -1.0, None, ALU.mult), a)
        yield a
        x = self.act.do(lambda e: e.activation(r[:, 51:55], groups, ACT.Exp, bias=r[:, 41:42],
                                               accum_out=r[:, 42:43]), a)
        a = v(lambda e: e.tensor_scalar(sel, experts[:, 0:4], g_hot[:, 0:1], None, ALU.mult), a)
        yield a
        for g in range(1, N_GROUPS):
            a = v(lambda e, g=g: e.scalar_tensor_tensor(out=sel, in0=experts[:, 4 * g:4 * g + 4],
                                                        scalar=g_hot[:, g:g + 1], in1=sel, op0=ALU.mult,
                                                        op1=ALU.add), a)
            yield a
        for a in first_of_largest(sel, r[:, 44:45], tmp, hot1, a):
            yield a
        a = v(lambda e: e.scalar_tensor_tensor(out=sel, in0=hot1, scalar=-MASKED, in1=sel, op0=ALU.mult,
                                               op1=ALU.add), a)
        yield a
        for a in first_of_largest(sel, r[:, 45:46], tmp, hot2, a):
            yield a
        a = v(lambda e: e.tensor_tensor(r[:, 46:47], r[:, 45:46], r[:, 44:45], ALU.subtract), a)
        yield a
        q = self.act.do(lambda e: e.activation(r[:, 47:48], r[:, 46:47], ACT.Exp), a)
        p_top = v(lambda e: e.reciprocal(r[:, 43:44], r[:, 42:43]), x)
        yield p_top
        a = v(lambda e: e.tensor_scalar(r[:, 48:49], r[:, 47:48], 1.0, None, ALU.add), q)
        yield a
        a = v(lambda e: e.reciprocal(r[:, 49:50], r[:, 48:49]), a)
        yield a
        a = v(lambda e: e.tensor_tensor(r[:, 49:50], r[:, 49:50], r[:, 43:44], ALU.mult), a, p_top)
        yield a
        a = v(lambda e: e.tensor_tensor(r[:, 48:49], r[:, 49:50], r[:, 47:48], ALU.mult), a)
        yield a
        a = v(lambda e: e.tensor_scalar(hot1, hot1, r[:, 49:50], None, ALU.mult), a)
        yield a
        a = v(lambda e: e.scalar_tensor_tensor(out=hot1, in0=hot2, scalar=r[:, 48:49], in1=hot1, op0=ALU.mult,
                                               op1=ALU.add), a)
        yield a
        for g in range(N_GROUPS):
            yield v(lambda e, g=g: e.tensor_scalar(m["combine"][:, t, 4 * g:4 * g + 4], hot1, g_hot[:, g:g + 1],
                                                   None, ALU.mult), a)

    def finish_norm(self, norm, g, b, rows):
        self.norm_finish(norm)
        return norm["centred"], (g, b, rows)

    def modulation(self, layer, chunks, ring):
        d, m = self.dram, self.m
        w = d["mod_w_2"][layer].rearrange("(k p) n -> p k n", p=P)
        acc = (m["b2"][:].rearrange("p (s v n) -> p s v n", s=2, v=2) if layer == 0 else
               m["decay"][:].rearrange("p (s v n) -> p s v n", s=2, v=1))
        slots = m[ring][:].rearrange("p (s k n) -> p s k n", s=2, k=2)
        acc_free = [self.claim("b2" if layer == 0 else "decay")] * 2
        slot_free = [self.claim(ring)] * 2
        bias_free = [self.freed.get("row_c")] * 2
        mg, b4 = self.tok("mg"), self.tok("b4")
        gate_rows = {0: [[mg[:, 0, :], mg[:, 1, :]], [b4[:, 0, :]], [b4[:, 1, :]]],
                     1: [[mg[:, 0, :]], [mg[:, 1, :]], [b4[:, 0, :]]]}[layer]
        gate_free = self.claim("mg", "b4")
        self.mod_ready = self.mod_ready or {}
        ready = self.mod_ready.setdefault(layer, [])
        quarters = [(c, q) for c in chunks for q in range(KD // 2)]
        landed = {}

        def fetch(i):
            if i < len(quarters):
                c, q = quarters[i]
                s = i % 2
                self.sync.wait(slot_free[s])
                sem = f"mod{s}"
                self.sems.add(sem)
                src = w[:, 2 * q:2 * q + 2, c * BANK:(c + 1) * BANK]
                self.sync.steps.append(("dma", lambda e: e.dma_start(slots[:, s, :, :], src), sem))
                self.mod_count[s] += 16
                landed[i] = (sem, self.mod_count[s])

        def start(at, c):
            vectors = 2 if layer == 0 and c // 2 < 5 else 1
            slot = (at // 4) % 2
            bias = m["row_c"][0:1, slot * BANK:(slot + 1) * BANK]
            b = self.load(f"mod_b{layer}_{c}", bias, d["mod_b_2"][layer:layer + 1, c * BANK:(c + 1) * BANK],
                          bias_free[slot])
            chain = [None] * vectors
            for q in range(KD // 2):
                i = at + q
                s = i % 2
                for v in range(vectors):
                    out = acc[:, slot, v, :]
                    for k in range(2):
                        kk = 2 * q + k
                        col = m["cvec"][:, v, kk:kk + 1]
                        wk = slots[:, s, k, :]
                        after = [landed[i], self.c_ready, acc_free[slot] if kk == 0 else None, chain[v]]
                        if kk == 0:
                            chain[v] = self.dve.do(lambda e, out=out, wk=wk, col=col: e.tensor_scalar(
                                out, wk, col, None, ALU.mult), after)
                        else:
                            chain[v] = self.dve.do(lambda e, out=out, wk=wk, col=col: e.scalar_tensor_tensor(
                                out=out, in0=wk, scalar=col, in1=out, op0=ALU.mult, op1=ALU.add), after)
                slot_free[s] = chain[-1]
                if q == KD // 2 - 1:
                    chain = [self.dve.do(lambda e, v=v: e.tensor_tensor(
                        acc[0:1, slot, v, :], acc[0:1, slot, v, :], bias, ALU.add), chain[v], b)
                        for v in range(vectors)]
                    bias_free[slot] = chain[-1]
                yield
                fetch(i + 2)
            self.started = (c, vectors, slot, list(chain))

        def finish(c, vectors, slot, summed):
            j, half = c // 2, c % 2
            for v in range(vectors):
                if j % 3 == 2:
                    if v >= len(gate_rows[j // 3]):
                        continue
                    bank, free = self.bank()
                    ps = self.ps(bank)

                    def issue(e, v=v, ps=ps):
                        return e.matmul(ps[:], m["ones"][:], acc[:, slot, v, :], start=True, stop=True)
                    done = self.pe.do(issue, summed, free, self.ones)
                    row = gate_rows[j // 3][v][:, half * BANK:(half + 1) * BANK]
                    half_of = 1.0 if j // 3 == 1 else 0.5
                    token = self.act.do(lambda e, ps=ps, row=row: e.activation(row, ps[:], ACT.Copy, scale=half_of),
                                        done, gate_free)
                else:
                    bank, free = self.bank()
                    ps = self.ps(bank)

                    def issue(e, v=v, ps=ps):
                        for i in range(4):
                            cols = slice(i * P, i * P + P)
                            last = e.matmul(ps[:, i:i + 1], acc[:, slot, v, cols], m["ones"][:, 0:1], start=True,
                                            stop=True)
                        return last
                    done = self.pe.do(issue, summed, free, self.ones)
                    f = j * KD + half * 4
                    out = m["mod"][:, 2 * layer + v, f:f + 4]
                    token = self.dve.do(lambda e, out=out, ps=ps: e.tensor_scalar(
                        out, ps[:, 0:4], 1.0 if j % 3 == 1 else 0.0, None, ALU.add), done)
                self.bank_free[bank] = token
                ready.append(token)
                acc_free[slot] = done

        fetch(0)
        fetch(1)
        yield
        started = None
        for n, c in enumerate(chunks):
            yield from start(4 * n, c)
            if started is not None:
                finish(*started)
            started = self.started
        finish(*started)
        self.release("b2" if layer == 0 else "decay", "row_c", ring)

    def paced(self, layer, chunks, ring, n_chunks, last=(), before=()):
        steps = self.then(before, self.modulation(layer, chunks, ring), last)
        total, ticks = 3 + 4 * len(chunks), 3 * n_chunks - 3
        at = [0, 0]

        def tick():
            at[0] += 1
            while at[1] < total * at[0] / ticks:
                at[1] += 1
                step(steps)
        return tick, steps

    def affine(self, which, layer, j, norm=None):
        m = self.m
        cols = m["mod"][:, 2 * layer + which, :]
        scale, shift = cols[:, (3 * j + 1) * KD:(3 * j + 2) * KD], cols[:, 3 * j * KD:(3 * j + 1) * KD]
        known = list(self.mod_ready[layer])
        if norm is None:
            return scale, shift, known
        g, b = self.gb(norm)
        slot = self.fold_at % 2
        self.fold_at += 1
        s2, t2 = m["fold"][:, slot, 0:KD], m["fold"][:, slot, KD:2 * KD]
        free = self.freed.get(f"fold{slot}")
        p = self.dve.do(lambda e: e.tensor_tensor(t2, b, scale, ALU.mult), known, self.cols_ready, free)
        q = self.dve.do(lambda e: e.tensor_tensor(t2, t2, shift, ALU.add), p)
        r = self.dve.do(lambda e: e.tensor_tensor(s2, g, scale, ALU.mult), free)
        return s2, t2, [q, r]

    def modulated(self, x, ready, which, layer, j, norm, free=None):
        m = self.m
        free = self.claim("xt") if free is None else free
        if norm is None:
            return self.to_lhs(x, [ready], (m["xt_hi"], m["xt_lo"]), free, self.affine(which, layer, j)), ready
        centred, (g, b, rows) = ready
        fold = self.affine(which, layer, j, norm)
        slot = (self.fold_at - 1) % 2
        lhs = self.to_lhs(x, centred, (m["xt_hi"], m["xt_lo"]), free, fold)
        self.freed[f"fold{slot}"] = lhs[2]
        self.hold = False
        if g is None:
            return lhs, None
        return lhs, self.gain(x, centred, g, b, rows, self.turned)

    def gated_residual(self, x, gate, known):
        m = self.m
        x_full = self.x_full

        def finish(t, half, ps, done):
            s = slice(half * BANK, (half + 1) * BANK)
            tmp = m["sm"][:, t, :]
            a = self.dve.do(lambda e: e.tensor_tensor(tmp, ps[:], gate[:, s], ALU.mult), done, known,
                            self.freed.get("sm"), self.freed.get(f"sm{t}"))
            b = self.dve.do(lambda e: e.scalar_tensor_tensor(out=x[:, t, s], in0=x[:, t, s], scalar=ALPHA_2,
                                                             in1=tmp, op0=ALU.mult, op1=ALU.add), a, x_full)
            self.freed[f"sm{t}"] = b
            self.norm_half(finish.norm, t, half, b)
            return a
        finish.norm = self.new_norm(x)
        return finish

    def conditioned_ffn(self, x, ready, which, layer, j, gate, norm, chunks=(), ending=None, rows=True,
                        before=()):
        d, m = self.dram, self.m
        f = j // 2
        lhs, self.x_full = ready if norm == "made" else self.modulated(x, ready, which, layer, j, norm)
        self.warm(ACT.Silu)
        g = b = None
        if rows:
            g, b, rows = self.rows(f"ln_{layer}{which}{j}", d["ln_g_2"][layer, j], d["ln_b_2"][layer, j])
        wi = d["ffn_wi_2"][layer, f].rearrange("(k p) n -> p k n", p=P)
        wo = d["ffn_wo_2"][layer, f]

        def up(i):
            c0 = i * F_CHUNK
            return [[(lambda s: whole(BANK)(s)[:, :, 0:F_CHUNK], wi[:, q * KH:(q + 1) * KH, c0:c0 + F_CHUNK]),
                     (lambda s: whole(BANK)(s)[:, :, F_CHUNK:],
                      wi[:, q * KH:(q + 1) * KH, D_FF + c0:D_FF + c0 + F_CHUNK])] for q in range(2)]

        def down(i):
            return [(whole(D), wo[i * F_CHUNK:(i + 1) * F_CHUNK, :].rearrange("(k p) n -> p k n", p=P))]

        def pair(i, t, out, a, g_):
            return lambda e: e.tensor_tensor(out, a, g_, ALU.mult)
        self.combined = None
        n_chunks = D_FF // F_CHUNK
        tick, mods = self.paced(1, chunks, "b2", n_chunks, before=before) if chunks else (None, iter(()))
        finish = self.gated_residual(x, gate, list(self.mod_ready[layer]))
        self.feed_forward(lhs, n_chunks, up, down, pair, finish, tick, None, ending)
        drain(mods)
        self.release("xt")
        return self.finish_norm(finish.norm, g, b, rows)

    def rotate(self, x, heads, t, table, tmp, ready):
        m = self.m
        v = x.rearrange("p (h a s f) -> p h a s f", a=2, s=2, f=AXIS_DIM // 2)
        x1, x2 = v[:, :, :, 0, :], v[:, :, :, 1, :]
        shape = [P, heads, 2, AXIS_DIM // 2]
        cos, sin = [m["rope"][:, t, table + i, :].rearrange("p (a f) -> p a f", a=2).unsqueeze(1).to_broadcast(shape)
                    for i in range(2)]
        half = heads * HEAD_DIM // 2
        t1, t2 = [tmp[:, i * half:(i + 1) * half].rearrange("p (h a f) -> p h a f", h=heads, a=2) for i in range(2)]
        v_ = self.dve.do
        a = v_(lambda e: e.tensor_tensor(t1, x1, sin, ALU.mult), ready, self.tables, self.freed.get("rotated"))
        b = v_(lambda e: e.tensor_tensor(t2, x2, sin, ALU.mult), a)
        c = v_(lambda e: e.tensor_tensor(x1, x1, cos, ALU.mult), b)
        e_ = v_(lambda e: e.tensor_tensor(x2, x2, cos, ALU.mult), c)
        f = v_(lambda e: e.tensor_tensor(x1, x1, t2, ALU.subtract), e_)
        self.freed["rotated"] = v_(lambda e: e.tensor_tensor(x2, x2, t1, ALU.add), f)
        return self.freed["rotated"]

    def keys_values_steps(self, lhs, kv, free, made):
        row = self.kv_row

        def evacuate(c, t, ps, done):
            made.append(self.dve.do(lambda e: e.tensor_tensor(kv[:, t, :], ps[:], row, ALU.add), done, free,
                                    self.qkv_bias))
            return made[-1]
        weights = columns(self.dram["attn_wqkv_2"][0], N_HEADS * HEAD_DIM, 2 * N_KV * HEAD_DIM)
        yield from self.gemm_token(lhs, weights, evacuate)

    def double_keys(self, kv, twice, made, free):
        n = N_KV * HEAD_DIM
        copied = []
        for t in range(NT):
            src = kv[:, t, 0:n].rearrange("p (g n) -> p g n", g=N_KV)
            dst = twice[:, t * 2 * n:(t + 1) * 2 * n].rearrange("p (g c n) -> p g c n", g=N_KV, c=2)
            for c in range(2):
                copied.append(self.dve.do(lambda e, c=c, src=src, dst=dst: e.tensor_copy(dst[:, :, c, :], src),
                                          made[t], free))
        return copied

    def turn_keys(self, twice, copied, free, plain=None, halves=None):
        m = self.m
        out = []
        n = N_KV * HEAD_DIM
        for g in range(0, N_KV, 2):
            b, bank_free = self.bank()
            ps = self.ps(b)

            def turn(e, g=g, ps=ps):
                for i in range(2):
                    for t in range(NT):
                        cols = t * 2 * n + (g + i) * P
                        last = e.transpose(ps[:, i * SEQ + t * P:i * SEQ + t * P + P], twice[:, cols:cols + P],
                                           m["ident"][:])
                return last
            turned = self.pe.do(turn, copied, bank_free)
            to = plain[:, g:g + 2, :] if halves is None else halves[:, 0, g:g + 2, :]
            a = self.act.do(lambda e, ps=ps, to=to: e.activation(to, ps[:], ACT.Copy), turned, free)
            if halves is not None:
                lo = halves[:, 1, g:g + 2, :]
                out.append(a)
                a = self.dve.do(lambda e, ps=ps, to=to, lo=lo: e.tensor_tensor(lo, ps[:], to.bitcast(F32),
                                                                               ALU.subtract), a)
            self.bank_free[b] = a
            out.append(a)
        return out + copied

    def window_units(self, q, kr, vr, y, ready):
        m = self.m
        for h in range(N_HEADS):
            for t in range(NT):
                g = h // GROUP

                def score(u, h=h, t=t, g=g):
                    b, free = self.bank()
                    ps = self.ps(b)
                    rows = slice((h % 2) * HEAD_DIM, (h % 2 + 1) * HEAD_DIM)

                    def issue(e):
                        both = ps[:].rearrange("p (c s) -> p c s", c=2)
                        for i, (x, w) in enumerate(((0, 0), (0, 1), (1, 0))):
                            last = e.matmul(both, q[x][rows, h // 2, t * P:t * P + P], kr[rows, :, w, g, :],
                                            start=(i == 0), stop=(i == 2))
                        return last
                    return b, self.pe.do(issue, free, ready)

                def soften(u, scored, h=h, t=t):
                    b, done = scored
                    ps = self.ps(b)
                    st = m["st"][:, u % 4, :]
                    ex = m["work"][:, u % 4, :]
                    other = slice(P, 2 * P) if t == 0 else slice(0, P)
                    a = self.dve.do(lambda e: e.tensor_tensor(ps[:, other], ps[:, other], m["window"][:, t, :],
                                                              ALU.add), done, self.tables)
                    a = self.dve.do(lambda e: e.tensor_reduce(st[:, 0:1], ps[:], AX.X, ALU.max, negate=True), a,
                                    self.freed.get(f"st{u % 4}"))
                    a = self.dve.do(lambda e: e.tensor_scalar(st[:, 1:2], st[:, 0:1], m["sinks"][:, 1, h:h + 1],
                                                              None, ALU.min), a, self.sinks)
                    x = self.act.do(lambda e: e.activation(ex, ps[:], ACT.Exp, bias=st[:, 1:2],
                                                           accum_out=st[:, 2:3]), a, self.slot_free[u % 4])
                    self.bank_free[b] = x
                    s = self.act.do(lambda e: e.activation(st[:, 3:4], m["sinks"][:, 0, h:h + 1], ACT.Exp,
                                                           bias=st[:, 1:2]), a)
                    return ex, x, s, st

                def weigh(u, soft):
                    ex, x, s, st = soft
                    r = self.dve.do(lambda e: e.tensor_tensor(st[:, 4:5], st[:, 2:3], st[:, 3:4], ALU.add), s)
                    r = self.dve.do(lambda e: e.reciprocal(st[:, 5:6], st[:, 4:5]), r)
                    return ex, x, 4, r, st

                def write(u, out, mixed, weighed, h=h, t=t):
                    r, st = weighed[3:]
                    to = y[:, t, h * HEAD_DIM:(h + 1) * HEAD_DIM]
                    a = self.act.do(lambda e: e.activation(to, out[:, HEAD_DIM:], ACT.Copy, scale=st[:, 5:6]),
                                    mixed, r, self.claim("b0"))
                    return self.dve.do(lambda e: e.scalar_tensor_tensor(
                        out=to, in0=out[:, 0:HEAD_DIM], scalar=st[:, 5:6], in1=to, op0=ALU.mult, op1=ALU.add), a)
                cols = slice(g * HEAD_DIM, (g + 1) * HEAD_DIM)
                values = [vr[:, source, :, k, cols] for source in range(2) for k in range(NT)]
                yield score, soften, weigh, (values, ready), write

    def second_block(self):
        d, m = self.dram, self.m
        x = self.tok("x")
        mg, b4 = self.tok("mg"), self.tok("b4")
        columns_1 = [c for c in range(2 * N_MOD) if (c // 2) % 3 < 2]
        rows_1 = [c for c in range(2 * N_MOD) if (c // 2) % 3 == 2]

        x_state = self.x_ready
        made = {}

        def gain():
            made["gain"] = self.gain(x, x_state[0], *x_state[1])
            yield

        ctx = self.tok("b3")

        def tokens_next(up_done):
            made["x"] = self.modulated(x, made["gain"], 0, 0, 0, None, up_done)
        c_state = self.conditioned_ffn(ctx, self.ctx_lhs, 1, 0, 0, mg[:, 1, :], "made", columns_1[:6], tokens_next,
                                       rows=False, before=gain())

        def context_next(up_done):
            made["ctx"], _ = self.modulated(ctx, c_state, 1, 0, 1, (0, 0), up_done)
            self.release("b3")
        x_state = self.conditioned_ffn(x, made["x"], 0, 0, 0, mg[:, 0, :], "made", columns_1[6:], context_next)

        qkv = d["attn_bqkv_2"][0]
        q_width = N_HEADS * HEAD_DIM
        self.kv_row = m["row_c"][:, 0:BANK]
        self.qkv_bias = [self.load("bias_kv", self.kv_row, qkv[q_width:].partition_broadcast(P),
                                   self.freed.get("row_c"))]
        self.sinks = self.load("sink", m["sinks"][:, 0, :], d["attn_sink_2"][0].partition_broadcast(P))
        self.sinks = self.dve.do(lambda e: e.tensor_scalar(m["sinks"][:, 1, :], m["sinks"][:, 0, :], -1.0, None,
                                                           ALU.mult), self.sinks)
        vc_t = m["b3"][:, 0:2 * BANK].rearrange("p (t n) -> p t n", t=NT)
        kc_f = m["b3"][:, 2 * BANK:].rearrange("p (g s) -> p g s", g=N_KV)
        kv_made = []
        self.hold = True
        drain(self.keys_values_steps(made["ctx"], vc_t, self.claim("b3"), kv_made))
        self.freed["row_c"] = kv_made
        self.release("xt")

        lhs, self.x_full = self.modulated(x, x_state, 0, 0, 1, (0, 0))
        rows_free = self.freed.get("rows")
        bias_q = self.load("bias_q", m["row_g"][:], qkv[0:q_width].partition_broadcast(P), rows_free)
        q_t, q_made = self.tok("b0"), [[] for _ in range(NT)]

        def evacuate(c, t, ps, done):
            s = slice(c * BANK, (c + 1) * BANK)
            token = self.dve.do(lambda e: e.tensor_tensor(q_t[:, t, s], ps[:], m["row_g"][:, s], ALU.add), done,
                                self.claim("b0"), bias_q)
            q_made[t].append(token)
            return token
        drain(self.gemm_token(lhs, columns(d["attn_wqkv_2"][0], 0, q_width), evacuate))
        twice = m["b2"][:, 0:2 * BANK]
        copied = self.double_keys(vc_t, twice, kv_made, self.claim("b2", "b3"))
        context = self.turn_keys(twice, copied, self.claim("b3"), plain=kc_f)
        self.release("b2", "mg")
        free = self.claim("b1", "b2", "mg")
        kr, vr = m["k_halves"], m["v_halves"]
        n = N_KV * HEAD_DIM
        ready = []
        for dst, src in ((kr[:, 1], kc_f), (vr[:, 1], vc_t[:, :, n:])):
            a = self.act.do(lambda e, dst=dst, src=src: e.activation(dst[:, 0], src, ACT.Copy), context, free)
            v = self.dve.do(lambda e, dst=dst, src=src: e.tensor_tensor(dst[:, 1], src, dst[:, 0].bitcast(F32),
                                                                        ALU.subtract), a)
            ready += [a, v]
        self.release("b3")
        self.kv_row = m["row_b"][:, 0:BANK]
        self.qkv_bias = [self.load("bias_kv2", self.kv_row, qkv[q_width:].partition_broadcast(P), rows_free)]
        kv = m["b3"][:, 0:2 * BANK].rearrange("p (t n) -> p t n", t=NT)
        kv_made = []
        product = self.keys_values_steps(lhs, kv, self.claim("b3"), kv_made)
        step(product)
        step(product)
        rotated = [self.rotate(q_t[:, t, :], N_HEADS, t, 2, m["row_c"][:], q_made[t]) for t in range(NT)]
        drain(product)
        self.freed["rows"] = self.latest()
        self.release("xt")
        kv_made = [self.rotate(kv[:, t, 0:n], N_KV, t, 0, m["row_c"][:], kv_made[t]) for t in range(NT)]
        self.freed["row_c"] = kv_made
        twice = m["b3"][:, 2 * BANK:]
        copied = self.double_keys(kv, twice, kv_made, self.claim("b1", "mg"))
        q_hi, q_lo, q_ready = self.to_lhs(q_t, rotated, (m["xt_hi"], m["xt_lo"]), self.claim("xt"))
        self.warm(ACT.Exp)
        ready += self.turn_keys(twice, copied, self.claim("b1", "mg"), halves=kr[:, 0])
        values = kv[:, :, n:]
        a = self.act.do(lambda e: e.activation(vr[:, 0, 0], values, ACT.Copy), kv_made, self.claim("mg"))
        v = self.dve.do(lambda e: e.tensor_tensor(vr[:, 0, 1], values, vr[:, 0, 0].bitcast(F32), ALU.subtract), a)
        ready += [a, v]
        self.release("b0", "b3")
        y = self.tok("b0")
        written = self.softmax_heads(self.window_units((q_hi, q_lo), kr, vr, y, [ready, q_ready]), None,
                                     (m["at_hi"], m["at_lo"]))
        self.release("mg", "b1", "b2", "b3", "xt")
        lhs = self.to_lhs(y, [written], (m["xt_hi"], m["xt_lo"]), self.claim("xt"))
        self.release("b0")
        x_state = self.mixer_out(x, lhs, d["attn_wo_2"][0], b4[:, 0, :], 0)

        x_state = self.conditioned_ffn(x, x_state, 0, 0, 2, b4[:, 1, :], (0, 1), rows_1)

        x_state = self.conditioned_ffn(x, x_state, 0, 1, 0, mg[:, 0, :], (0, 2))
        x_state = self.fourier(x, x_state, mg[:, 1, :], (1, 0))
        centred, (g, b, rows) = self.conditioned_ffn(x, x_state, 0, 1, 2, b4[:, 0, :], (1, 1))
        self.x_ready = self.gain(x, centred, g, b, rows)

    def mixer_out(self, x, lhs, w, gate, layer):
        d = self.dram
        g, b, rows = self.rows(f"mix{layer}", d["ln_g_2"][layer, 1], d["ln_b_2"][layer, 1])
        finish = self.gated_residual(x, gate, list(self.mod_ready[layer]))
        self.warm(ACT.Sqrt)
        drain(self.gemm_token(lhs, columns(w, 0, D), lambda c, t, ps, done: finish(t, c, ps, done)))
        self.release("xt")
        return self.finish_norm(finish.norm, g, b, rows)

    def fourier(self, x, state, gate, norm):
        d, m = self.dram, self.m
        (hi, lo, made), self.x_full = self.modulated(x, state, 0, 1, 1, norm)
        n = self.take([(lambda s: s[:, 0:2 * BANK].rearrange("p (k n) -> p k n", k=2),
                        d["dft"].rearrange("(k p) n -> p k n", p=P))], size=2 * BANK)
        wh, wl = [w[:, 0:2 * BANK].rearrange("p (k n) -> p k n", k=2) for w in self.halves(n)]
        split = []
        free = self.claim("b0", "b1", "b2", "b3")
        for g in range(4):
            for t in range(NT):
                b, bank_free = self.bank()
                ps = self.ps(b)

                def issue(e, g=g, t=t, ps=ps):
                    for k in range(2):
                        for i, (a, w) in enumerate(((hi, wh), (hi, wl), (lo, wh))):
                            last = e.matmul(ps[:], a[:, 2 * g + k, t * P:t * P + P], w[:, k, :],
                                            start=(k == 0 and i == 0), stop=(k == 1 and i == 2))
                    return last
                done = self.pe.do(issue, made, self.full(n), bank_free)
                ph, pl = m["pq_hi"][:, t, g, :], m["pq_lo"][:, t, g, :]
                a = self.act.do(lambda e, ph=ph, ps=ps: e.activation(ph[:, 0:SEQ], ps[:, 0:SEQ], ACT.Copy), done,
                                free)
                a = self.act.do(lambda e, ph=ph, ps=ps: e.activation(ph[:, SEQ:], ps[:, SEQ:], ACT.Copy, scale=-1.0),
                                done)
                v = self.dve.do(lambda e, ph=ph, pl=pl, ps=ps: e.tensor_tensor(
                    pl[:, 0:SEQ], ps[:, 0:SEQ], ph[:, 0:SEQ].bitcast(F32), ALU.subtract), a, free)
                v = self.dve.do(lambda e, ph=ph, pl=pl, ps=ps: e.scalar_tensor_tensor(
                    out=pl[:, SEQ:], in0=ps[:, SEQ:], scalar=-1.0, in1=ph[:, SEQ:].bitcast(F32), op0=ALU.mult,
                    op1=ALU.subtract), a)
                self.bank_free[b] = v
                split.append([a, v])
        first_done = done
        out = []
        for f in range(0, KD, 2):
            b, bank_free = self.bank()
            ps = self.ps(b)

            def issue(e, f=f, ps=ps):
                for i in range(2):
                    g, c0 = (f + i) // 2, ((f + i) % 2) * P
                    terms = [(part, k) for part in range(2) for k in range(NT)]
                    for n_, (part, k) in enumerate(terms):
                        cols = slice(part * SEQ + c0, part * SEQ + c0 + P)
                        w = slice(part * SEQ, (part + 1) * SEQ)
                        ph, pl = m["pq_hi"][:, k, g, cols], m["pq_lo"][:, k, g, cols]
                        for j, (a, c) in enumerate(((ph, wh), (ph, wl), (pl, wh))):
                            last = e.matmul(ps[:, i * SEQ:(i + 1) * SEQ], a, c[:, k, w],
                                            start=(n_ == 0 and j == 0), stop=(n_ == len(terms) - 1 and j == 2))
                return last
            done = self.pe.do(issue, split, bank_free)
            scale = 1.0 / SEQ
            h, l = hi[:, f:f + 2, :], lo[:, f:f + 2, :]
            a = self.act.do(lambda e, h=h, ps=ps: e.activation(h, ps[:], ACT.Copy, scale=scale), done, first_done)
            v = self.dve.do(lambda e, h=h, l=l, ps=ps: e.scalar_tensor_tensor(
                out=l, in0=ps[:], scalar=scale, in1=h.bitcast(F32), op0=ALU.mult, op1=ALU.subtract), a, first_done)
            self.bank_free[b] = v
            out.append([a, v])
        self.done_with(n, done)
        self.release("b0", "b1", "b2", "b3")
        return self.mixer_out(x, (hi, lo, out), d["fourier_wo_2"][0], gate, 1)

    def end(self):
        x = self.tok("x")
        self.stores = [self.load("out", self.dram["out"][0].rearrange("(t p) n -> p t n", p=P), x, self.x_ready,
                                 queue=self.sync)]
        self.sync.wait(self.stores)

    def build(self):
        self.combined = self.mod_ready = self.junk_free = self.x_full = None
        self.fold_at = 0
        self.begin()
        self.first_block()
        self.second_block()
        self.end()


def build_program(nc, dram):
    with ExitStack() as ctx:
        m = {}

        def sb(name, shape, dt=F32, to=None):
            m[name] = (to or ctx).enter_context(nc.sbuf_tensor(name, shape, dt))
        sb("raw", [P, RAW_SLOTS, PIECE])
        sb("hi", [P, SPLIT_SLOTS, PIECE], F32R)
        sb("lo", [P, SPLIT_SLOTS, PIECE], F32R)
        sb("x", [P, NT * D])
        sb("xt_hi", [P, KD, SEQ], F32R)
        sb("xt_lo", [P, KD, SEQ], F32R)
        for n in ("row_g", "row_b", "row_c"):
            sb(n, [P, D])
        sb("work", [P, 4, BANK])
        m["sm"], m["ex"] = m["work"][:, 0:2, :], m["work"][:, 2:4, :]
        sb("at", [P, 2, BANK])
        sb("ident", [P, P])
        sb("ones", [P, P])
        sb("dist", [P, SEQ])
        sb("decay", [P, RET_HEADS * 2 * P])
        sb("window", [P, 2, P])
        sb("rope", [P, NT, 4, AXIS_DIM])
        sb("index", [P, N_GROUPS])
        sb("st", [P, 4, 16])
        sb("unit", [P, 16])
        sb("junk", [P, P])
        sb("lam", [P, 8])
        sb("da_g", [P, P])
        sb("bn", [P, NT, 2, 6])
        sb("mv", [P, NT, 2])
        sb("gn", [P, NT * RET_HEADS, 2])
        sb("rstd", [P, 8])
        sb("nb", [P, 8])
        n_route = N_GROUPS + N_EXPERTS
        sb("r_raw", [P, KD, n_route])
        sb("r_w", [P, KD, 2 * n_route], F32R)
        sb("r_rows", [P, SEQ])
        sb("r_fold", [P, n_route])
        sb("r_bias", [P, n_route])
        sb("route", [P, NT, 56])
        sb("combine", [P, NT, N_EXPERTS])
        sb("cols", [P, P])
        sb("cols1", [P, 2 * KD])
        sb("fold", [P, 2, 2 * KD])
        sb("warm", [P, 2])
        sb("cvec", [P, 2, KD])
        sb("mod", [P, 3, N_MOD * KD])
        sb("sinks", [P, 2, N_HEADS])
        with ExitStack() as plain:
            for n in ("mg", "b0", "b1", "b2", "b3", "b4"):
                sb(n, [P, NT * D], to=plain)
        with ExitStack() as halves:
            sb("under_yt_hi", [P, NT * D], to=halves)
            sb("yt_hi", [P, KD, SEQ], F32R, to=halves)
            sb("yt_lo", [P, KD, SEQ], F32R, to=halves)
        with ExitStack() as halves:
            sb("under_ht_hi", [P, NT * D], to=halves)
            sb("ht_hi", [P, 2, 2, SEQ], F32R, to=halves)
            sb("ht_lo", [P, 2, 2, SEQ], F32R, to=halves)
        with ExitStack() as halves:
            sb("under_pq_hi", [P, NT * D], to=halves)
            sb("pq_hi", [P, NT, 4, BANK], F32R, to=halves)
            sb("pq_lo", [P, NT, 4, BANK], F32R, to=halves)
        with ExitStack() as halves:
            sb("v_halves", [P, 2, 2, NT, N_KV * HEAD_DIM], F32R, to=halves)
            sb("under_k", [P, NT * D], to=halves)
            sb("k_halves", [P, 2, 2, N_KV, SEQ], F32R, to=halves)
            sb("at_hi", [P, 2, BANK], F32R, to=halves)
            sb("at_lo", [P, 2, BANK], F32R, to=halves)
        m["psum"] = [ctx.enter_context(nc.psum_tensor(f"bank{i}", [P, BANK], F32)) for i in range(8)]
        first = Blocks(dram, m, None)
        first.build()
        program = Blocks(dram, m, first.taken)
        program.build()
        sems = {n: ctx.enter_context(nc.semaphore(n)) for n in sorted(program.sems)}
        block = ctx.enter_context(nc.Block())

        @block.sync
        def _(e):
            program.sync.run(e, sems)

        @block.gpsimd
        def _(e):
            program.pool.run(e, sems)

        @block.scalar
        def _(e):
            program.act.run(e, sems)

        @block.vector
        def _(e):
            program.dve.run(e, sems)

        @block.tensor
        def _(e):
            program.pe.run(e, sems)


def kernel(**inputs):
    import concourse.bacc as bacc
    from concourse.bass_utils import run_bass_kernel_spmd
    arrays = {n: np.ascontiguousarray(a) for n, a in inputs.items()}
    arrays.update(constants())
    nc = bacc.Bacc("TRN2", target_bir_lowering=False, num_devices=1)
    dram = {n: nc.dram_tensor(f"in_{n}", a.shape, F32, kind="ExternalInput").ap() for n, a in arrays.items()}
    dram["out"] = nc.dram_tensor("out", (1, SEQ, D), F32, kind="ExternalOutput").ap()
    build_program(nc, dram)
    r = run_bass_kernel_spmd(nc, [{f"in_{n}": a for n, a in arrays.items()}], core_ids=[0])
    return r.results[0]["out"]
```
